# Optimizing a Trainium2 kernel written in Bass

```python
import jax, jax.numpy as jnp
from jax import lax
import numpy as np
import math

D_MODEL = 1024
BATCH = 1
SEQ = 256
DEPTH = 1

CHUNK = 64
M_HEADS = 4
M_HEAD_DIM = D_MODEL // M_HEADS
M_WIDTH = M_HEADS * M_HEAD_DIM
CONV_K = 4
SGU_BLOCK = 128
SGU_GROUPS = 4
SGU_WIDTH = D_MODEL
SGU_GROUP_DIM = SGU_WIDTH // SGU_GROUPS
D_FF = 2816
PROJ_SIZES = (M_WIDTH, M_WIDTH, M_WIDTH, M_WIDTH, M_HEADS, M_HEADS, 2 * SGU_WIDTH, D_MODEL, D_MODEL)
N_PROJ = 4 * M_WIDTH + 2 * M_HEADS + 2 * SGU_WIDTH + 2 * D_MODEL
RMS_EPS = 1e-6
LN_EPS = 1e-5


def rmsnorm(x, g):
    x32 = x.astype(jnp.float32)
    y = x32 * lax.rsqrt(jnp.mean(x32 * x32, axis=-1, keepdims=True) + RMS_EPS)
    return (y * g.astype(jnp.float32)).astype(x.dtype)

def layernorm32(x, eps):
    x32 = x.astype(jnp.float32)
    xc = x32 - jnp.mean(x32, axis=-1, keepdims=True)
    return xc * lax.rsqrt(jnp.mean(xc * xc, axis=-1, keepdims=True) + eps)

def swiglu(x, w_in, w_out):
    gate, up = jnp.split(x @ w_in, 2, axis=-1)
    return (jax.nn.silu(gate) * up) @ w_out

def causal_depthwise_conv(x, w, b):
    y = lax.conv_general_dilated(
        x, w[:, None, :].astype(x.dtype), window_strides=(1,),
        padding=[(CONV_K - 1, 0)], dimension_numbers=('NWC', 'WIO', 'NWC'),
        feature_group_count=x.shape[-1])
    return y + b.astype(x.dtype)

def mlstm_chunkwise(q, k, v, log_i, log_f):
    bsz, nh, seqlen, dh = q.shape
    nc = seqlen // CHUNK

    def to_chunks(t):
        return jnp.moveaxis(t.reshape(bsz, nh, nc, CHUNK, *t.shape[3:]), 2, 0)

    causal = jnp.tril(jnp.ones((CHUNK, CHUNK), dtype=bool))

    def step(carry, xs):
        c_state, n_state, m_state = carry
        qc, kc, vc, lic, lfc = xs
        b = jnp.cumsum(lfc, axis=-1)
        a_inter = b + m_state[..., None]
        d = jnp.where(causal, b[..., :, None] - b[..., None, :] + lic[..., None, :], -jnp.inf)
        m_t = jnp.maximum(a_inter, jnp.max(d, axis=-1))
        w_inter = jnp.exp(a_inter - m_t)
        scores = jnp.einsum('bhtd,bhsd->bhts', qc, kc) * jnp.exp(d - m_t[..., None])
        num = (w_inter[..., None] * jnp.einsum('bhed,bhtd->bhte', c_state, qc)
               + jnp.einsum('bhts,bhse->bhte', scores, vc))
        den = w_inter * jnp.einsum('bhd,bhtd->bht', n_state, qc) + jnp.sum(scores, axis=-1)
        h = num / jnp.maximum(jnp.abs(den), jnp.exp(-m_t))[..., None]
        b_last = b[..., -1]
        g = b_last[..., None] - b + lic
        m_new = jnp.maximum(b_last + m_state, jnp.max(g, axis=-1))
        decay = jnp.exp(b_last + m_state - m_new)
        wk = jnp.exp(g - m_new[..., None])
        c_new = decay[..., None, None] * c_state + jnp.einsum('bhs,bhse,bhsd->bhed', wk, vc, kc)
        n_new = decay[..., None] * n_state + jnp.einsum('bhs,bhsd->bhd', wk, kc)
        return (c_new, n_new, m_new), h

    init = (jnp.zeros((bsz, nh, dh, dh), jnp.float32),
            jnp.zeros((bsz, nh, dh), jnp.float32),
            jnp.zeros((bsz, nh), jnp.float32))
    xs = (to_chunks(q), to_chunks(k), to_chunks(v), to_chunks(log_i), to_chunks(log_f))
    _, hs = lax.scan(step, init, xs)
    return jnp.moveaxis(hs, 0, 2).reshape(bsz, nh, seqlen, dh)

def mlstm_branch(q_pre, k_pre, v_pre, o_pre, i_pre, f_pre, conv_w, conv_b, b_i, b_f, head_g):
    bsz, seqlen, _ = q_pre.shape
    qk = jax.nn.silu(causal_depthwise_conv(jnp.concatenate([q_pre, k_pre], axis=-1), conv_w, conv_b))
    q, k = jnp.split(qk, 2, axis=-1)

    def heads(t):
        return t.reshape(bsz, seqlen, M_HEADS, M_HEAD_DIM).transpose(0, 2, 1, 3).astype(jnp.float32)

    log_i = (i_pre + b_i).astype(jnp.float32).transpose(0, 2, 1)
    log_f = jax.nn.log_sigmoid((f_pre + b_f).astype(jnp.float32)).transpose(0, 2, 1)
    h = mlstm_chunkwise(heads(q), heads(k) * (M_HEAD_DIM ** -0.5), heads(v_pre), log_i, log_f)
    h = layernorm32(h, LN_EPS).transpose(0, 2, 1, 3).reshape(bsz, seqlen, M_WIDTH)
    return (jax.nn.sigmoid(o_pre.astype(jnp.float32)) * h * head_g).astype(q_pre.dtype)

def sgu_branch(z_pre, norm_g, norm_b, w_s, b_s):
    bsz, seqlen, _ = z_pre.shape
    u, v = jnp.split(jax.nn.gelu(z_pre, approximate=False), 2, axis=-1)
    v = (layernorm32(v, LN_EPS) * norm_g + norm_b).astype(z_pre.dtype)
    nb = seqlen // SGU_BLOCK
    v = v.reshape(bsz, nb, SGU_BLOCK, SGU_GROUPS, SGU_GROUP_DIM)
    chunk_id = jnp.arange(SGU_BLOCK) // CHUNK
    mask = chunk_id[:, None] >= chunk_id[None, :]
    w = jnp.where(mask, w_s, 0.0).astype(v.dtype)
    sv = jnp.einsum('gts,bnsgc->bntgc', w, v) + b_s.T[:, :, None].astype(v.dtype)
    return u * sv.reshape(bsz, seqlen, SGU_WIDTH)

def first_inputs(seed: int = 0) -> dict:
    key = jax.random.key(seed)
    ks = jax.random.split(key, 20)
    L = DEPTH

    def nrm(k, shape, scale):
        return jax.random.normal(k, shape, jnp.float32) * scale

    return {
        'x': nrm(ks[0], (BATCH, SEQ, D_MODEL), 1.0),
        'ffn1_norm_g': 1.0 + nrm(ks[1], (L, D_MODEL), 0.05),
        'ffn1_w_in': nrm(ks[2], (L, D_MODEL, 2 * D_FF), D_MODEL ** -0.5),
        'ffn1_w_out': nrm(ks[3], (L, D_FF, D_MODEL), D_FF ** -0.5),
        'mix_norm_g': 1.0 + nrm(ks[4], (L, D_MODEL), 0.05),
        'w_mix_in': nrm(ks[5], (L, D_MODEL, N_PROJ), D_MODEL ** -0.5),
        'mlstm_conv_w': nrm(ks[6], (L, CONV_K, 2 * M_WIDTH), CONV_K ** -0.5),
        'mlstm_conv_b': nrm(ks[7], (L, 2 * M_WIDTH), 0.01),
        'mlstm_b_igate': nrm(ks[8], (L, M_HEADS), 0.1),
        'mlstm_b_fgate': jnp.linspace(3.0, 6.0, M_HEADS, dtype=jnp.float32) + nrm(ks[9], (L, M_HEADS), 0.1),
        'mlstm_head_norm_g': 1.0 + nrm(ks[10], (L, M_WIDTH), 0.05),
        'sgu_norm_g': 1.0 + nrm(ks[11], (L, SGU_WIDTH), 0.05),
        'sgu_norm_b': nrm(ks[12], (L, SGU_WIDTH), 0.01),
        'sgu_w_s': nrm(ks[13], (L, SGU_GROUPS, SGU_BLOCK, SGU_BLOCK), SGU_BLOCK ** -0.5),
        'sgu_b_s': 1.0 + nrm(ks[14], (L, SGU_GROUPS, SGU_BLOCK), 0.1),
        'w_mix_out': nrm(ks[15], (L, D_MODEL, D_MODEL), D_MODEL ** -0.5),
        'ffn2_norm_g': 1.0 + nrm(ks[16], (L, D_MODEL), 0.05),
        'ffn2_w_in': nrm(ks[17], (L, D_MODEL, 2 * D_FF), D_MODEL ** -0.5),
        'ffn2_w_out': nrm(ks[18], (L, D_FF, D_MODEL), D_FF ** -0.5),
        'final_norm_g': 1.0 + nrm(ks[19], (D_MODEL,), 0.05),
    }

def first_block(x, ffn1_norm_g, ffn1_w_in, ffn1_w_out, mix_norm_g, w_mix_in, mlstm_conv_w, mlstm_conv_b,
              mlstm_b_igate, mlstm_b_fgate, mlstm_head_norm_g, sgu_norm_g, sgu_norm_b, sgu_w_s, sgu_b_s,
              w_mix_out, ffn2_norm_g, ffn2_w_in, ffn2_w_out, final_norm_g):
    split_idx = np.cumsum(PROJ_SIZES)[:-1].tolist()
    for l in range(DEPTH):
        x = x + 0.5 * swiglu(rmsnorm(x, ffn1_norm_g[l]), ffn1_w_in[l], ffn1_w_out[l])
        xn = rmsnorm(x, mix_norm_g[l])
        proj = xn @ w_mix_in[l]
        q_pre, k_pre, v_pre, o_pre, i_pre, f_pre, z_pre, gate_m, gate_s = jnp.split(proj, split_idx, axis=-1)
        h_m = mlstm_branch(q_pre, k_pre, v_pre, o_pre, i_pre, f_pre, mlstm_conv_w[l], mlstm_conv_b[l],
                           mlstm_b_igate[l], mlstm_b_fgate[l], mlstm_head_norm_g[l])
        h_s = sgu_branch(z_pre, sgu_norm_g[l], sgu_norm_b[l], sgu_w_s[l], sgu_b_s[l])
        merged = jax.nn.sigmoid(gate_m) * h_m + jax.nn.sigmoid(gate_s) * h_s
        x = x + merged @ w_mix_out[l]
        x = x + 0.5 * swiglu(rmsnorm(x, ffn2_norm_g[l]), ffn2_w_in[l], ffn2_w_out[l])
    return rmsnorm(x, final_norm_g)


DEPTH_2 = 2

N_EVEN = (DEPTH_2 + 1) // 2
N_ODD = DEPTH_2 // 2
N_SUB = 3
FFN_RES = 0.5
D_FF_2 = ((8 * D_MODEL // 3 + 127) // 128) * 128
POOL_WINDOWS = (2, 4, 8, 16)
POOL_GROUPS = len(POOL_WINDOWS)
POOL_DIM = D_MODEL // 2
POOL_GROUP_DIM = POOL_DIM // POOL_GROUPS
D_SSM = D_MODEL
SSD_HEADDIM = 64
SSD_HEADS = D_SSM // SSD_HEADDIM
SSD_GROUPS = 2
D_STATE = 128
CONV_DIM = D_SSM + 2 * SSD_GROUPS * D_STATE
SSD_CHUNK = 128
IN_AB = POOL_DIM + D_SSM + CONV_DIM + SSD_HEADS
OUT_AB = POOL_DIM + D_SSM
MLA_HEADS = 16
QK_NOPE = 64
QK_ROPE = 32
V_DIM = 64
Q_LORA = 768
KV_LORA = 256
IN_MLA = Q_LORA + KV_LORA + QK_ROPE
ROPE_THETA = 10000.0
Q_BLOCK = 128


def rmsnorm_2(x, g):
    xf = x.astype(jnp.float32)
    y = xf * lax.rsqrt(jnp.mean(xf * xf, axis=-1, keepdims=True) + RMS_EPS)
    return (y * g.astype(jnp.float32)).astype(x.dtype)

def modulate(h, shift, scale):
    return h * (1 + scale[:, None, :]) + shift[:, None, :]

def swiglu_2(h, w13, w2):
    a, b = jnp.split(h @ w13, 2, axis=-1)
    return (jax.nn.silu(a) * b) @ w2

def multiscale_pool(u, w, scale):
    bsz, L, _ = u.shape
    uf = u.astype(jnp.float32)
    cs_pad = jnp.pad(jnp.cumsum(uf, axis=1), ((0, 0), (1, 0), (0, 0)))
    t = jnp.arange(L, dtype=jnp.float32)
    outs = []
    for gi, win in enumerate(POOL_WINDOWS):
        sl = slice(gi * POOL_GROUP_DIM, (gi + 1) * POOL_GROUP_DIM)
        c_g = cs_pad[:, :, sl]
        lag = jnp.pad(c_g[:, :L + 1 - win], ((0, 0), (win - 1, 0), (0, 0)))
        count = jnp.minimum(t + 1.0, float(win))[None, :, None]
        outs.append((c_g[:, 1:] - lag) / count - uf[:, :, sl])
    d = jnp.stack(outs, axis=2)
    y = jnp.einsum("blgc,gcd->blgd", d, w.astype(jnp.float32)).reshape(bsz, L, POOL_DIM)
    return (y * scale.astype(jnp.float32)).astype(u.dtype)

def causal_depthwise_conv_2(u, w, b):
    y = lax.conv_general_dilated(u, w[:, None, :], window_strides=(1,),
                                 padding=[(CONV_K - 1, 0)],
                                 dimension_numbers=("NWC", "WIO", "NWC"),
                                 feature_group_count=u.shape[-1])
    return y + b

def ssd_chunked(xh, dt, a, bm, cm):
    bsz, L, H, P = xh.shape
    nc = L // SSD_CHUNK
    r = H // SSD_GROUPS
    x = (xh * dt[..., None]).reshape(bsz, nc, SSD_CHUNK, SSD_GROUPS, r, P)
    adt = (dt * a).reshape(bsz, nc, SSD_CHUNK, SSD_GROUPS, r).transpose(0, 3, 4, 1, 2)
    bc = bm.reshape(bsz, nc, SSD_CHUNK, SSD_GROUPS, D_STATE)
    cc = cm.reshape(bsz, nc, SSD_CHUNK, SSD_GROUPS, D_STATE)
    a_cs = jnp.cumsum(adt, axis=-1)
    causal = jnp.tril(jnp.ones((SSD_CHUNK, SSD_CHUNK), dtype=bool))
    decay = jnp.exp(jnp.where(causal, a_cs[..., :, None] - a_cs[..., None, :], -jnp.inf))
    cb = jnp.einsum("bclgn,bcsgn->bgcls", cc, bc)
    y_diag = jnp.einsum("bgcls,bgrcls,bcsgrp->bclgrp", cb, decay, x)
    decay_to_end = jnp.exp(a_cs[..., -1:] - a_cs)
    states = jnp.einsum("bcsgn,bgrcs,bcsgrp->cbgrpn", bc, decay_to_end, x)
    chunk_decay = jnp.exp(a_cs[..., -1]).transpose(3, 0, 1, 2)

    def step(h, inp):
        s_c, d_c = inp
        return d_c[..., None, None] * h + s_c, h

    h0 = jnp.zeros(states.shape[1:], states.dtype)
    _, prev = lax.scan(step, h0, (states, chunk_decay))
    y_off = jnp.einsum("bclgn,cbgrpn,bgrcl->bclgrp", cc, prev, jnp.exp(a_cs))
    return (y_diag + y_off).reshape(bsz, L, H, P)

def pool_ssd_mixer(h, w_in, pool_w, pool_scale, conv_w, conv_b, dt_bias, a_log, d_skip, norm_g, w_out):
    bsz, L, _ = h.shape
    proj = h @ w_in
    u_pool, z, xbc, dt_raw = jnp.split(
        proj, [POOL_DIM, POOL_DIM + D_SSM, POOL_DIM + D_SSM + CONV_DIM], axis=-1)
    y_pool = multiscale_pool(u_pool, pool_w, pool_scale)
    xbc = jax.nn.silu(causal_depthwise_conv_2(xbc, conv_w, conv_b))
    xs, bm, cm = jnp.split(xbc, [D_SSM, D_SSM + SSD_GROUPS * D_STATE], axis=-1)
    f32 = jnp.float32
    xh = xs.astype(f32).reshape(bsz, L, SSD_HEADS, SSD_HEADDIM)
    dt = jax.nn.softplus(dt_raw.astype(f32) + dt_bias.astype(f32))
    a = -jnp.exp(a_log.astype(f32))
    y = ssd_chunked(xh, dt, a,
                    bm.astype(f32).reshape(bsz, L, SSD_GROUPS, D_STATE),
                    cm.astype(f32).reshape(bsz, L, SSD_GROUPS, D_STATE))
    y = y + d_skip.astype(f32)[:, None] * xh
    y = y.reshape(bsz, L, D_SSM) * jax.nn.silu(z.astype(f32))
    yg = y.reshape(bsz, L, SSD_GROUPS, D_SSM // SSD_GROUPS)
    yg = yg * lax.rsqrt(jnp.mean(yg * yg, axis=-1, keepdims=True) + RMS_EPS)
    y = (yg.reshape(bsz, L, D_SSM) * norm_g.astype(f32)).astype(h.dtype)
    return jnp.concatenate([y_pool, y], axis=-1) @ w_out

def rope_tables(positions):
    inv_freq = ROPE_THETA ** (-jnp.arange(0, QK_ROPE, 2, dtype=jnp.float32) / QK_ROPE)
    ang = positions.astype(jnp.float32)[..., None] * inv_freq
    return jnp.cos(ang), jnp.sin(ang)

def apply_rope(x, cos, sin):
    xf = x.astype(jnp.float32)
    x1, x2 = jnp.split(xf, 2, axis=-1)
    return jnp.concatenate([x1 * cos - x2 * sin, x2 * cos + x1 * sin], axis=-1).astype(x.dtype)

def mla_mixer(h, positions, w_in, q_norm_g, w_uq, kv_norm_g, w_ukv, w_o):
    bsz, L, _ = h.shape
    q_a, kv_a, k_rope = jnp.split(h @ w_in, [Q_LORA, Q_LORA + KV_LORA], axis=-1)
    q = (rmsnorm_2(q_a, q_norm_g) @ w_uq).reshape(bsz, L, MLA_HEADS, QK_NOPE + QK_ROPE)
    q_nope, q_rope = q[..., :QK_NOPE], q[..., QK_NOPE:]
    kv = (rmsnorm_2(kv_a, kv_norm_g) @ w_ukv).reshape(bsz, L, MLA_HEADS, QK_NOPE + V_DIM)
    k_nope, v = kv[..., :QK_NOPE], kv[..., QK_NOPE:]
    cos, sin = rope_tables(positions)
    q_rope = apply_rope(q_rope, cos[:, :, None], sin[:, :, None])
    k_rope = apply_rope(k_rope, cos, sin)
    scale = 1.0 / math.sqrt(QK_NOPE + QK_ROPE)
    nb = L // Q_BLOCK
    k_idx = jnp.arange(L)

    def blocks(t):
        return jnp.moveaxis(t.reshape(bsz, nb, Q_BLOCK, *t.shape[2:]), 1, 0)

    def attend(args):
        qn, qr, start = args
        s = (jnp.einsum("bqhd,bkhd->bhqk", qn, k_nope, preferred_element_type=jnp.float32)
             + jnp.einsum("bqhd,bkd->bhqk", qr, k_rope, preferred_element_type=jnp.float32)) * scale
        q_idx = start + jnp.arange(Q_BLOCK)
        s = jnp.where(k_idx[None, :] <= q_idx[:, None], s, -jnp.inf)
        p = jax.nn.softmax(s, axis=-1).astype(v.dtype)
        return jnp.einsum("bhqk,bkhd->bqhd", p, v)

    starts = jnp.arange(nb, dtype=jnp.int32) * Q_BLOCK
    o = lax.map(attend, (blocks(q_nope), blocks(q_rope), starts))
    o = jnp.moveaxis(o, 0, 1).reshape(bsz, L, MLA_HEADS * V_DIM)
    return o @ w_o

def second_inputs(seed: int = 0) -> dict:
    key = jax.random.key(seed)
    ks = jax.random.split(key, 32)
    f32 = jnp.float32

    def nrm(k, shape, std):
        return jax.random.normal(k, shape, f32) * std

    def gain(k, shape):
        return 1.0 + 0.05 * jax.random.normal(k, shape, f32)

    x = jax.random.normal(ks[0], (BATCH, SEQ, D_MODEL), f32)
    c = jax.random.normal(ks[1], (BATCH, D_MODEL), f32)
    positions = (jnp.arange(SEQ, dtype=jnp.int32)[None, :]
                 + jax.random.randint(ks[2], (BATCH, 1), 0, 1024, dtype=jnp.int32))
    mod_w = nrm(ks[3], (DEPTH_2, D_MODEL, 3 * N_SUB * D_MODEL), 0.5 * D_MODEL ** -0.5)
    mod_b = nrm(ks[4], (DEPTH_2, 3 * N_SUB * D_MODEL), 0.02)
    norm_g = gain(ks[5], (DEPTH_2, N_SUB, D_MODEL))
    ffn_w13 = nrm(ks[6], (DEPTH_2, 2, D_MODEL, 2 * D_FF_2), D_MODEL ** -0.5)
    ffn_w2 = nrm(ks[7], (DEPTH_2, 2, D_FF_2, D_MODEL), D_FF_2 ** -0.5)
    ab_w_in = nrm(ks[8], (N_EVEN, D_MODEL, IN_AB), D_MODEL ** -0.5)
    pool_w = nrm(ks[9], (N_EVEN, POOL_GROUPS, POOL_GROUP_DIM, POOL_GROUP_DIM), POOL_GROUP_DIM ** -0.5)
    pool_scale = gain(ks[10], (N_EVEN, POOL_DIM))
    ssd_conv_w = nrm(ks[11], (N_EVEN, CONV_K, CONV_DIM), CONV_K ** -0.5)
    ssd_conv_b = nrm(ks[12], (N_EVEN, CONV_DIM), 0.02)
    dt0 = jnp.exp(jax.random.uniform(ks[13], (N_EVEN, SSD_HEADS), f32,
                                     minval=math.log(1e-3), maxval=math.log(1e-1)))
    ssd_dt_bias = dt0 + jnp.log(-jnp.expm1(-dt0))
    ssd_a_log = jnp.log(jax.random.uniform(ks[14], (N_EVEN, SSD_HEADS), f32, minval=1.0, maxval=16.0))
    ssd_d = gain(ks[15], (N_EVEN, SSD_HEADS))
    ssd_norm_g = gain(ks[16], (N_EVEN, D_SSM))
    ab_w_out = nrm(ks[17], (N_EVEN, OUT_AB, D_MODEL), OUT_AB ** -0.5)
    mla_w_in = nrm(ks[18], (N_ODD, D_MODEL, IN_MLA), D_MODEL ** -0.5)
    mla_q_norm_g = gain(ks[19], (N_ODD, Q_LORA))
    mla_w_uq = nrm(ks[20], (N_ODD, Q_LORA, MLA_HEADS * (QK_NOPE + QK_ROPE)), Q_LORA ** -0.5)
    mla_kv_norm_g = gain(ks[21], (N_ODD, KV_LORA))
    mla_w_ukv = nrm(ks[22], (N_ODD, KV_LORA, MLA_HEADS * (QK_NOPE + V_DIM)), KV_LORA ** -0.5)
    mla_w_o = nrm(ks[23], (N_ODD, MLA_HEADS * V_DIM, D_MODEL), (MLA_HEADS * V_DIM) ** -0.5)
    final_norm_g = gain(ks[24], (D_MODEL,))
    return {"x": x, "c": c, "positions": positions, "mod_w": mod_w, "mod_b": mod_b,
            "norm_g": norm_g, "ffn_w13": ffn_w13, "ffn_w2": ffn_w2, "ab_w_in": ab_w_in,
            "pool_w": pool_w, "pool_scale": pool_scale, "ssd_conv_w": ssd_conv_w,
            "ssd_conv_b": ssd_conv_b, "ssd_dt_bias": ssd_dt_bias, "ssd_a_log": ssd_a_log,
            "ssd_d": ssd_d, "ssd_norm_g": ssd_norm_g, "ab_w_out": ab_w_out,
            "mla_w_in": mla_w_in, "mla_q_norm_g": mla_q_norm_g, "mla_w_uq": mla_w_uq,
            "mla_kv_norm_g": mla_kv_norm_g, "mla_w_ukv": mla_w_ukv, "mla_w_o": mla_w_o,
            "final_norm_g": final_norm_g}

def second_block(x, c, positions, mod_w, mod_b, norm_g, ffn_w13, ffn_w2, ab_w_in, pool_w,
              pool_scale, ssd_conv_w, ssd_conv_b, ssd_dt_bias, ssd_a_log, ssd_d, ssd_norm_g,
              ab_w_out, mla_w_in, mla_q_norm_g, mla_w_uq, mla_kv_norm_g, mla_w_ukv, mla_w_o,
              final_norm_g):
    c_act = jax.nn.silu(c)
    for i in range(DEPTH_2):
        mod = c_act @ mod_w[i] + mod_b[i]
        sh1, sc1, g1, sh2, sc2, g2, sh3, sc3, g3 = jnp.split(mod, 3 * N_SUB, axis=-1)
        h = modulate(rmsnorm_2(x, norm_g[i, 0]), sh1, sc1)
        x = x + FFN_RES * g1[:, None, :] * swiglu_2(h, ffn_w13[i, 0], ffn_w2[i, 0])
        h = modulate(rmsnorm_2(x, norm_g[i, 1]), sh2, sc2)
        j = i // 2
        if i % 2 == 0:
            m = pool_ssd_mixer(h, ab_w_in[j], pool_w[j], pool_scale[j], ssd_conv_w[j],
                               ssd_conv_b[j], ssd_dt_bias[j], ssd_a_log[j], ssd_d[j],
                               ssd_norm_g[j], ab_w_out[j])
        else:
            m = mla_mixer(h, positions, mla_w_in[j], mla_q_norm_g[j], mla_w_uq[j],
                          mla_kv_norm_g[j], mla_w_ukv[j], mla_w_o[j])
        x = x + g2[:, None, :] * m
        h = modulate(rmsnorm_2(x, norm_g[i, 2]), sh3, sc3)
        x = x + FFN_RES * g3[:, None, :] * swiglu_2(h, ffn_w13[i, 1], ffn_w2[i, 1])
    return rmsnorm_2(x, final_norm_g)


def setup_inputs(seed=0):
    out = dict(first_inputs(seed))
    for name, value in second_inputs(seed + 1).items():
        if name != "x":
            out[name + "_2"] = value
    return out


def reference(
    x, ffn1_norm_g, ffn1_w_in, ffn1_w_out, mix_norm_g, w_mix_in, mlstm_conv_w, mlstm_conv_b,
    mlstm_b_igate, mlstm_b_fgate, mlstm_head_norm_g, sgu_norm_g, sgu_norm_b, sgu_w_s, sgu_b_s,
    w_mix_out, ffn2_norm_g, ffn2_w_in, ffn2_w_out, final_norm_g, c_2, positions_2, mod_w_2,
    mod_b_2, norm_g_2, ffn_w13_2, ffn_w2_2, ab_w_in_2, pool_w_2, pool_scale_2, ssd_conv_w_2,
    ssd_conv_b_2, ssd_dt_bias_2, ssd_a_log_2, ssd_d_2, ssd_norm_g_2, ab_w_out_2, mla_w_in_2,
    mla_q_norm_g_2, mla_w_uq_2, mla_kv_norm_g_2, mla_w_ukv_2, mla_w_o_2, final_norm_g_2,
):
    x = first_block(
        x, ffn1_norm_g, ffn1_w_in, ffn1_w_out, mix_norm_g, w_mix_in, mlstm_conv_w, mlstm_conv_b,
        mlstm_b_igate, mlstm_b_fgate, mlstm_head_norm_g, sgu_norm_g, sgu_norm_b, sgu_w_s,
        sgu_b_s, w_mix_out, ffn2_norm_g, ffn2_w_in, ffn2_w_out, final_norm_g,
    )
    return second_block(
        x, c_2, positions_2, mod_w_2, mod_b_2, norm_g_2, ffn_w13_2, ffn_w2_2, ab_w_in_2,
        pool_w_2, pool_scale_2, ssd_conv_w_2, ssd_conv_b_2, ssd_dt_bias_2, ssd_a_log_2, ssd_d_2,
        ssd_norm_g_2, ab_w_out_2, mla_w_in_2, mla_q_norm_g_2, mla_w_uq_2, mla_kv_norm_g_2,
        mla_w_ukv_2, mla_w_o_2, final_norm_g_2,
    )


_drawn_inputs = setup_inputs


def setup_inputs(seed=0):
    import zlib

    import numpy as np

    out = dict(_drawn_inputs(seed))
    spreads = {}
    factors = {'mlstm_conv_b': 8.0,
     'mlstm_b_igate': 8.0,
     'mlstm_head_norm_g': 4.352,
     'sgu_norm_g': 4.095,
     'sgu_norm_b': 8.0,
     'ffn2_norm_g': 3.075,
     'pool_scale_2': 7.122,
     'ssd_conv_b_2': 8.0,
     'ssd_d_2': 8.0,
     'ssd_norm_g_2': 4.354,
     'mla_q_norm_g_2': 8.0,
     'mla_kv_norm_g_2': 8.0}
    for name, (base, spread) in spreads.items():
        noise = np.random.default_rng([zlib.crc32(name.encode()), seed]).standard_normal(out[name].shape)
        drawn = base * np.exp(spread * noise) if base else spread * noise
        out[name] = __import__('jax').numpy.asarray(drawn.astype(out[name].dtype))
    for name, factor in factors.items():
        out[name] = (out[name] * factor).astype(out[name].dtype)
    return out
```

```python
import numpy as np
import concourse.bass as bass
from concourse import mybir
from contextlib import ExitStack

P = 128
T = 256
D = 1024
KD = D // P
DFF = 2816
STEPS = DFF // 256
BLK = 2048
SLOTS = 3
HEADS_M, DH_M = 4, 256
SGU_G = 4
SSD_H, SSD_P = 16, 64
MLA_H, NOPE, ROPE = 16, 64, 32
DQ = NOPE + ROPE
NEG = -1.0e30
RMS_EPS, LN_EPS = 1e-6, 1e-5

FFN_BLOCKS = 3 * STEPS
MIX1_IN, MIX1_OUT = 32, 4
MIX2_IN, MIX2_OUT = 12, 6
MIX3_IN, MIX3_UQ, MIX3_UKV, MIX3_OUT = 4, 8, 2, 4
PHASES = [("ffn", 0, FFN_BLOCKS), ("mix1", 0, MIX1_IN + MIX1_OUT), ("ffn", 1, FFN_BLOCKS), ("final", 0, 0),
          ("ffn", 2, FFN_BLOCKS), ("mix2", 0, MIX2_IN + MIX2_OUT), ("ffn", 3, FFN_BLOCKS),
          ("ffn", 4, FFN_BLOCKS), ("mix3", 0, MIX3_IN + MIX3_UQ + MIX3_UKV + MIX3_OUT), ("ffn", 5, FFN_BLOCKS),
          ("final", 1, 0)]
MOD_GROUPS = {0: 5, 1: 5, 2: 5, 3: 3, 4: 0, 5: 0}

PARAMS = [("g_ffn1", 8), ("g_mix", 8), ("g_ffn2", 8), ("g_final", 8), ("conv_w1", 64), ("conv_b1", 16),
          ("b_i", 1), ("b_f", 1), ("head_g", 8), ("sgu_bs", 128), ("mod_b", 144), ("norm_g2", 48),
          ("pool_scale", 4), ("conv_w2", 48), ("conv_b2", 12), ("dt_bias", 1), ("a_log", 1), ("ssd_d", 8),
          ("ssd_g", 8), ("q_g", 6), ("kv_g", 2), ("g_final2", 8), ("c", 8), ("w_if", 512), ("w_dt", 128),
          ("w_krope", 768), ("pool_w", 512), ("sgu_wT", 512)]
CONSTS = [("ident", 128), ("maskT", 128), ("mask", 128), ("ones", 128), ("rope_perm", 96), ("inv_freq", 1),
          ("pool_fix", 64)]


def offsets(table):
    at, o = {}, 0
    for name, width in table:
        at[name] = (o, o + width)
        o += width
    return at, o


def build_program(nc, a_x, a_pos, a_stream, a_mod, a_params, a_consts, a_sgu, a_out, phases=PHASES):
    F32, F32R, I32 = mybir.dt.float32, mybir.dt.float32r, mybir.dt.int32
    ALU, ACT, AX = mybir.AluOpType, mybir.ActivationFunctionType, mybir.AxisListType
    ds = bass.ds
    P_AT, P_N = offsets(PARAMS)
    C_AT, C_N = offsets(CONSTS)
    first_block, b0 = [], 0
    for _, _, nb in phases:
        first_block.append(b0)
        b0 += nb
    N_BLOCKS = b0
    N_GROUPS = sum(MOD_GROUPS[i] for kind, i, _ in phases if kind == "ffn")

    with ExitStack() as ctx:
        def sb(name, shape, dt=F32):
            return ctx.enter_context(nc.sbuf_tensor(name, shape, dt))

        sems = {}

        def sem(name):
            if name not in sems:
                sems[name] = ctx.enter_context(nc.semaphore(name))
            return sems[name]

        raw = sb("raw", [P, SLOTS, BLK])
        whi = sb("whi", [P, SLOTS, BLK], F32R)
        wlo = sb("wlo", [P, SLOTS, BLK], F32R)
        mod_raw = sb("mod_raw", [P, 2, BLK])
        mod_acc = sb("mod_acc", [P, D])
        mod_tab = sb("mod_tab", [P, 144])
        c_act = sb("c_act", [P, KD])
        x = sb("x", [P, KD, T])
        xm = sb("xm", [P, KD, T])
        xh = sb("xh", [P, KD, T], F32R)
        xl = sb("xl", [P, KD, T], F32R)
        std = sb("std", [P, T])
        rstd = sb("rstd", [P, T])
        gmod = sb("gmod", [P, KD])
        gres = sb("gres", [P, KD])
        params = sb("params", [P, P_N])
        consts = sb("consts", [P, C_N])
        cos96 = sb("cos96", [P, T])
        sin96 = sb("sin96", [P, T])
        rows = sb("rows", [16, 5, T])
        rstats = sb("rstats", [P, 2, 12])
        cols = sb("cols", [P, 66])

        def region(**tensors):
            with ExitStack() as here:
                return [here.enter_context(nc.sbuf_tensor(name, shape, dt)) for name, (shape, dt) in tensors.items()]

        gate, hid, hid_hi, hid_lo = region(gate=([P, 2, T], F32), hid=([P, 2, T], F32),
                                           hid_hi=([P, 2, 2, T], F32R), hid_lo=([P, 2, 2, T], F32R))

        bank = [ctx.enter_context(nc.psum_tensor(f"bank{i}", [P, 512], F32)) for i in range(8)]
        ACC = bank[0:4]
        GATE, UP, STAT, MODP = bank[4:8]

        def pair(b):
            return b[:, :].rearrange("p (m t) -> p m t", m=2)

        def prm(name):
            lo, hi = P_AT[name]
            return params[:, lo:hi]

        def cst(name):
            lo, hi = C_AT[name]
            return consts[:, lo:hi]

        ident, ones = cst("ident"), cst("ones")

        def slot_of(n0):
            return n0 % SLOTS

        def use_of(n0, i=0, per=0):
            return n0 // SLOTS + (per // SLOTS) * i

        def act_split(act, n0, i=0, per=0):
            if n0 >= N_BLOCKS:
                return
            s = slot_of(n0)
            act.wait_ge(sem(f"w_loaded{s}"), 16 * use_of(n0, i, per) + 16)
            if n0 >= SLOTS:
                act.wait_ge(sem("w_used"), n0 - SLOTS + 1 + per * i)
            act.activation(whi[:, s, :], raw[:, s, :], ACT.Copy).then_inc(sem("w_hi_ready"), 1)

        def dve_split(dve, n0, i=0, per=0):
            if n0 >= N_BLOCKS:
                return
            s = slot_of(n0)
            dve.wait_ge(sem("w_hi_ready"), n0 + 1 + per * i)
            dve.tensor_tensor(wlo[:, s, :], raw[:, s, :], whi[:, s, :].bitcast(F32), ALU.subtract)\
               .then_inc(sem("w_lo_ready"), 1)

        PASSES = ((0, 0), (0, 1), (1, 0))

        def pe_in(pe, n0, out, i=0, per=0, first_pass_waits=None):
            s = slot_of(n0)
            pe.wait_ge(sem("w_lo_ready"), n0 + 1 + per * i)
            for m in range(2):
                for k in range(KD):
                    if m == 0 and first_pass_waits is not None and k % 2 == 0:
                        pe.wait_ge(sem("xn_split"), first_pass_waits + k // 2 + 1)
                    for j, (wp, ap) in enumerate(PASSES):
                        last = pe.matmul(out[:, m, :], (whi, wlo)[wp][:, s, k * 256 + m * P:k * 256 + m * P + P],
                                         (xh, xl)[ap][:, k, :], start=(k == 0 and j == 0), stop=(k == KD - 1 and j == 2))
            last.then_inc(sem("w_used"), 1)

        def pe_tok(pe, n0, out):
            s = slot_of(n0)
            pe.wait_ge(sem("w_lo_ready"), n0 + 1)
            for tt in range(2):
                for k in range(KD):
                    for j, (wp, ap) in enumerate(PASSES):
                        last = pe.matmul(out[:, tt, :], (xh, xl)[ap][:, k, tt * P:tt * P + P],
                                         (whi, wlo)[wp][:, s, k * 256:k * 256 + 256],
                                         start=(k == 0 and j == 0), stop=(k == KD - 1 and j == 2))
            last.then_inc(sem("w_used"), 1)

        def pe_out(pe, n0, hi, lo, first, last_block, i=0, per=0, acc=ACC):
            s = slot_of(n0)
            pe.wait_ge(sem("w_lo_ready"), n0 + 1 + per * i)
            for d in range(KD):
                for kt in range(2):
                    for j, (wp, ap) in enumerate(PASSES):
                        c = kt * D + d * P
                        mm = pe.matmul(pair(acc[d // 2])[:, d % 2, :], (whi, wlo)[wp][:, s, c:c + P],
                                       (hi, lo)[ap][:, kt, :], start=(first and d % 2 == 0 and kt == 0 and j == 0),
                                       stop=(last_block and kt == 1 and j == 2), skip_group_check=True)
                if last_block and d % 2 == 1 and d < KD - 1:
                    mm.then_inc(sem("acc_ready"), 1)
            mm.then_inc(sem("w_used"), 1)

        def dve_residual(dve, r, last, scale=None, gain=None, acc=ACC):
            for b in range(4):
                if b < 3:
                    dve.wait_ge(sem("acc_ready"), 3 * r + b + 1)
                else:
                    dve.wait_ge(sem("w_used"), last + 1)
                if gain is None:
                    dve.scalar_tensor_tensor(out=x[:, 2 * b:2 * b + 2, :], in0=pair(acc[b]), scalar=scale,
                                             in1=x[:, 2 * b:2 * b + 2, :], op0=ALU.mult, op1=ALU.add)\
                       .then_inc(sem("x_updated"), 1)
                else:
                    for m in range(2):
                        ins = dve.scalar_tensor_tensor(out=x[:, 2 * b + m, :], in0=pair(acc[b])[:, m, :],
                                                       scalar=gain[:, 2 * b + m:2 * b + m + 1],
                                                       in1=x[:, 2 * b + m, :], op0=ALU.mult, op1=ALU.add)
                    ins.then_inc(sem("x_updated"), 1)

        def act_norm(act, n, split=True):
            for b in range(4):
                if n == 0:
                    act.wait_ge(sem("x_loaded"), 16)
                else:
                    act.wait_ge(sem("x_updated"), 4 * (n - 1) + b + 1)
                act.activation(xm[:, 2 * b:2 * b + 2, :], x[:, 2 * b:2 * b + 2, :], ACT.Square)\
                   .then_inc(sem("x_squared"), 1)
            act.wait_ge(sem("x_summed"), n + 1)
            act.activation(std[:, :], STAT[:, 0:T], ACT.Sqrt, scale=1.0 / D, bias=cols[:, 64:65]).then_inc(sem("std_ready"), 1)
            if split:
                j = split_index[n]
                for b in range(4):
                    act.wait_ge(sem("xn_ready"), 4 * j + b + 1)
                    act.activation(xh[:, 2 * b:2 * b + 2, :], xm[:, 2 * b:2 * b + 2, :], ACT.Copy)\
                       .then_inc(sem("xn_rounded"), 1)

        def pe_norm(pe, n):
            for k in range(KD):
                if k % 2 == 0:
                    pe.wait_ge(sem("x_squared"), 4 * n + k // 2 + 1)
                mm = pe.matmul(STAT[:, 0:T], ones, xm[:, k, :], start=(k == 0), stop=(k == KD - 1))
            mm.then_inc(sem("x_summed"), 1)

        def dve_norm(dve, n, g, shift=None, split=True):
            dve.wait_ge(sem("std_ready"), n + 1)
            dve.reciprocal(rstd[:, :], std[:, :]).then_inc(sem("rstd_ready"), 1)
            dve.wait_ge(sem("rstd_ready"), n + 1)

            def rest(b):
                dve.wait_ge(sem("xn_rounded"), 4 * split_index[n] + b + 1)
                dve.tensor_tensor(xl[:, 2 * b:2 * b + 2, :], xm[:, 2 * b:2 * b + 2, :],
                                  xh[:, 2 * b:2 * b + 2, :].bitcast(F32), ALU.subtract).then_inc(sem("xn_split"), 1)

            dst = xm if split else x
            for b in range(4):
                for k in (2 * b, 2 * b + 1):
                    ins = dve.scalar_tensor_tensor(out=dst[:, k, :], in0=x[:, k, :], scalar=g[:, k:k + 1],
                                                   in1=rstd[:, :], op0=ALU.mult, op1=ALU.mult)
                    if shift is not None:
                        ins.then_inc(sem("xn_scaled"), 1)
                        dve.wait_ge(sem("xn_scaled"), 8 * shift_index[n] + k + 1)
                        ins = dve.tensor_scalar(dst[:, k, :], dst[:, k, :], shift[:, k:k + 1], None, ALU.add)
                ins.then_inc(sem("xn_ready" if split else "x_updated"), 1)
                if split and b >= 1:
                    rest(b - 1)
            if split:
                rest(3)

        split_index, shift_index, k_split, k_shift = {}, {}, 0, 0
        for n, (kind, idx, _) in enumerate(phases):
            if kind != "final":
                split_index[n] = k_split
                k_split += 1
                if n > 3:
                    shift_index[n] = k_shift
                    k_shift += 1
        residual_index = split_index

        def mod_col(layer, j):
            c = (9 * layer + j) * KD
            return mod_tab[:, c:c + KD]

        MOD_OF = {4: (0, 0), 5: (0, 3), 6: (0, 6), 7: (1, 0), 8: (1, 3), 9: (1, 6)}
        GAIN_OF = {0: "g_ffn1", 1: "g_mix", 2: "g_ffn2", 3: "g_final", 10: "g_final2"}

        def dve_phase_norm(dve, n):
            if n in MOD_OF:
                layer, j = MOD_OF[n]
                g = prm("norm_g2")[:, (3 * layer + j // 3) * KD:(3 * layer + j // 3 + 1) * KD]
                k = shift_index[n]
                dve.wait_ge(sem("x_updated"), 4 * n)
                dve.scalar_tensor_tensor(out=gmod[:, :], in0=mod_col(layer, j + 1), scalar=1.0, in1=g,
                                         op0=ALU.add, op1=ALU.mult).then_inc(sem("gmod_ready"), 1)
                dve.tensor_scalar(gres[:, :], mod_col(layer, j + 2), 1.0 if j == 3 else 0.5, None,
                                  ALU.mult).then_inc(sem("gmod_ready"), 1)
                dve.wait_ge(sem("gmod_ready"), 2 * k + 2)
                dve_norm(dve, n, gmod, mod_col(layer, j))
            else:
                dve_norm(dve, n, prm(GAIN_OF[n]), None, split=(n not in (3, 10)))

        def dve_phase_residual(dve, n):
            last = first_block[n] + phases[n][2] - 1
            acc = ACC if phases[n][0] == "ffn" else MIX_ACC
            if n in MOD_OF:
                dve_residual(dve, residual_index[n], last, gain=gres, acc=acc)
            else:
                dve_residual(dve, residual_index[n], last, acc=acc, scale=0.5 if n != 1 else 1.0)

        def pe_ffn(pe, n, f, groups):
            F0, S0 = first_block[n], STEPS * f
            pe_norm(pe, n)
            if S0:
                pe.wait_ge(sem("silu_done"), S0)
                pe.wait_ge(sem("hid_ready"), S0)
            pe_in(pe, F0, pair(GATE), first_pass_waits=4 * split_index[n])
            pe_in(pe, F0 + 1, pair(UP))

            def step(q, i, with_mod, g0):
                b = F0 + 2 + 3 * q
                pe.wait_ge(sem("silu_done"), S0 + 1 + q + 2 * i)
                pe_in(pe, b, pair(GATE), i, 6)
                pe.wait_ge(sem("hid_ready"), S0 + 1 + q + 2 * i)
                pe_in(pe, b + 1, pair(UP), i, 6)
                if q == 1 and with_mod:
                    pe.wait_ge(sem("mod_step"), 8 * (g0 + 1) + 8 * i)
                    for j in range(KD):
                        mm = pe.matmul(MODP[:, j:j + 1], mod_acc[:, j * P:j * P + P], ones[:, 0:1],
                                       start=True, stop=True)
                    mm.then_inc(sem("mod_reduced"), 1)
                pe.wait_ge(sem("hid_split"), S0 + 1 + q + 2 * i)
                return b + 2

            def turns(lo, hi, with_mod):
                g0 = group0[f]
                def turn(i, first):
                    for q in range(2):
                        b = step(q, i, with_mod, g0)
                        pe_out(pe, b, hid_hi[:, q], hid_lo[:, q], first and q == 0, False, i, 6)
                if lo == 0:
                    turn(0, True)
                    lo = 1
                if hi > lo:
                    with pe.Fori(lo, hi) as i:
                        turn(i, False)

            if groups:
                turns(0, groups, True)
            if groups < 5:
                turns(groups, 5, False)
            pe.wait_ge(sem("hid_split"), S0 + STEPS)
            pe_out(pe, F0 + 32, hid_hi[:, 0], hid_lo[:, 0], False, True)

        def act_ffn(act, n, f, groups):
            F0, S0 = first_block[n], STEPS * f
            act_norm(act, n)
            act_split(act, F0 + 2)

            def post(gate_block, s, parity, i=0, per=0, ps=0):
                act.wait_ge(sem("w_used"), gate_block + 1 + per * i)
                act.activation(gate[:, :, :], pair(GATE), ACT.Silu).then_inc(sem("silu_done"), 1)
                act.wait_ge(sem("hid_ready"), s + 1 + ps * i)
                act.activation(hid_hi[:, parity], hid[:, :, :], ACT.Copy).then_inc(sem("hid_rounded"), 1)

            post(F0, S0, 0)
            with act.Fori(0, 5) as i:
                for q in range(2):
                    b = F0 + 2 + 3 * q
                    act_split(act, b + 1, i, 6)
                    act_split(act, b + 2, i, 6)
                    act_split(act, b + 3, i, 6)
                    post(b, S0 + 1 + q, (1 + q) % 2, i, 6, 2)
            act_split(act, F0 + 33)
            act_split(act, F0 + 34)

        def dve_ffn(dve, n, f, groups):
            F0, S0 = first_block[n], STEPS * f
            dve_phase_norm(dve, n)
            dve_split(dve, F0 + 2)

            def post(up_block, s, parity, i=0, per=0, ps=0):
                dve.wait_ge(sem("silu_done"), s + 1 + ps * i)
                dve.wait_ge(sem("w_used"), up_block + 1 + per * i)
                dve.tensor_tensor(hid[:, :, :], gate[:, :, :], pair(UP), ALU.mult).then_inc(sem("hid_ready"), 1)
                dve.wait_ge(sem("hid_rounded"), s + 1 + ps * i)
                dve.tensor_tensor(hid_lo[:, parity], hid[:, :, :], hid_hi[:, parity].bitcast(F32), ALU.subtract)\
                   .then_inc(sem("hid_split"), 1)

            def mod_block(q, g0, i):
                s = q % 2
                dve.wait_ge(sem(f"mod_loaded{s}"), 16 * (2 * g0 + q // 2 + 1) + 32 * i)
                for t in range(2):
                    k = 2 * q + t
                    if k == 0:
                        if g0 > 0:
                            dve.wait_ge(sem("mod_reduced"), g0 + i)
                        ins = dve.tensor_scalar(mod_acc[:, :], mod_raw[:, s, 0:D], c_act[:, 0:1], None, ALU.mult)
                    else:
                        dve.wait_ge(sem("mod_step"), 8 * g0 + k + 8 * i)
                        ins = dve.scalar_tensor_tensor(out=mod_acc[:, :], in0=mod_raw[:, s, t * D:t * D + D],
                                                       scalar=c_act[:, k:k + 1], in1=mod_acc[:, :],
                                                       op0=ALU.mult, op1=ALU.add)
                    ins.then_inc(sem("mod_step"), 1)

            def mod_store(g0, i):
                dve.wait_ge(sem("mod_reduced"), g0 + 1 + i)
                lo, _ = P_AT["mod_b"]
                dve.tensor_tensor(mod_tab[:, ds(8 * g0 + 8 * i, 8)], MODP[:, 0:8],
                                  params[:, ds(lo + 8 * g0 + 8 * i, 8)], ALU.add).then_inc(sem("mod_stored"), 1)

            post(F0 + 1, S0, 0)

            def turns(lo, hi, with_mod):
                g0 = group0[f]
                with dve.Fori(lo, hi) as i:
                    for q in range(2):
                        b = F0 + 2 + 3 * q
                        dve_split(dve, b + 1, i, 6)
                        dve_split(dve, b + 2, i, 6)
                        dve_split(dve, b + 3, i, 6)
                        if with_mod and q == 1:
                            mod_block(3, g0, i)
                        post(b + 1, S0 + 1 + q, (1 + q) % 2, i, 6, 2)
                        if with_mod and q == 0:
                            for m in range(3):
                                mod_block(m, g0, i)
                        if with_mod and q == 1:
                            mod_store(g0, i)

            if groups:
                turns(0, groups, True)
            if groups < 5:
                turns(groups, 5, False)
            dve_split(dve, F0 + 33)
            dve_split(dve, F0 + 34)
            if groups:
                dve.wait_ge(sem("mod_stored"), group0[f] + groups)
            dve_phase_residual(dve, n)

        group0, g = {}, 0
        for f in range(6):
            group0[f] = g
            g += MOD_GROUPS[f]

        MIX_ACC = (STAT, MODP, GATE, UP)

        def over(ap, shape):
            return ap.unsqueeze(1).to_broadcast(shape)

        def row_pick(n_rows, r):
            return ident[0:n_rows, r:r + 1].to_broadcast([n_rows, P])

        def dve_conv(dve, name, src, dst, w, b, t0, done):
            step = 0
            for s in range(4):
                for m in range(2):
                    wcol = w[:, 4 * (t0 + m) + 3 - s:4 * (t0 + m) + 4 - s]
                    if s == 0:
                        ins = dve.tensor_scalar(dst[:, m, :], src[:, m, :], wcol, b[:, t0 + m:t0 + m + 1],
                                                ALU.mult, ALU.add)
                    else:
                        dve.wait_ge(sem(name), done + step - 1)
                        ins = dve.scalar_tensor_tensor(out=dst[:, m, s:T], in0=src[:, m, 0:T - s], scalar=wcol,
                                                       in1=dst[:, m, s:T], op0=ALU.mult, op1=ALU.add)
                    ins.then_inc(sem(name), 1)
                    step += 1

        def pe_mask(pe, out, which):
            return pe.matmul(out, ident, cst(which), start=False, stop=True, skip_group_check=True)

        (qk, v_tok, fo, gsu, sgu_v, pre, e1, p1) = region(
            m1_qk=([P, 16, T], F32), m1_v=([P, 2, D], F32), m1_fo=([P, KD, T], F32), m1_gsu=([P, KD, T], F32),
            m1_sgu_v=([P, 2, D], F32), m1_pre=([P, 2, 2, T], F32), m1_e=([P, 2, 384], F32), m1_p=([P, 2, 384], F32))
        sgu_gb = qk[:, 8:16, :]
        HEAD_A = {17: 0, 20: 1, 23: 2, 26: 3}
        HEAD_B = {18: 0, 21: 1, 24: 2, 27: 3}
        CCOLS_AFTER, MEAN_AFTER, VAR_AFTER, SGU_AFTER = 7, 28, 29, 31

        def pe_mix1(pe, n, _):
            F0 = first_block[n]
            pe_norm(pe, n)

            def blk(j, **kw):
                if 2 <= j < 10:
                    pe.wait_ge(sem("m1_conv"), 8 * (j - 1))
                elif j >= 10:
                    pe.wait_ge(sem("m1_evac"), j - 9)
                out = pair((GATE, UP)[j % 2])
                (pe_tok if 8 <= j < 16 else pe_in)(pe, F0 + j, out, **kw)

            def gates():
                for k in range(KD):
                    mm = pe.matmul(MODP[0:64, 0:T], prm("w_if")[:, k * 64:k * 64 + 64], xm[:, k, :],
                                   start=(k == 0), stop=(k == KD - 1))
                mm.then_inc(sem("m1_gates"), 1)

            def ccols():
                pe.wait_ge(sem("m1_row"), 13)
                for tt in range(2):
                    mm = pe.matmul(STAT[:, 4 * tt:4 * tt + 4], rows[0:4, 0, tt * P:tt * P + P], ident[0:4, 0:4],
                                   start=True, stop=True)
                mm.then_inc(sem("m1_ccols"), 1)

            def head_a(h):
                if h >= 1:
                    pe.wait_ge(sem("m1_p"), h)
                else:
                    pe.wait_ge(sem("m1_silu"), 8)
                for st in range(2):
                    for k in range(2):
                        mm = pe.matmul(ACC[0][:, 256 * st:256 * st + T - P * st], qk[:, 8 + 2 * h + k, st * P:st * P + P],
                                       qk[:, 2 * h + k, st * P:T], start=(st == 0 and k == 0), stop=(k == 1),
                                       skip_group_check=True)
                mm.then_inc(sem("m1_scores"), 1)
                if h >= 1:
                    pe.wait_ge(sem("m1_e_ready"), 2 * h)
                pe.matmul(ACC[1][:, 0:T], row_pick(4, h), rows[0:4, 2, :], start=True, stop=True, skip_group_check=True)
                pe.matmul(ACC[1][:, 256:384], row_pick(4, h), rows[0:4, 2, P:T], start=False, stop=True,
                          skip_group_check=True)
                pe_mask(pe, ACC[1][:, 0:P], "maskT")
                pe_mask(pe, ACC[1][:, 256:384], "maskT").then_inc(sem("m1_bias"), 1)

            def head_b(h):
                if h >= 1:
                    pe.wait_ge(sem("m1_h"), h)
                pe.wait_ge(sem("m1_p"), h + 1)
                p = p1[:, h % 2, :]
                pe.matmul(ACC[3][:, 0:T], ones, p[:, 0:T], start=True, stop=False, skip_group_check=True)
                pe.matmul(ACC[3][:, P:T], ones, p[:, 256:384], start=False, stop=True, skip_group_check=True)
                pe.matmul(ACC[3][:, T:2 * T], row_pick(4, h), rows[0:4, 3, :], start=False, stop=True,
                          skip_group_check=True).then_inc(sem("m1_den"), 1)
                for e in range(2):
                    c = h * DH_M + e * P
                    pe.matmul(ACC[2][:, e * T:e * T + T], v_tok[:, 0, c:c + P], p[:, 0:T], start=(e == 0), stop=False,
                              skip_group_check=True)
                    mm = pe.matmul(ACC[2][:, e * T + P:e * T + T], v_tok[:, 1, c:c + P], p[:, 256:384], start=False,
                                   stop=True, skip_group_check=True)
                mm.then_inc(sem("m1_num"), 1)

            def head_sums(src, ready, banks, done):
                for h in range(HEADS_M):
                    pe.wait_ge(sem(ready), h + 1)
                    for e in range(2):
                        mm = pe.matmul(pair(banks[h // 2])[:, h % 2, :], ones, src[:, 2 * h + e, :], start=(e == 0),
                                       stop=(e == 1))
                    mm.then_inc(sem(done), 1)

            def sgu():
                pe.wait_ge(sem("m1_centred"), 4)
                pe.wait_ge(sem("m1_std"), 2)
                pe.wait_ge(sem("m1_sgu_ready"), 2)
                for c in range(KD):
                    for nb in range(2):
                        out = pair(ACC[c // 2])[:, c % 2, nb * P:nb * P + P]
                        pe.matmul(out, sgu_v[:, nb, c * P:c * P + P], prm("sgu_wT")[:, (c // 2) * P:(c // 2) * P + P],
                                  start=True, stop=False, skip_group_check=True)
                        mm = pe.matmul(out, row_pick(4, c // 2), prm("sgu_bs")[0:4, :], start=False, stop=True,
                                       skip_group_check=True)
                    if c % 2 == 1:
                        mm.then_inc(sem("m1_sgu_mixed"), 1)

            for j in range(MIX1_IN):
                blk(j, **({"first_pass_waits": 4 * split_index[n]} if j == 0 else {}))
                if j == 1:
                    gates()
                if j == CCOLS_AFTER:
                    ccols()
                if j in HEAD_A:
                    head_a(HEAD_A[j])
                if j in HEAD_B:
                    head_b(HEAD_B[j])
                if j == MEAN_AFTER:
                    pe.wait_ge(sem("m1_p"), 4)
                    pe.wait_ge(sem("m1_e_ready"), 8)
                    head_sums(qk, "m1_h", ACC[0:2], "m1_mean")
                if j == VAR_AFTER:
                    head_sums(xm, "m1_squared", ACC[2:4], "m1_var")
                if j == SGU_AFTER:
                    sgu()
            for b in range(MIX1_OUT):
                if b == 0:
                    pe.wait_ge(sem("m1_evac"), 24)
                pe.wait_ge(sem("m1_split"), b + 1)
                pe_out(pe, F0 + MIX1_IN + b, xh[:, 2 * b:2 * b + 2, :], xl[:, 2 * b:2 * b + 2, :], b == 0,
                       b == MIX1_OUT - 1, acc=MIX_ACC)

        def act_mix1(act, n, _):
            F0 = first_block[n]
            act_norm(act, n)
            r = rows

            def row_chain():
                act.wait_ge(sem("m1_gates"), 1)
                act.activation(r[0:4, 0, :], MODP[0:4, 0:T], ACT.Identity, bias=prm("b_i")[0:4, :]).then_inc(sem("m1_row"), 1)
                act.activation(r[0:4, 1, :], MODP[32:36, 0:T], ACT.Identity, bias=prm("b_f")[32:36, :])\
                   .then_inc(sem("m1_row"), 1)
                act.wait_ge(sem("m1_row"), 2)
                act.activation(r[0:4, 2, :], r[0:4, 1, :], ACT.Abs).then_inc(sem("m1_row"), 1)
                act.wait_ge(sem("m1_row"), 3)
                act.activation(r[0:4, 2, :], r[0:4, 2, :], ACT.Exp, scale=-1.0).then_inc(sem("m1_row"), 1)
                act.wait_ge(sem("m1_row"), 4)
                act.activation(r[0:4, 2, :], r[0:4, 2, :], ACT.Ln, bias=cst("ones")[0:4, 0:1]).then_inc(sem("m1_row"), 1)
                act.wait_ge(sem("m1_row"), 12)
                act.activation(r[0:4, 3, :], r[0:4, 3, :], ACT.Exp, scale=-1.0).then_inc(sem("m1_row"), 1)

            def head_a(h):
                if h == 0:
                    act.wait_ge(sem("m1_cols"), 1)
                if h >= 2:
                    act.wait_ge(sem("m1_p"), h - 1)
                act.wait_ge(sem("m1_bias"), h + 1)
                for st in range(2):
                    c0, c1 = 256 * st, 256 * st + T - P * st
                    act.activation(e1[:, h % 2, c0:c1], ACC[1][:, c0:c1], ACT.Exp,
                                   bias=cols[:, 4 * st + h:4 * st + h + 1]).then_inc(sem("m1_e_ready"), 1)

            def head_b(h):
                act.wait_ge(sem("m1_den"), h + 1)
                if h >= 1:
                    act.wait_ge(sem("m1_h"), h)
                act.activation(std[:, :], ACC[3][:, 0:T], ACT.Abs).then_inc(sem("m1_abs"), 1)

            def blk(j):
                act_split(act, F0 + j + 2)
                bank_j = pair((GATE, UP)[j % 2])
                if j < 8:
                    act.wait_ge(sem("m1_conv"), 8 * j + 8)
                    act.activation(qk[:, 2 * j:2 * j + 2, :], pre[:, j % 2], ACT.Silu).then_inc(sem("m1_silu"), 1)
                    return
                act.wait_ge(sem("w_used"), F0 + j + 1)
                c = (j % 4) * 256
                if j < 12:
                    act.activation(v_tok[:, :, c:c + 256], bank_j, ACT.Copy).then_inc(sem("m1_evac"), 1)
                elif j < 16:
                    act.activation(sgu_v[:, :, c:c + 256], bank_j, ACT.Gelu).then_inc(sem("m1_evac"), 1)
                    if j == 15:
                        for tt in range(2):
                            act.wait_ge(sem("m1_sgu_var"), tt + 1)
                            act.activation(cols[:, 20 + tt:21 + tt], cols[:, 17 + 2 * tt:18 + 2 * tt], ACT.Sqrt,
                                           bias=cols[:, 65:66]).then_inc(sem("m1_sgu_std"), 1)
                else:
                    k = 2 * (j % 4)
                    if j < 20:
                        dst, f = fo[:, k:k + 2, :], ACT.Sigmoid
                    elif j < 24:
                        dst, f = pre[:, j % 2], ACT.Sigmoid
                    elif j < 28:
                        dst, f = gsu[:, k:k + 2, :], ACT.Sigmoid
                    else:
                        dst, f = pre[:, j % 2], ACT.Gelu
                    if 22 <= j < 24:
                        act.wait_ge(sem("m1_gated"), j - 21)
                    if j >= 28:
                        act.wait_ge(sem("m1_gated"), 4 + max(0, j - 29))
                    act.activation(dst, bank_j, f).then_inc(sem("m1_evac"), 1)

            act_split(act, F0 + 2)
            for j in range(MIX1_IN):
                if j >= 1:
                    blk(j)
                else:
                    act.wait_ge(sem("m1_conv"), 8)
                    act.activation(qk[:, 0:2, :], pre[:, 0], ACT.Silu).then_inc(sem("m1_silu"), 1)
                if j == 1:
                    row_chain()
                if j in HEAD_A:
                    head_a(HEAD_A[j])
                    if HEAD_A[j] == 3:
                        act.wait_ge(sem("m1_scores"), 4)
                        act.dma_start(sgu_gb, a_sgu.rearrange("p (k t) -> p k t", k=KD)).then_inc(sem("sgu_loaded"), 16)
                if j in HEAD_B:
                    head_b(HEAD_B[j])
                if j == MEAN_AFTER:
                    for h in range(HEADS_M):
                        act.wait_ge(sem("m1_centred"), h + 1)
                        act.activation(xm[:, 2 * h:2 * h + 2, :], qk[:, 2 * h:2 * h + 2, :], ACT.Square)\
                           .then_inc(sem("m1_squared"), 1)
                if j == VAR_AFTER + 1:
                    for b in range(2):
                        act.wait_ge(sem("m1_var"), 2 * b + 2)
                        act.activation(e1[:, :, :].rearrange("p a b -> p (a b)")[:, 0:512] if b == 0 else
                                       p1[:, :, :].rearrange("p a b -> p (a b)")[:, 0:512], ACC[2 + b][:, :], ACT.Sqrt,
                                       scale=1.0 / DH_M, bias=cols[:, 65:66]).then_inc(sem("m1_std"), 1)
            for b in range(4):
                act.wait_ge(sem("m1_merged"), b + 1)
                act.activation(xh[:, 2 * b:2 * b + 2, :], xm[:, 2 * b:2 * b + 2, :], ACT.Copy).then_inc(sem("m1_rounded"), 1)
                act_split(act, F0 + MIX1_IN + 2 + b)

        def dve_mix1(dve, n, _):
            F0 = first_block[n]
            dve_phase_norm(dve, n)
            wt = prm("sgu_wT").rearrange("p (g t) -> p g t", g=SGU_G)
            dve.memset(wt[64:128, :, 0:64], 0.0).then_inc(sem("m1_masked"), 1)

            def row_chain():
                r = rows
                dve.wait_ge(sem("m1_row"), 5)
                dve.tensor_scalar(r[0:4, 3, :], r[0:4, 1, :], 0.0, None, ALU.min).then_inc(sem("m1_row"), 1)
                dve.wait_ge(sem("m1_row"), 6)
                dve.tensor_tensor(r[0:4, 3, :], r[0:4, 3, :], r[0:4, 2, :], ALU.subtract).then_inc(sem("m1_row"), 1)
                dve.wait_ge(sem("m1_row"), 7)
                dve.tensor_tensor_scan(r[0:4, 4, :], ones[0:4, 0:1].to_broadcast([4, T]), r[0:4, 3, :], 0.0,
                                       ALU.mult, ALU.add).then_inc(sem("m1_row"), 1)
                dve.wait_ge(sem("m1_row"), 8)
                dve.tensor_tensor(r[0:4, 0, :], r[0:4, 0, :], r[0:4, 4, :], ALU.subtract).then_inc(sem("m1_row"), 1)
                dve.wait_ge(sem("m1_row"), 9)
                dve.tensor_tensor_scan(r[0:4, 1, :], r[0:4, 0, :], r[0:4, 0, :], 0.0, ALU.max, ALU.max)\
                   .then_inc(sem("m1_row"), 1)
                dve.wait_ge(sem("m1_row"), 10)
                dve.tensor_tensor(r[0:4, 3, :], r[0:4, 4, :], r[0:4, 1, :], ALU.add).then_inc(sem("m1_row"), 1)
                dve.tensor_scalar(r[0:4, 2, :], r[0:4, 1, :], -1.0, None, ALU.mult).then_inc(sem("m1_row"), 1)

            def head_a(h):
                dve.wait_ge(sem("m1_scores"), h + 1)
                dve.wait_ge(sem("m1_e_ready"), 2 * h + 2)
                if h >= 2:
                    dve.wait_ge(sem("m1_num"), h - 1)
                dve.scalar_tensor_tensor(out=p1[:, h % 2, :], in0=ACC[0][:, 0:384], scalar=DH_M ** -0.5,
                                         in1=e1[:, h % 2, :], op0=ALU.mult, op1=ALU.mult).then_inc(sem("m1_p"), 1)

            def head_b(h):
                dve.wait_ge(sem("m1_abs"), h + 1)
                dve.tensor_tensor(rstd[:, :], std[:, :], ACC[3][:, T:2 * T], ALU.max).then_inc(sem("m1_div"), 1)
                dve.wait_ge(sem("m1_div"), 2 * h + 1)
                dve.reciprocal(rstd[:, :], rstd[:, :]).then_inc(sem("m1_div"), 1)
                dve.wait_ge(sem("m1_div"), 2 * h + 2)
                dve.wait_ge(sem("m1_num"), h + 1)
                dve.tensor_tensor(qk[:, 2 * h:2 * h + 2, :], pair(ACC[2]), over(rstd[:, :], [P, 2, T]), ALU.mult)\
                   .then_inc(sem("m1_h"), 1)

            def sgu_stats():
                for tt in range(2):
                    st = rstats[:, tt]
                    dve.wait_ge(sem("m1_evac"), 8)
                    for half in range(2):
                        dve.bn_stats(st[:, 6 * half:6 * half + 6], sgu_v[:, tt, 512 * half:512 * half + 512])\
                           .then_inc(sem("m1_bn"), 1)
                    dve.wait_ge(sem("m1_bn"), 2 * tt + 2)
                    dve.bn_aggr(cols[:, 16 + 2 * tt:18 + 2 * tt], st).then_inc(sem("m1_sgu_var"), 1)

            def sgu_norm():
                gb = sgu_gb.rearrange("p k t -> p (k t)")
                for tt in range(2):
                    dve.wait_ge(sem("m1_sgu_std"), tt + 1)
                    dve.reciprocal(cols[:, 22 + tt:23 + tt], cols[:, 20 + tt:21 + tt]).then_inc(sem("m1_sgu_step"), 1)
                    dve.wait_ge(sem("m1_sgu_step"), 3 * tt + 1)
                    v = sgu_v[:, tt, :]
                    dve.tensor_scalar(v, v, cols[:, 16 + 2 * tt:17 + 2 * tt], cols[:, 22 + tt:23 + tt], ALU.subtract,
                                      ALU.mult).then_inc(sem("m1_sgu_step"), 1)
                    dve.wait_ge(sem("m1_sgu_step"), 3 * tt + 2)
                    dve.wait_ge(sem("sgu_loaded"), 16)
                    dve.tensor_tensor(v, v, gb[:, 0:D], ALU.mult).then_inc(sem("m1_sgu_step"), 1)
                    dve.wait_ge(sem("m1_sgu_step"), 3 * tt + 3)
                    dve.tensor_tensor(v, v, gb[:, D:2 * D], ALU.add).then_inc(sem("m1_sgu_ready"), 1)

            def blk(j):
                bank_j = pair((GATE, UP)[j % 2])
                if j < 8:
                    dve.wait_ge(sem("w_used"), F0 + j + 1)
                    if j >= 2:
                        dve.wait_ge(sem("m1_silu"), j - 1)
                    dve_conv(dve, "m1_conv", bank_j, pre[:, j % 2], prm("conv_w1"), prm("conv_b1"), 2 * j, 8 * j)
                elif 20 <= j < 24:
                    k = 2 * (j % 4)
                    dve.wait_ge(sem("m1_evac"), j - 7)
                    dve.tensor_tensor(fo[:, k:k + 2, :], fo[:, k:k + 2, :], pre[:, j % 2], ALU.mult)\
                       .then_inc(sem("m1_gated"), 1)
                elif j >= 28:
                    k = 2 * (j % 4)
                    dve.wait_ge(sem("m1_evac"), j - 7)
                    dve.tensor_tensor(gsu[:, k:k + 2, :], gsu[:, k:k + 2, :], pre[:, j % 2], ALU.mult)\
                       .then_inc(sem("m1_gated"), 1)

            def finish_heads():
                for b in range(2):
                    s = (e1, p1)[b][:, :, :].rearrange("p a b -> p (a b)")[:, 0:512]
                    dve.wait_ge(sem("m1_std"), b + 1)
                    dve.reciprocal(s, s).then_inc(sem("m1_inv"), 1)
                    dve.wait_ge(sem("m1_inv"), b + 1)
                    for h in (2 * b, 2 * b + 1):
                        hp = qk[:, 2 * h:2 * h + 2, :]
                        dve.tensor_tensor(hp, hp, over(s[:, (h % 2) * T:(h % 2) * T + T], [P, 2, T]), ALU.mult)\
                           .then_inc(sem("m1_normed"), 1)
                for k in range(KD):
                    if k % 2 == 0:
                        dve.wait_ge(sem("m1_normed"), k // 2 + 1)
                    dve.scalar_tensor_tensor(out=qk[:, k, :], in0=qk[:, k, :], scalar=prm("head_g")[:, k:k + 1],
                                             in1=fo[:, k, :], op0=ALU.mult, op1=ALU.mult).then_inc(sem("m1_branch"), 1)

            dve_split(dve, F0 + 2)
            for j in range(MIX1_IN):
                if j >= 1:
                    dve_split(dve, F0 + j + 2)
                blk(j)
                if j == 1:
                    row_chain()
                if j == CCOLS_AFTER:
                    dve.wait_ge(sem("m1_ccols"), 1)
                    dve.tensor_copy(cols[:, 0:8], STAT[:, 0:8]).then_inc(sem("m1_cols"), 1)
                if j == 15:
                    sgu_stats()
                if j in HEAD_A:
                    head_a(HEAD_A[j])
                if j in HEAD_B:
                    head_b(HEAD_B[j])
                if j == MEAN_AFTER:
                    for h in range(HEADS_M):
                        dve.wait_ge(sem("m1_mean"), 2 * (h // 2) + 2)
                        hp = qk[:, 2 * h:2 * h + 2, :]
                        mean = over(ACC[h // 2][:, (h % 2) * T:(h % 2) * T + T], [P, 2, T])
                        dve.scalar_tensor_tensor(out=hp, in0=mean, scalar=-1.0 / DH_M, in1=hp, op0=ALU.mult, op1=ALU.add)\
                           .then_inc(sem("m1_centred"), 1)
                    sgu_norm()
                if j == VAR_AFTER + 1:
                    finish_heads()

            def rest(b):
                dve.wait_ge(sem("m1_rounded"), b + 1)
                dve.tensor_tensor(xl[:, 2 * b:2 * b + 2, :], xm[:, 2 * b:2 * b + 2, :],
                                  xh[:, 2 * b:2 * b + 2, :].bitcast(F32), ALU.subtract).then_inc(sem("m1_split"), 1)

            for b in range(4):
                k = 2 * b
                dve.wait_ge(sem("m1_sgu_mixed"), b + 1)
                dve.wait_ge(sem("m1_gated"), 4 + b + 1)
                dve.wait_ge(sem("m1_branch"), k + 2)
                dve.tensor_tensor(xm[:, k:k + 2, :], pair(ACC[b]), gsu[:, k:k + 2, :], ALU.mult).then_inc(sem("m1_sum"), 1)
                dve.wait_ge(sem("m1_sum"), b + 1)
                dve.tensor_tensor(xm[:, k:k + 2, :], xm[:, k:k + 2, :], qk[:, k:k + 2, :], ALU.add)\
                   .then_inc(sem("m1_merged"), 1)
                if b >= 1:
                    rest(b - 1)
            rest(3)
            for b in range(4):
                dve_split(dve, F0 + MIX1_IN + 2 + b)
            dve_phase_residual(dve, n)

        (xbc, pu, zs, x_tok, cb, pre2, e2, p2, cat_hi, cat_lo) = region(
            m2_xbc=([P, 12, T], F32), m2_pu=([P, 4, T], F32), m2_zs=([P, KD, T], F32), m2_x_tok=([P, 2, D], F32),
            m2_cb=([P, 2, 384], F32), m2_pre=([P, 2, 2, T], F32), m2_e=([P, 2, 384], F32), m2_p=([P, 2, 384], F32),
            m2_cat_hi=([P, 4, T], F32R), m2_cat_lo=([P, 4, T], F32R))
        NEG_A, DT_C = 0, 32

        def pe_mix2(pe, n, _):
            F0 = first_block[n]
            pe_norm(pe, n)

            def blk(j, **kw):
                if 2 <= j < 8:
                    pe.wait_ge(sem("m2_conv"), 8 * (j - 1))
                elif j >= 8:
                    pe.wait_ge(sem("m2_evac"), j - 7)
                pe_in(pe, F0 + j, pair((GATE, UP)[j % 2]), **kw)

            def dt():
                for k in range(KD):
                    mm = pe.matmul(MODP[0:16, 0:T], prm("w_dt")[:, k * 16:k * 16 + 16], xm[:, k, :],
                                   start=(k == 0), stop=(k == KD - 1))
                mm.then_inc(sem("m2_dt"), 1)

            def columns():
                pe.wait_ge(sem("m2_row"), 9)
                for r in range(2):
                    for tt in range(2):
                        mm = pe.matmul(STAT[:, 32 * r + 16 * tt:32 * r + 16 * tt + 16],
                                       rows[0:16, 4 - r, tt * P:tt * P + P], ident[0:16, 0:16], start=True, stop=True)
                mm.then_inc(sem("m2_columns"), 1)

            def turn_x():
                pe.wait_ge(sem("m2_silu"), 4)
                for q in range(4):
                    tt, half = q // 2, q % 2
                    for c in range(4):
                        mm = pe.transpose(ACC[q][:, c * P:c * P + P], xbc[:, 4 * half + c, tt * P:tt * P + P], ident)
                    mm.then_inc(sem("m2_turned"), 1)

            def cb_products():
                pe.wait_ge(sem("m2_silu"), 6)
                for g in range(2):
                    pe.wait_ge(sem("m2_x_tok"), g + 1)
                    pe.matmul(ACC[g][:, 0:T], xbc[:, 8 + g, 0:P], xbc[:, 10 + g, :], start=True, stop=True,
                              skip_group_check=True)
                    pe.matmul(ACC[g][:, 256:384], xbc[:, 8 + g, P:T], xbc[:, 10 + g, P:T], start=False, stop=True,
                              skip_group_check=True).then_inc(sem("m2_cb"), 1)

            def pool():
                pe.wait_ge(sem("m2_x_tok"), 4)
                pe.wait_ge(sem("m2_pool_d"), 4)
                for g in range(4):
                    mm = pe.matmul(pair(ACC[2 + g // 2])[:, g % 2, :], prm("pool_w")[:, g * P:g * P + P], xm[:, g, :],
                                   start=True, stop=True)
                    if g % 2 == 1:
                        mm.then_inc(sem("m2_pooled"), 1)

            def bias(h):
                b = ACC[h % 2]
                if h == 0:
                    pe.wait_ge(sem("m2_cb_read"), 2)
                if h >= 2:
                    pe.wait_ge(sem("m2_e_ready"), 2 * (h - 1))
                pe.matmul(b[:, 0:T], row_pick(16, h), rows[0:16, 4, :], start=True, stop=True, skip_group_check=True)
                pe.matmul(b[:, 256:384], row_pick(16, h), rows[0:16, 4, P:T], start=False, stop=True,
                          skip_group_check=True)
                pe_mask(pe, b[:, 0:P], "maskT")
                pe_mask(pe, b[:, 256:384], "maskT").then_inc(sem("m2_bias"), 1)

            def head(h):
                k, r0 = h // 2, 64 * (h % 2)
                out = ACC[2 + k % 2]
                pe.wait_ge(sem("m2_m_ready"), 2 * h + 2)
                if h == 0:
                    pe.wait_ge(sem("m2_cat"), 4)
                if h >= 4 and h % 2 == 0:
                    pe.wait_ge(sem("m2_y"), k - 1)
                p = p2[:, h % 2, :]
                pe.matmul(out[r0:r0 + 64, 0:T], x_tok[:, 0, h * 64:h * 64 + 64], p[:, 0:T], start=True, stop=False,
                          skip_group_check=True)
                pe.matmul(out[r0:r0 + 64, P:T], x_tok[:, 1, h * 64:h * 64 + 64], p[:, 256:384], start=False, stop=True,
                          skip_group_check=True).then_inc(sem("m2_head"), 1)

            for j in range(MIX2_IN):
                blk(j, **({"first_pass_waits": 4 * split_index[n]} if j == 0 else {}))
                if j == 1:
                    dt()
                if j == 6:
                    columns()
                    turn_x()
                if j == 8:
                    cb_products()
                if j == 10:
                    pool()
            bias(0)
            for h in range(SSD_H):
                if h + 1 < SSD_H:
                    bias(h + 1)
                head(h)
            for g in range(2):
                for k in range(4 * g, 4 * g + 4):
                    if k % 2 == 0:
                        pe.wait_ge(sem("m2_squared"), k // 2 + 1)
                    mm = pe.matmul(ACC[g][:, 0:T], ones, zs[:, k, :], start=(k % 4 == 0), stop=(k % 4 == 3))
                mm.then_inc(sem("m2_var"), 1)
            for b in range(MIX2_OUT):
                if b < 2:
                    if b == 0:
                        pe.wait_ge(sem("m2_evac"), 6)
                    pe.wait_ge(sem("m2_cat"), 4)
                    hi, lo = cat_hi[:, 2 * b:2 * b + 2, :], cat_lo[:, 2 * b:2 * b + 2, :]
                else:
                    pe.wait_ge(sem("m2_split"), b - 1)
                    hi, lo = xh[:, 2 * b - 4:2 * b - 2, :], xl[:, 2 * b - 4:2 * b - 2, :]
                pe_out(pe, F0 + MIX2_IN + b, hi, lo, b == 0, b == MIX2_OUT - 1, acc=MIX_ACC)

        def act_mix2(act, n, _):
            F0 = first_block[n]
            act_norm(act, n)
            r = rows

            def row_chain():
                act.wait_ge(sem("m2_dt"), 1)
                act.activation(r[0:16, 0, :], MODP[0:16, 0:T], ACT.Identity, bias=prm("dt_bias")[0:16, :])\
                   .then_inc(sem("m2_row"), 1)
                act.activation(rstd[0:16, 0:1], prm("a_log")[0:16, :], ACT.Exp).then_inc(sem("m2_row"), 1)
                act.wait_ge(sem("m2_row"), 2)
                act.activation(r[0:16, 1, :], r[0:16, 0, :], ACT.Abs).then_inc(sem("m2_row"), 1)
                act.wait_ge(sem("m2_row"), 3)
                act.activation(r[0:16, 1, :], r[0:16, 1, :], ACT.Exp, scale=-1.0).then_inc(sem("m2_row"), 1)
                act.wait_ge(sem("m2_row"), 4)
                act.activation(r[0:16, 1, :], r[0:16, 1, :], ACT.Ln, bias=cst("ones")[0:16, 0:1]).then_inc(sem("m2_row"), 1)

            def blk(j):
                bank_j = pair((GATE, UP)[j % 2])
                if j < 6:
                    act.wait_ge(sem("m2_conv"), 8 * j + 8)
                    act.activation(xbc[:, 2 * j:2 * j + 2, :], pre2[:, j % 2], ACT.Silu).then_inc(sem("m2_silu"), 1)
                    return
                act.wait_ge(sem("w_used"), F0 + j + 1)
                k = 2 * (j - 6) if j < 8 else 2 * (j - 8)
                act.activation((pu if j < 8 else zs)[:, k:k + 2, :], bank_j, ACT.Copy if j < 8 else ACT.Silu)\
                   .then_inc(sem("m2_evac"), 1)

            act_split(act, F0 + 2)
            for j in range(MIX2_IN):
                if j >= 1:
                    act_split(act, F0 + j + 2)
                blk(j)
                if j == 1:
                    row_chain()
                if j == 7:
                    for q in range(4):
                        act.wait_ge(sem("m2_turned"), q + 1)
                        act.activation(x_tok[:, q // 2, 512 * (q % 2):512 * (q % 2) + 512], ACC[q][:, :], ACT.Copy)\
                           .then_inc(sem("m2_x_tok"), 1)
                if j == 11:
                    for g in range(4):
                        act.wait_ge(sem("m2_pooled"), g // 2 + 1)
                        act.activation(cat_hi[:, g, :], pair(ACC[2 + g // 2])[:, g % 2, :], ACT.Identity,
                                       scale=prm("pool_scale")[:, g:g + 1]).then_inc(sem("m2_cat_hi"), 1)
            for h in range(SSD_H):
                act.wait_ge(sem("m2_bias"), h + 1)
                if h == 0:
                    act.wait_ge(sem("m2_cols"), 2)
                if h >= 2:
                    act.wait_ge(sem("m2_m_ready"), 2 * (h - 1))
                for st in range(2):
                    c0, c1 = 256 * st, 256 * st + T - P * st
                    a = NEG_A + 16 * st + h
                    act.activation(e2[:, h % 2, c0:c1], ACC[h % 2][:, c0:c1], ACT.Exp, bias=cols[:, a:a + 1])\
                       .then_inc(sem("m2_e_ready"), 1)
            for b in range(4):
                act.wait_ge(sem("m2_gated"), b + 1)
                act.activation(zs[:, 2 * b:2 * b + 2, :], xm[:, 2 * b:2 * b + 2, :], ACT.Square)\
                   .then_inc(sem("m2_squared"), 1)
            for g in range(2):
                act.wait_ge(sem("m2_var"), g + 1)
                act.activation(e2[:, g, 0:T], ACC[g][:, 0:T], ACT.Sqrt, scale=1.0 / 512, bias=cols[:, 64:65])\
                   .then_inc(sem("m2_std"), 1)
            for b in range(4):
                act.wait_ge(sem("m2_normed"), b + 1)
                act.activation(xh[:, 2 * b:2 * b + 2, :], xm[:, 2 * b:2 * b + 2, :], ACT.Copy).then_inc(sem("m2_rounded"), 1)
            for b in range(MIX2_OUT):
                act_split(act, F0 + MIX2_IN + 2 + b)

        def dve_mix2(dve, n, _):
            F0 = first_block[n]
            dve_phase_norm(dve, n)
            r = rows

            def row_chain():
                dve.wait_ge(sem("m2_row"), 5)
                dve.tensor_scalar(r[0:16, 2, :], r[0:16, 0, :], 0.0, None, ALU.max).then_inc(sem("m2_row"), 1)
                dve.wait_ge(sem("m2_row"), 6)
                dve.tensor_tensor(r[0:16, 3, :], r[0:16, 2, :], r[0:16, 1, :], ALU.add).then_inc(sem("m2_row"), 1)
                dve.wait_ge(sem("m2_row"), 7)
                dve.tensor_scalar(r[0:16, 0, :], r[0:16, 3, :], rstd[0:16, 0:1], -1.0, ALU.mult, ALU.mult)\
                   .then_inc(sem("m2_row"), 1)
                dve.wait_ge(sem("m2_row"), 8)
                dve.tensor_tensor_scan(r[0:16, 4, :], ones[0:16, 0:1].to_broadcast([16, T]), r[0:16, 0, :], 0.0,
                                       ALU.mult, ALU.add).then_inc(sem("m2_row"), 1)

            def pool():
                step = 0
                src, halves = pu, (xm[:, 0:4, :], xm[:, 4:8, :])
                dve.wait_ge(sem("m2_evac"), 2)
                for lv in range(4):
                    sh, dst = 1 << lv, halves[(lv + 1) % 2]
                    if lv:
                        dve.wait_ge(sem("m2_pool"), step)
                    if lv:
                        dve.tensor_copy(dst[:, 0:lv, :], src[:, 0:lv, :]).then_inc(sem("m2_pool"), 1)
                        step += 1
                    dve.tensor_copy(dst[:, lv:4, 0:sh], src[:, lv:4, 0:sh]).then_inc(sem("m2_pool"), 1)
                    dve.tensor_tensor(dst[:, lv:4, sh:T], src[:, lv:4, sh:T], src[:, lv:4, 0:T - sh], ALU.add)\
                       .then_inc(sem("m2_pool"), 1)
                    step += 2
                    src = dst
                fix = cst("pool_fix").rearrange("p (g t) -> p g t", g=4)
                dve.wait_ge(sem("m2_pool"), step)
                dve.tensor_tensor(src[:, :, 0:16], src[:, :, 0:16], fix, ALU.mult).then_inc(sem("m2_pool"), 1)
                dve.wait_ge(sem("m2_pool"), step + 1)
                assert step == 11
                for g in range(4):
                    ins = dve.scalar_tensor_tensor(out=src[:, g, :], in0=src[:, g, :], scalar=1.0 / (2 << g),
                                                   in1=pu[:, g, :], op0=ALU.mult, op1=ALU.subtract)
                    ins.then_inc(sem("m2_pool_d"), 1)

            dve_split(dve, F0 + 2)
            for j in range(MIX2_IN):
                if j >= 1:
                    dve_split(dve, F0 + j + 2)
                if j < 6:
                    dve.wait_ge(sem("w_used"), F0 + j + 1)
                    if j >= 2:
                        dve.wait_ge(sem("m2_silu"), j - 1)
                    dve_conv(dve, "m2_conv", pair((GATE, UP)[j % 2]), pre2[:, j % 2], prm("conv_w2"), prm("conv_b2"),
                             2 * j, 8 * j)
                if j == 1:
                    row_chain()
                if j == 7:
                    dve.wait_ge(sem("m2_columns"), 1)
                    dve.tensor_scalar(cols[:, NEG_A:NEG_A + 32], STAT[:, 0:32], -1.0, None, ALU.mult)\
                       .then_inc(sem("m2_cols"), 1)
                    dve.tensor_copy(cols[:, DT_C:DT_C + 32], STAT[:, 32:64]).then_inc(sem("m2_cols"), 1)
                    pool()
                if j == 9:
                    for g in range(2):
                        dve.wait_ge(sem("m2_cb"), g + 1)
                        dve.tensor_copy(cb[:, g, :], ACC[g][:, 0:384]).then_inc(sem("m2_cb_read"), 1)
                if j == 11:
                    for g in range(4):
                        dve.wait_ge(sem("m2_cat_hi"), 2 * (g // 2) + 2)
                        dve.scalar_tensor_tensor(out=cat_lo[:, g, :], in0=pair(ACC[2 + g // 2])[:, g % 2, :],
                                                 scalar=prm("pool_scale")[:, g:g + 1], in1=cat_hi[:, g, :].bitcast(F32),
                                                 op0=ALU.mult, op1=ALU.subtract).then_inc(sem("m2_cat"), 1)
            for h in range(SSD_H):
                if h == 0:
                    dve.wait_ge(sem("m2_cb_read"), 2)
                    dve.wait_ge(sem("m2_cols"), 2)
                if h >= 2:
                    dve.wait_ge(sem("m2_head"), h - 1)
                for st in range(2):
                    c0, c1 = 256 * st, 256 * st + T - P * st
                    d = DT_C + 16 * st + h
                    dve.wait_ge(sem("m2_e_ready"), 2 * h + st + 1)
                    dve.scalar_tensor_tensor(out=p2[:, h % 2, c0:c1], in0=e2[:, h % 2, c0:c1], scalar=cols[:, d:d + 1],
                                             in1=cb[:, h // 8, c0:c1], op0=ALU.mult, op1=ALU.mult)\
                       .then_inc(sem("m2_m_ready"), 1)
                if h % 2 == 1:
                    y_pair(dve, h // 2 - 1)
            y_pair(dve, 7)
            for b in range(4):
                dve.wait_ge(sem("m2_y"), 2 * b + 2)
                if b == 0:
                    dve.wait_ge(sem("m2_evac"), 6)
                dve.tensor_tensor(xm[:, 2 * b:2 * b + 2, :], xm[:, 2 * b:2 * b + 2, :], zs[:, 2 * b:2 * b + 2, :],
                                  ALU.mult).then_inc(sem("m2_gated"), 1)
            for g in range(2):
                dve.wait_ge(sem("m2_std"), g + 1)
                dve.reciprocal(e2[:, g, 0:T], e2[:, g, 0:T]).then_inc(sem("m2_inv"), 1)
                dve.wait_ge(sem("m2_inv"), g + 1)
                for k in range(4 * g, 4 * g + 4):
                    ins = dve.scalar_tensor_tensor(out=xm[:, k, :], in0=xm[:, k, :], scalar=prm("ssd_g")[:, k:k + 1],
                                                   in1=e2[:, g, 0:T], op0=ALU.mult, op1=ALU.mult)
                    if k % 2 == 1:
                        ins.then_inc(sem("m2_normed"), 1)
            for b in range(4):
                dve.wait_ge(sem("m2_rounded"), b + 1)
                dve.tensor_tensor(xl[:, 2 * b:2 * b + 2, :], xm[:, 2 * b:2 * b + 2, :],
                                  xh[:, 2 * b:2 * b + 2, :].bitcast(F32), ALU.subtract).then_inc(sem("m2_split"), 1)
            for b in range(MIX2_OUT):
                dve_split(dve, F0 + MIX2_IN + 2 + b)
            dve_phase_residual(dve, n)

        def y_pair(dve, k):
            if k < 0:
                return
            dve.wait_ge(sem("m2_head"), 2 * k + 2)
            if k == 0:
                dve.wait_ge(sem("m2_pooled"), 2)
            dve.scalar_tensor_tensor(out=xm[:, k, :], in0=xbc[:, k, :], scalar=prm("ssd_d")[:, k:k + 1],
                                     in1=ACC[2 + k % 2][:, 0:T], op0=ALU.mult, op1=ALU.add).then_inc(sem("m2_y"), 1)

        (qt, kt, v3, qs, t1, e3, pt3, kr, nm, pos_i, ang) = region(
            m3_qt=([P, MLA_H, T], F32), m3_kt=([P, MLA_H, T], F32), m3_v=([P, 2, D], F32), m3_qs=([P, 2, 2, T], F32),
            m3_t1=([P, 2, T], F32), m3_e=([P, 2, 384], F32), m3_pt=([P, 2, 384], F32), m3_kr=([P, T], F32),
            m3_nm=([P, MLA_H, 8], F32), m3_pos=([P, T], I32), m3_ang=([P, T], F32))
        SCALE = float(DQ) ** -0.5
        UQ0, UKV0, OUT0 = MIX3_IN, MIX3_IN + MIX3_UQ, MIX3_IN + MIX3_UQ + MIX3_UKV

        def pe_mix3(pe, n, _):
            F0 = first_block[n]
            pe_norm(pe, n)

            def krope():
                for k in range(KD):
                    mm = pe.matmul(MODP[0:DQ, 0:T], prm("w_krope")[:, k * DQ:k * DQ + DQ], xm[:, k, :],
                                   start=(k == 0), stop=(k == KD - 1))
                mm.then_inc(sem("m3_krope"), 1)

            def swap_k():
                pe.wait_ge(sem("m3_ks"), 1)
                pe.matmul(MODP[0:DQ, 0:T], cst("rope_perm")[0:DQ, :], qs[0:DQ, 1, 0, :], start=True, stop=True)\
                  .then_inc(sem("m3_kswap"), 1)

            def low_norms():
                for g, (k0, k1) in enumerate(((0, 6), (6, 8))):
                    for k in range(k0, k1):
                        if k % 2 == 0:
                            pe.wait_ge(sem("m3_squared"), k // 2 + 1)
                        mm = pe.matmul(ACC[2 + g][:, 0:T], ones, kt[:, k, :], start=(k == k0), stop=(k == k1 - 1))
                    mm.then_inc(sem("m3_var"), 1)

            def uq(j):
                b = F0 + UQ0 + j
                s = slot_of(b)
                out = pair((GATE, UP)[j % 2])
                pe.wait_ge(sem("w_lo_ready"), b + 1)
                if j == 0:
                    pe.wait_ge(sem("m3_split"), 4)
                if j >= 2:
                    pe.wait_ge(sem("m3_qs"), j - 1)
                for hd in range(2):
                    for k in range(6):
                        for i, (wp, ap) in enumerate(PASSES):
                            c = k * 2 * DQ + hd * DQ
                            mm = pe.matmul(out[0:DQ, hd, :], (whi, wlo)[wp][:, s, c:c + DQ], (xh, xl)[ap][:, k, :],
                                           start=(k == 0 and i == 0), stop=(k == 5 and i == 2))
                mm.then_inc(sem("w_used"), 1)

            def swap_q(j):
                pe.wait_ge(sem("m3_qs"), j + 1)
                if j >= 2:
                    pe.wait_ge(sem("m3_q"), j - 1)
                pe.matmul(ACC[j % 2][0:DQ, :], cst("rope_perm")[0:DQ, :], qs[0:DQ, j % 2].rearrange("p a t -> p (a t)"),
                          start=True, stop=True).then_inc(sem("m3_qswap"), 1)

            def uk():
                b = F0 + UKV0
                s = slot_of(b)
                pe.wait_ge(sem("w_lo_ready"), b + 1)
                pe.wait_ge(sem("m3_q"), MIX3_UQ)
                for m in range(8):
                    for k in range(2):
                        for i, (wp, ap) in enumerate(PASSES):
                            c = k * D + m * P
                            mm = pe.matmul(pair(ACC[m // 2])[:, m % 2, :], (whi, wlo)[wp][:, s, c:c + P],
                                           (xh, xl)[ap][:, 6 + k, :], start=(k == 0 and i == 0), stop=(k == 1 and i == 2))
                mm.then_inc(sem("w_used"), 1)

            def uv():
                b = F0 + UKV0 + 1
                s = slot_of(b)
                pe.wait_ge(sem("w_lo_ready"), b + 1)
                for q in range(4):
                    tt, half = q // 2, q % 2
                    pe.wait_ge(sem("m3_k"), 2 * q + 2)
                    for k in range(2):
                        for i, (wp, ap) in enumerate(PASSES):
                            c = k * D + half * 512
                            mm = pe.matmul(ACC[q][:, :], (xh, xl)[ap][:, 6 + k, tt * P:tt * P + P],
                                           (whi, wlo)[wp][:, s, c:c + 512], start=(k == 0 and i == 0),
                                           stop=(k == 1 and i == 2))
                    if q < 3:
                        mm.then_inc(sem("m3_v_bank"), 1)
                mm.then_inc(sem("w_used"), 1)

            def scores(h):
                b = ACC[h % 2]
                if h == 0:
                    pe.wait_ge(sem("m3_v"), 4)
                    pe.wait_ge(sem("m3_k_rope"), 1)
                if h >= 2:
                    pe.wait_ge(sem("m3_e"), 2 * (h - 1))
                q = qt[0:DQ, h, :]
                pe.matmul(b[:, 0:P], q[:, 0:P], kt[0:DQ, h, 0:P], start=True, stop=True, skip_group_check=True)
                pe.matmul(b[:, P:384], q[:, P:T], kt[0:DQ, h, :], start=False, stop=True, skip_group_check=True)
                pe_mask(pe, b[:, 0:P], "mask")
                pe_mask(pe, b[:, 256:384], "mask").then_inc(sem("m3_scores"), 1)

            def turn(h):
                b = ACC[2 + h % 2]
                if h >= 2:
                    pe.wait_ge(sem("m3_pt"), h - 1)
                pe.wait_ge(sem("m3_p"), 2 * h + 2)
                for c in range(3):
                    mm = pe.transpose(b[:, c * P:c * P + P], e3[:, h % 2, c * P:c * P + P], ident)
                mm.then_inc(sem("m3_turned"), 1)

            def sums(h):
                k, r0 = h // 2, 64 * (h % 2)
                out = (GATE, UP)[k % 2]
                if k >= 2 and h % 2 == 0:
                    pe.wait_ge(sem("m3_o"), k - 1)
                pe.wait_ge(sem("m3_pt"), h + 1)
                p = pt3[:, h % 2, :]
                pe.matmul(out[r0:r0 + 64, 0:T], v3[:, 0, h * 64:h * 64 + 64], p[:, 0:T], start=True, stop=False,
                          skip_group_check=True)
                pe.matmul(out[r0:r0 + 64, P:T], v3[:, 1, h * 64:h * 64 + 64], p[:, 256:384], start=False, stop=True,
                          skip_group_check=True).then_inc(sem("m3_sums"), 1)

            for j in range(MIX3_IN):
                if j >= 2:
                    pe.wait_ge(sem("m3_evac"), j - 1)
                pe_in(pe, F0 + j, pair((GATE, UP)[j % 2]), **({"first_pass_waits": 4 * split_index[n]} if j == 0 else {}))
                if j == 0:
                    krope()
            swap_k()
            low_norms()
            for j in range(MIX3_UQ):
                uq(j)
                if j >= 1:
                    swap_q(j - 1)
            swap_q(MIX3_UQ - 1)
            uk()
            uv()
            for h in range(MLA_H + 2):
                if h < MLA_H:
                    scores(h)
                if 1 <= h <= MLA_H:
                    turn(h - 1)
                if h >= 2:
                    sums(h - 2)
            for b in range(MIX3_OUT):
                pe.wait_ge(sem("m3_o"), 8)
                pe_out(pe, F0 + OUT0 + b, xh[:, 2 * b:2 * b + 2, :], xl[:, 2 * b:2 * b + 2, :], b == 0,
                       b == MIX3_OUT - 1, acc=MIX_ACC)

        def act_mix3(act, n, _):
            F0 = first_block[n]
            act.dma_start(pos_i[:, :], a_pos).then_inc(sem("pos_loaded"), 16)
            act_norm(act, n)
            act_split(act, F0 + 2)
            for j in range(MIX3_IN):
                if j >= 1:
                    act_split(act, F0 + j + 2)
                act.wait_ge(sem("w_used"), F0 + j + 1)
                if j == 0:
                    act.wait_ge(sem("m3_krope"), 1)
                act.activation(xm[:, 2 * j:2 * j + 2, :], pair((GATE, UP)[j % 2]), ACT.Copy).then_inc(sem("m3_evac"), 1)
                act.wait_ge(sem("m3_evac"), j + 1)
                act.activation(kt[:, 2 * j:2 * j + 2, :], xm[:, 2 * j:2 * j + 2, :], ACT.Square).then_inc(sem("m3_squared"), 1)
                if j == 0:
                    act.activation(qs[0:DQ, 1, 0, :], MODP[0:DQ, 0:T], ACT.Copy).then_inc(sem("m3_ks"), 1)
            for i, dst in enumerate((sin96, cos96)):
                act.wait_ge(sem("m3_angle"), i + 1)
                act.activation(dst[:, :], ang[:, :] if i == 0 else kr[:, :], ACT.Sin).then_inc(sem("m3_tables"), 1)
            for g in range(2):
                act.wait_ge(sem("m3_var"), g + 1)
                act.activation(e3[:, g, 0:T], ACC[2 + g][:, 0:T], ACT.Sqrt, scale=1.0 / (768, 256)[g], bias=cols[:, 64:65])\
                   .then_inc(sem("m3_std"), 1)
            for b in range(4):
                act.wait_ge(sem("m3_normed"), b + 1)
                act.activation(xh[:, 2 * b:2 * b + 2, :], xm[:, 2 * b:2 * b + 2, :], ACT.Copy).then_inc(sem("m3_rounded"), 1)
            for j in range(MIX3_UQ):
                act_split(act, F0 + UQ0 + j + 2)
                act.wait_ge(sem("w_used"), F0 + UQ0 + j + 1)
                if j == 1:
                    act.wait_ge(sem("m3_kr"), 1)
                if j >= 2:
                    act.wait_ge(sem("m3_q_read"), j - 1)
                    act.wait_ge(sem("m3_qswap"), j - 1)
                act.activation(qs[0:DQ, j % 2], pair((GATE, UP)[j % 2])[0:DQ], ACT.Copy).then_inc(sem("m3_qs"), 1)
            act.wait_ge(sem("m3_kr"), 3)
            act.activation(kt[64:DQ, :, :], kr[64:DQ, :].unsqueeze(1).to_broadcast([32, MLA_H, T]), ACT.Copy)\
               .then_inc(sem("m3_k_rope"), 1)
            act.wait_ge(sem("w_used"), F0 + UKV0 + 1)
            for q in range(4):
                for r in range(2):
                    act.activation(kt[0:64, 4 * q + r:4 * q + r + 3:2, :], pair(ACC[q])[64 * r:64 * r + 64], ACT.Copy)\
                       .then_inc(sem("m3_k"), 1)
            act_split(act, F0 + OUT0)
            act_split(act, F0 + OUT0 + 1)
            for q in range(4):
                if q < 3:
                    act.wait_ge(sem("m3_v_bank"), q + 1)
                else:
                    act.wait_ge(sem("w_used"), F0 + UKV0 + 2)
                act.activation(v3[:, q // 2, 512 * (q % 2):512 * (q % 2) + 512], ACC[q][:, :], ACT.Copy)\
                   .then_inc(sem("m3_v"), 1)

            def exps(h):
                act.wait_ge(sem("m3_max"), h + 1)
                if h >= 2:
                    act.wait_ge(sem("m3_turned"), h - 1)
                for lt, (c0, c1) in enumerate(((0, P), (P, 384))):
                    act.activation(e3[:, h % 2, c0:c1], ACC[h % 2][:, c0:c1], ACT.Exp, bias=nm[:, h, 2 + lt:3 + lt],
                                   scale=SCALE, accum_out=nm[:, h, 4 + lt:5 + lt]).then_inc(sem("m3_e"), 1)

            def turned(h):
                act.wait_ge(sem("m3_turned"), h + 1)
                if h >= 2:
                    act.wait_ge(sem("m3_sums"), h - 1)
                act.activation(pt3[:, h % 2, :], ACC[2 + h % 2][:, 0:384], ACT.Copy).then_inc(sem("m3_pt"), 1)

            def out_pair(k):
                act.wait_ge(sem("m3_sums"), 2 * k + 2)
                act.activation(xh[:, k, :], (GATE, UP)[k % 2][:, 0:T], ACT.Copy).then_inc(sem("m3_o_hi"), 1)

            for h in range(MLA_H + 2):
                if h < MLA_H:
                    exps(h)
                if 1 <= h <= MLA_H:
                    turned(h - 1)
                if h >= 3 and h % 2 == 1:
                    out_pair((h - 3) // 2)
            for b in range(MIX3_OUT):
                act_split(act, F0 + OUT0 + 2 + b)

        def dve_mix3(dve, n, _):
            F0 = first_block[n]
            dve_phase_norm(dve, n)
            TWO_PI = 2 * np.pi
            C1 = 6.28125
            C2 = float(TWO_PI - C1)
            ROUND = 1.5 * 2.0 ** 23
            LIMIT = 3.1415925
            dve.wait_ge(sem("pos_loaded"), 16)
            dve.tensor_copy(t1[:, 0, :], pos_i[:, :]).then_inc(sem("m3_pos"), 1)
            dve.wait_ge(sem("m3_pos"), 1)
            dve.tensor_scalar(t1[:, 0, :], t1[:, 0, :], cst("inv_freq"), None, ALU.mult).then_inc(sem("m3_pos"), 1)
            dve.wait_ge(sem("m3_pos"), 2)
            for i, (dst, quarter) in enumerate(((ang, 0.0), (kr, 0.25))):
                turns = t1[:, 1, :]
                a = sem("m3_angle_step")
                dve.tensor_scalar(turns, t1[:, 0, :], 1.0 / TWO_PI, quarter, ALU.mult, ALU.add).then_inc(a, 1)
                dve.wait_ge(a, 5 * i + 1)
                dve.tensor_scalar(turns, turns, ROUND, ROUND, ALU.add, ALU.subtract).then_inc(a, 1)
                dve.wait_ge(a, 5 * i + 2)
                dve.scalar_tensor_tensor(out=dst[:, :], in0=turns, scalar=-C1, in1=t1[:, 0, :], op0=ALU.mult, op1=ALU.add)\
                   .then_inc(a, 1)
                dve.wait_ge(a, 5 * i + 3)
                dve.scalar_tensor_tensor(out=dst[:, :], in0=turns, scalar=-C2, in1=dst[:, :], op0=ALU.mult, op1=ALU.add)\
                   .then_inc(a, 1)
                dve.wait_ge(a, 5 * i + 4)
                dve.tensor_scalar(dst[:, :], dst[:, :], quarter * TWO_PI, LIMIT, ALU.add, ALU.min).then_inc(a, 1)
                dve.wait_ge(a, 5 * i + 5)
                dve.tensor_scalar(dst[:, :], dst[:, :], -LIMIT, None, ALU.max).then_inc(sem("m3_angle"), 1)
            dve_split(dve, F0 + 2)
            for j in range(1, MIX3_IN):
                dve_split(dve, F0 + j + 2)
            for g, (k0, k1) in enumerate(((0, 6), (6, 8))):
                gain = prm(("q_g", "kv_g")[g])
                inv = e3[:, g, 0:T]
                dve.wait_ge(sem("m3_std"), g + 1)
                dve.reciprocal(inv, inv).then_inc(sem("m3_inv"), 1)
                dve.wait_ge(sem("m3_inv"), g + 1)
                for k in range(k0, k1):
                    ins = dve.scalar_tensor_tensor(out=xm[:, k, :], in0=xm[:, k, :], scalar=gain[:, k - k0:k - k0 + 1],
                                                   in1=inv, op0=ALU.mult, op1=ALU.mult)
                    if k % 2 == 1:
                        ins.then_inc(sem("m3_normed"), 1)
            for b in range(4):
                dve.wait_ge(sem("m3_rounded"), b + 1)
                dve.tensor_tensor(xl[:, 2 * b:2 * b + 2, :], xm[:, 2 * b:2 * b + 2, :],
                                  xh[:, 2 * b:2 * b + 2, :].bitcast(F32), ALU.subtract).then_inc(sem("m3_split"), 1)
            dve.wait_ge(sem("m3_tables"), 2)
            dve.wait_ge(sem("m3_kswap"), 1)
            dve.tensor_tensor(t1[0:DQ, 0, :], qs[0:DQ, 1, 0, :], cos96[0:DQ, :], ALU.mult).then_inc(sem("m3_kr"), 1)
            dve.tensor_tensor(kr[0:DQ, :], MODP[0:DQ, 0:T], sin96[0:DQ, :], ALU.mult).then_inc(sem("m3_kr"), 1)
            dve.wait_ge(sem("m3_kr"), 2)
            dve.tensor_tensor(kr[0:DQ, :], kr[0:DQ, :], t1[0:DQ, 0, :], ALU.add).then_inc(sem("m3_kr"), 1)
            dve.wait_ge(sem("m3_kr"), 3)

            def rope_q(j):
                q = qt[0:DQ, 2 * j:2 * j + 2, :]
                dve.wait_ge(sem("m3_qs"), j + 1)
                if j >= 1:
                    dve.wait_ge(sem("m3_q"), j)
                dve.tensor_tensor(t1[0:DQ], qs[0:DQ, j % 2], over(cos96[0:DQ, :], [DQ, 2, T]), ALU.mult)\
                   .then_inc(sem("m3_q_read"), 1)
                dve.wait_ge(sem("m3_qswap"), j + 1)
                dve.tensor_tensor(q, pair(ACC[j % 2])[0:DQ], over(sin96[0:DQ, :], [DQ, 2, T]), ALU.mult)\
                   .then_inc(sem("m3_q_part"), 1)
                dve.wait_ge(sem("m3_q_part"), j + 1)
                dve.wait_ge(sem("m3_q_read"), j + 1)
                dve.tensor_tensor(q, q, t1[0:DQ], ALU.add).then_inc(sem("m3_q"), 1)

            for j in range(MIX3_UQ):
                dve_split(dve, F0 + UQ0 + j + 2)
                if j >= 1:
                    rope_q(j - 1)
            rope_q(MIX3_UQ - 1)
            dve_split(dve, F0 + OUT0)
            dve_split(dve, F0 + OUT0 + 1)

            def maxima(h):
                dve.wait_ge(sem("m3_scores"), h + 1)
                for lt, (c0, c1) in enumerate(((0, P), (P, 384))):
                    dve.tensor_reduce(nm[:, h, lt:lt + 1], ACC[h % 2][:, c0:c1], AX.X, ALU.max).then_inc(sem("m3_max_part"), 1)
                dve.wait_ge(sem("m3_max_part"), 2 * h + 2)
                dve.tensor_scalar(nm[:, h, 2:4], nm[:, h, 0:2], -SCALE, None, ALU.mult).then_inc(sem("m3_max"), 1)

            def weights(h):
                dve.wait_ge(sem("m3_e"), 2 * h + 2)
                dve.reciprocal(nm[:, h, 6:8], nm[:, h, 4:6]).then_inc(sem("m3_rsum"), 1)
                dve.wait_ge(sem("m3_rsum"), h + 1)
                for lt, (c0, c1) in enumerate(((0, P), (P, 384))):
                    dve.tensor_scalar(e3[:, h % 2, c0:c1], e3[:, h % 2, c0:c1], nm[:, h, 6 + lt:7 + lt], None, ALU.mult)\
                       .then_inc(sem("m3_p"), 1)

            def out_pair(k):
                dve.wait_ge(sem("m3_o_hi"), k + 1)
                dve.tensor_tensor(xl[:, k, :], (GATE, UP)[k % 2][:, 0:T], xh[:, k, :].bitcast(F32), ALU.subtract)\
                   .then_inc(sem("m3_o"), 1)

            for h in range(MLA_H + 2):
                if h < MLA_H:
                    maxima(h)
                    weights(h)
                if h >= 3 and h % 2 == 1:
                    out_pair((h - 3) // 2)
            for b in range(MIX3_OUT):
                dve_split(dve, F0 + OUT0 + 2 + b)
            dve_phase_residual(dve, n)


        PE = {"ffn": lambda pe, n, f: pe_ffn(pe, n, f, MOD_GROUPS[f]), "final": lambda pe, n, f: pe_norm(pe, n),
              "mix1": pe_mix1, "mix2": pe_mix2, "mix3": pe_mix3}
        ACTS = {"ffn": lambda e, n, f: act_ffn(e, n, f, MOD_GROUPS[f]),
                "final": lambda e, n, f: act_norm(e, n, split=False),
                "mix1": act_mix1, "mix2": act_mix2, "mix3": act_mix3}
        DVE = {"ffn": lambda e, n, f: dve_ffn(e, n, f, MOD_GROUPS[f]), "final": lambda e, n, f: dve_phase_norm(e, n),
               "mix1": dve_mix1, "mix2": dve_mix2, "mix3": dve_mix3}

        block = ctx.enter_context(nc.Block())

        @block.sync
        def _(sp):
            sp.dma_start(x[:, :, :], a_x).then_inc(sem("x_loaded"), 16)
            sp.dma_start(params[:, :], a_params).then_inc(sem("params_loaded"), 16)
            sp.dma_start(consts[:, :], a_consts).then_inc(sem("params_loaded"), 16)
            for n in range(min(SLOTS, N_BLOCKS)):
                sp.dma_start(raw[:, n, :], a_stream[n * P:n * P + P, :]).then_inc(sem(f"w_loaded{n}"), 16)
            full = N_BLOCKS // SLOTS

            def load(s, turn):
                sp.wait_ge(sem("w_lo_ready"), s - SLOTS + 1 + SLOTS * turn)
                sp.dma_start(raw[:, s, :], a_stream[ds(s * P + SLOTS * P * turn, P), :])\
                  .then_inc(sem(f"w_loaded{s}"), 16)

            if full > 1:
                with sp.Fori(1, full) as turn:
                    for s in range(SLOTS):
                        load(s, turn)
            for s in range(N_BLOCKS % SLOTS):
                load(s, full)
            sp.wait_ge(sem("x_updated"), 4 * (len(phases)))
            sp.dma_start(a_out, x[:, :, :]).then_inc(sem("stored"), 16)
            sp.wait_ge(sem("stored"), 16)

        @block.gpsimd
        def _(pool):
            def load(s, turn):
                pool.dma_start(mod_raw[:, s, :], a_mod[ds(s * P + 2 * P * turn, P), :])\
                    .then_inc(sem(f"mod_loaded{s}"), 16)

            if N_GROUPS:
                for s in range(2):
                    load(s, 0)
                with pool.Fori(1, 2 * N_GROUPS) as turn:
                    for s in range(2):
                        pool.wait_ge(sem("mod_step"), 2 * s + 2 - 4 + 4 * turn)
                        load(s, turn)

        @block.tensor
        def _(pe):
            pe.wait_ge(sem("params_loaded"), 32)
            for n, (kind, f, _) in enumerate(phases):
                PE[kind](pe, n, f)

        @block.scalar
        def _(act):
            act.wait_ge(sem("params_loaded"), 32)
            act.activation(c_act[:, :], prm("c"), ACT.Silu).then_inc(sem("c_ready"), 1)
            act.wait_ge(sem("eps_ready"), 2)
            act_split(act, 0)
            act_split(act, 1)
            for n, (kind, f, _) in enumerate(phases):
                ACTS[kind](act, n, f)

        @block.vector
        def _(dve):
            dve.memset(cols[:, 64:65], RMS_EPS).then_inc(sem("eps_ready"), 1)
            dve.memset(cols[:, 65:66], LN_EPS).then_inc(sem("eps_ready"), 1)
            dve.wait_ge(sem("params_loaded"), 32)
            dve.wait_ge(sem("c_ready"), 1)
            dve_split(dve, 0)
            dve_split(dve, 1)
            for n, (kind, f, _) in enumerate(phases):
                DVE[kind](dve, n, f)


def _in_blocks(w, width=256):
    k, n = w.shape
    b = w.reshape(k // P, P, n // width, width).transpose(2, 1, 0, 3).reshape(n // width, P, -1)
    return np.pad(b, ((0, 0), (0, 0), (0, BLK - b.shape[2])))


def _out_blocks(w):
    k, n = w.shape
    return w.reshape(k // (2 * P), 2, P, n).transpose(0, 2, 1, 3).reshape(k // (2 * P), P, 2 * n)


def _ffn_blocks(w_in, w_out):
    g, u, d = _in_blocks(w_in[:, :DFF]), _in_blocks(w_in[:, DFF:]), _out_blocks(w_out)
    order = [g[0], u[0]]
    for s in range(1, STEPS):
        order += [g[s], u[s], d[s - 1]]
    return np.stack(order + [d[STEPS - 1]])


def _cols(v):
    v = np.asarray(v)
    return np.moveaxis(v.reshape(-1, v.shape[-1] // P, P), 2, 0).reshape(P, -1)


def _top(a):
    a = np.asarray(a)
    return np.pad(a, ((0, P - a.shape[0]), (0, 0)))


def _stream(v):
    mix = v["w_mix_in"][0]
    M = HEADS_M * DH_M
    z0 = 4 * M + 2 * HEADS_M
    g0 = z0 + 2 * D
    q, k, vv, o = (mix[:, i * M:(i + 1) * M] for i in range(4))
    zu, zv, gm, gs = mix[:, z0:z0 + D], mix[:, z0 + D:g0], mix[:, g0:g0 + D], mix[:, g0 + D:g0 + 2 * D]
    parts = [_ffn_blocks(v["ffn1_w_in"][0], v["ffn1_w_out"][0])]
    parts += [_in_blocks(w) for w in (q, k, vv, zv, o, gm, gs, zu)] + [_out_blocks(v["w_mix_out"][0])]
    parts += [_ffn_blocks(v["ffn2_w_in"][0], v["ffn2_w_out"][0])]
    w13, w2 = v["ffn_w13_2"], v["ffn_w2_2"]
    parts += [_ffn_blocks(w13[0, 0], w2[0, 0])]
    ab = v["ab_w_in_2"][0]
    ab = np.concatenate([ab[:, 1536:3072], ab[:, :1536]], axis=1)
    parts += [_in_blocks(ab), _out_blocks(v["ab_w_out_2"][0])]
    parts += [_ffn_blocks(w13[0, 1], w2[0, 1]), _ffn_blocks(w13[1, 0], w2[1, 0])]
    ukv = v["mla_w_ukv_2"][0].reshape(256, MLA_H, 2, 64)
    parts += [_in_blocks(v["mla_w_in_2"][0][:, :1024]), _in_blocks(v["mla_w_uq_2"][0], 2 * DQ),
              _in_blocks(ukv[:, :, 0].reshape(256, 1024), 1024), _in_blocks(ukv[:, :, 1].reshape(256, 1024), 1024),
              _out_blocks(v["mla_w_o_2"][0])]
    parts += [_ffn_blocks(w13[1, 1], w2[1, 1])]
    return np.concatenate(parts).reshape(-1, BLK)


def _params(v):
    mix = v["w_mix_in"][0]
    i0 = 4 * D
    w_if = np.zeros((D, 64), np.float32)
    w_if[:, 0:4] = mix[:, i0:i0 + 4]
    w_if[:, 32:36] = mix[:, i0 + 4:i0 + 8]
    w_kr = np.zeros((D, DQ), np.float32)
    w_kr[:, NOPE:] = v["mla_w_in_2"][0][:, 1024:]

    def ktiles(w):
        return w.reshape(KD, P, -1).transpose(1, 0, 2).reshape(P, -1)

    def conv(w):
        return w.reshape(4, -1, P).transpose(2, 1, 0).reshape(P, -1)

    col = lambda a: np.asarray(a).reshape(-1, 1)
    b_f = np.zeros((P, 1), np.float32)
    b_f[32:36] = col(v["mlstm_b_fgate"][0])
    at = {"g_ffn1": _cols(v["ffn1_norm_g"]), "g_mix": _cols(v["mix_norm_g"]), "g_ffn2": _cols(v["ffn2_norm_g"]),
          "g_final": _cols(v["final_norm_g"]), "conv_w1": conv(v["mlstm_conv_w"][0]),
          "conv_b1": _cols(v["mlstm_conv_b"]), "b_i": _top(col(v["mlstm_b_igate"][0])), "b_f": b_f,
          "head_g": _cols(v["mlstm_head_norm_g"]), "sgu_bs": _top(v["sgu_b_s"][0]), "mod_b": _cols(v["mod_b_2"]),
          "norm_g2": _cols(v["norm_g_2"].reshape(6, D)), "pool_scale": _cols(v["pool_scale_2"]),
          "conv_w2": conv(v["ssd_conv_w_2"][0]), "conv_b2": _cols(v["ssd_conv_b_2"]),
          "dt_bias": _top(col(v["ssd_dt_bias_2"][0])), "a_log": _top(col(v["ssd_a_log_2"][0])),
          "ssd_d": _cols(np.repeat(v["ssd_d_2"], SSD_P, axis=1)), "ssd_g": _cols(v["ssd_norm_g_2"]),
          "q_g": _cols(v["mla_q_norm_g_2"]), "kv_g": _cols(v["mla_kv_norm_g_2"]), "g_final2": _cols(v["final_norm_g_2"]),
          "c": _cols(v["c_2"]), "w_if": ktiles(w_if), "w_dt": ktiles(v["ab_w_in_2"][0][:, 3072:]),
          "w_krope": ktiles(w_kr), "pool_w": v["pool_w_2"][0].transpose(1, 0, 2).reshape(P, -1),
          "sgu_wT": v["sgu_w_s"][0].transpose(2, 0, 1).reshape(P, -1)}
    return np.concatenate([at[name].reshape(P, width) for name, width in PARAMS], axis=1)


def _consts():
    r = np.arange(P)
    later = np.where(r[:, None] <= r[None, :], 0.0, NEG)
    perm = np.zeros((P, DQ))
    half = ROPE // 2
    for m in range(half):
        perm[NOPE + half + m, NOPE + m] = -1.0
        perm[NOPE + m, NOPE + half + m] = 1.0
    freq = np.zeros((P, 1))
    f = np.float32(10000.0) ** (-np.arange(0, ROPE, 2, dtype=np.float32) / np.float32(ROPE))
    freq[NOPE:NOPE + half, 0] = f
    freq[NOPE + half:NOPE + ROPE, 0] = f
    fix = np.stack([w / np.minimum(np.arange(16) + 1, w) for w in (2, 4, 8, 16)])
    at = {"ident": np.eye(P), "maskT": later, "mask": later.T, "ones": np.ones((P, P)), "rope_perm": perm,
          "inv_freq": freq, "pool_fix": np.broadcast_to(fix.reshape(1, -1), (P, 64))}
    return np.concatenate([at[name].reshape(P, width) for name, width in CONSTS], axis=1).astype(np.float32)


def kernel(**inputs):
    import concourse.bacc as bacc
    from concourse.bass_utils import run_bass_kernel_spmd as run

    v = {k: np.asarray(a) for k, a in inputs.items()}
    arrays = {
        "x_in": np.ascontiguousarray(v["x"][0].reshape(T, KD, P).transpose(2, 1, 0)),
        "pos_in": np.ascontiguousarray(np.broadcast_to(v["positions_2"].astype(np.int32), (P, T))),
        "stream_in": _stream(v),
        "mod_in": np.ascontiguousarray(v["mod_w_2"].reshape(2, 4, 2, P, 9, D).transpose(0, 4, 1, 3, 2, 5)).reshape(-1, BLK),
        "params_in": _params(v),
        "consts_in": _consts(),
        "sgu_in": np.ascontiguousarray(np.broadcast_to(
            np.concatenate([v["sgu_norm_g"][0], v["sgu_norm_b"][0]])[None], (P, 2 * D))),
    }
    nc = bacc.Bacc("TRN2", target_bir_lowering=False, num_devices=1)
    aps = [nc.dram_tensor(name, a.shape, mybir.dt.from_np(a.dtype), kind="ExternalInput").ap()
           for name, a in arrays.items()]
    out = nc.dram_tensor("y_out", (P, KD, T), mybir.dt.float32, kind="ExternalOutput").ap()
    build_program(nc, *aps, out)
    y = run(nc, [arrays], core_ids=[0]).results[0]["y_out"]
    return np.ascontiguousarray(y.transpose(2, 1, 0)).reshape(1, T, D)
```

```python
import numpy as np
import concourse.bass as bass
from concourse import mybir
from contextlib import ExitStack

P = 128
T = 256
D = 1024
KD = D // P
DFF = 2816
STEPS = DFF // 256
BLK = 2048
SLOTS = 3
HEADS_M, DH_M = 4, 256
SGU_G = 4
SSD_H, SSD_P = 16, 64
MLA_H, NOPE, ROPE = 16, 64, 32
DQ = NOPE + ROPE
NEG = -1.0e30
RMS_EPS, LN_EPS = 1e-6, 1e-5

FFN_BLOCKS = 3 * STEPS
MIX1_IN, MIX1_OUT = 32, 4
MIX2_IN, MIX2_OUT = 12, 6
MIX3_IN, MIX3_UQ, MIX3_UKV, MIX3_OUT = 4, 8, 2, 4
PHASES = [("ffn", 0, FFN_BLOCKS), ("mix1", 0, MIX1_IN + MIX1_OUT), ("ffn", 1, FFN_BLOCKS), ("final", 0, 0),
          ("ffn", 2, FFN_BLOCKS), ("mix2", 0, MIX2_IN + MIX2_OUT), ("ffn", 3, FFN_BLOCKS),
          ("ffn", 4, FFN_BLOCKS), ("mix3", 0, MIX3_IN + MIX3_UQ + MIX3_UKV + MIX3_OUT), ("ffn", 5, FFN_BLOCKS),
          ("final", 1, 0)]
TABLES_AT = 2
MOD_GROUPS = {0: 5, 1: 5, 2: 5, 3: 3, 4: 0, 5: 0}

PARAMS = [("g_ffn1", 8), ("g_mix", 8), ("g_ffn2", 8), ("g_final", 8), ("conv_w1", 64), ("conv_b1", 16),
          ("b_i", 1), ("b_f", 1), ("head_g", 8), ("sgu_bs", 128), ("mod_b", 144), ("norm_g2", 48),
          ("pool_scale", 4), ("conv_w2", 48), ("conv_b2", 12), ("dt_bias", 1), ("a_log", 1), ("ssd_d", 8),
          ("ssd_g", 8), ("q_g", 6), ("kv_g", 2), ("g_final2", 8), ("c", 8), ("w_if", 512), ("w_dt", 128),
          ("w_krope", 768), ("pool_w", 512), ("sgu_wT", 512)]
CONSTS = [("ident", 128), ("maskT", 128), ("ones", 128), ("rope_perm", 96), ("inv_freq", 1),
          ("pool_fix", 64)]


def offsets(table):
    at, o = {}, 0
    for name, width in table:
        at[name] = (o, o + width)
        o += width
    return at, o


def build_program(nc, a_x, a_pos, a_stream, a_mod, a_params, a_consts, a_sgu, a_out, phases=PHASES):
    F32, F32R, I32 = mybir.dt.float32, mybir.dt.float32r, mybir.dt.int32
    ALU, ACT, AX = mybir.AluOpType, mybir.ActivationFunctionType, mybir.AxisListType
    ds = bass.ds
    P_AT, P_N = offsets(PARAMS)
    C_AT, C_N = offsets(CONSTS)
    first_block, b0 = [], 0
    for _, _, nb in phases:
        first_block.append(b0)
        b0 += nb
    N_BLOCKS = b0
    N_GROUPS = sum(MOD_GROUPS[i] for kind, i, _ in phases if kind == "ffn")

    with ExitStack() as ctx:
        def sb(name, shape, dt=F32):
            return ctx.enter_context(nc.sbuf_tensor(name, shape, dt))

        sems = {}

        def sem(name):
            if name not in sems:
                sems[name] = ctx.enter_context(nc.semaphore(name))
            return sems[name]

        raw = sb("raw", [P, SLOTS, BLK])
        whi = sb("whi", [P, SLOTS, BLK], F32R)
        wlo = sb("wlo", [P, SLOTS, BLK], F32R)
        mod_raw = sb("mod_raw", [P, 2, BLK])
        mod_acc = sb("mod_acc", [P, D])
        mod_tab = sb("mod_tab", [P, 144])
        ident_b = sb("ident_b", [P, P], mybir.dt.bfloat16)
        mask_b = sb("mask_b", [P, P], mybir.dt.bfloat16)
        c_act = sb("c_act", [P, KD])
        x = sb("x", [P, KD, T])
        xm = sb("xm", [P, KD, T])
        xh = sb("xh", [P, KD, T], F32R)
        xl = sb("xl", [P, KD, T], F32R)
        std = sb("std", [P, T])
        rstd = sb("rstd", [P, T])
        gmod = sb("gmod", [P, KD])
        gres = sb("gres", [P, KD])
        params = sb("params", [P, P_N])
        consts = sb("consts", [P, C_N])
        cos96 = sb("cos96", [P, T])
        sin96 = sb("sin96", [P, T])
        rows = sb("rows", [16, 5, T])
        rstats = sb("rstats", [P, 2, 12])
        cols = sb("cols", [P, 66])

        def region(**tensors):
            with ExitStack() as here:
                return [here.enter_context(nc.sbuf_tensor(name, shape, dt)) for name, (shape, dt) in tensors.items()]

        gate, hid, hid_hi, hid_lo = region(gate=([P, 2, T], F32), hid=([P, 2, T], F32),
                                           hid_hi=([P, 2, 2, T], F32R), hid_lo=([P, 2, 2, T], F32R))

        bank = [ctx.enter_context(nc.psum_tensor(f"bank{i}", [P, 512], F32)) for i in range(8)]
        ACC = bank[0:4]
        GATE, UP, STAT, MODP = bank[4:8]

        def pair(b):
            return b[:, :].rearrange("p (m t) -> p m t", m=2)

        def prm(name):
            lo, hi = P_AT[name]
            return params[:, lo:hi]

        def cst(name):
            lo, hi = C_AT[name]
            return consts[:, lo:hi]

        ident, ones = cst("ident"), cst("ones")

        def slot_of(n0):
            return n0 % SLOTS

        def use_of(n0, i=0, per=0):
            return n0 // SLOTS + (per // SLOTS) * i

        def act_split(act, n0, i=0, per=0):
            if n0 >= N_BLOCKS:
                return
            s = slot_of(n0)
            act.wait_ge(sem(f"w_loaded{s}"), 16 * use_of(n0, i, per) + 16)
            if n0 >= SLOTS:
                act.wait_ge(sem("w_used"), n0 - SLOTS + 1 + per * i)
            act.activation(whi[:, s, :], raw[:, s, :], ACT.Copy).then_inc(sem("w_hi_ready"), 1)

        def dve_split(dve, n0, i=0, per=0):
            if n0 >= N_BLOCKS:
                return
            s = slot_of(n0)
            dve.wait_ge(sem("w_hi_ready"), n0 + 1 + per * i)
            dve.tensor_tensor(wlo[:, s, :], raw[:, s, :], whi[:, s, :].bitcast(F32), ALU.subtract)\
               .then_inc(sem("w_lo_ready"), 1)

        H = BLK // 2

        def norm_block(n):
            if n == 0:
                return 0
            if phases[n - 1][0] == "final" or first_block[n] + 1 >= N_BLOCKS:
                return None
            return first_block[n] + 1

        halves_index, n_halves = {}, 0
        for n in range(len(phases)):
            if norm_block(n) is not None:
                halves_index[n] = n_halves
                n_halves += 1

        def act_split_halves(act, n):
            if n >= len(phases) or norm_block(n) is None:
                return
            b = norm_block(n)
            s = slot_of(b)
            act.wait_ge(sem(f"w_loaded{s}"), 16 * use_of(b) + 16)
            if b >= SLOTS:
                act.wait_ge(sem("w_used"), b - SLOTS + 1)
            act.activation(whi[:, s, 0:H], raw[:, s, 0:H], ACT.Copy).then_inc(sem("w_half_ready"), 1)
            act.activation(whi[:, s, H:BLK], raw[:, s, H:BLK], ACT.Copy).then_inc(sem("w_hi_ready"), 1)

        def dve_split_half(dve, n, half):
            if norm_block(n) is None:
                return
            b = norm_block(n)
            s = slot_of(b)
            if half == 0:
                dve.wait_ge(sem("w_half_ready"), halves_index[n] + 1)
                dve.tensor_tensor(wlo[:, s, 0:H], raw[:, s, 0:H], whi[:, s, 0:H].bitcast(F32), ALU.subtract)\
                   .then_inc(sem("w_lo_half"), 1)
            else:
                dve.wait_ge(sem("w_hi_ready"), b + 1)
                dve.tensor_tensor(wlo[:, s, H:BLK], raw[:, s, H:BLK], whi[:, s, H:BLK].bitcast(F32), ALU.subtract)\
                   .then_inc(sem("w_lo_ready"), 1)

        PASSES = ((0, 0), (0, 1), (1, 0))

        def pe_in(pe, n0, out, i=0, per=0, first_pass_waits=None, beside=None):
            s = slot_of(n0)
            pe.wait_ge(sem("w_lo_ready"), n0 + 1 + per * i)
            if first_pass_waits is not None:
                for part in range(2):
                    for k in range(KD):
                        pe.wait_ge(sem(("xn_rounded", "xn_split")[part]), first_pass_waits + k + 1)
                        for m in range(2):
                            c = k * 256 + m * P
                            for w in ((whi, wlo) if part == 0 else (whi,)):
                                last = pe.matmul(out[:, m, :], w[:, s, c:c + P], (xh, xl)[part][:, k, :],
                                                 start=(part == 0 and k == 0 and m == 0 and w is whi),
                                                 stop=(part == 1 and k == KD - 1), skip_group_check=True)
                last.then_inc(sem("w_used"), 1)
                return
            for m in range(2):
                for k in range(KD):
                    for j, (wp, ap) in enumerate(PASSES):
                        last = pe.matmul(out[:, m, :], (whi, wlo)[wp][:, s, k * 256 + m * P:k * 256 + m * P + P],
                                         (xh, xl)[ap][:, k, :], start=(k == 0 and j == 0), stop=(k == KD - 1 and j == 2))
                    if beside is not None and k % 4 == 3 and (m, k) != (1, 7):
                        beside(2 * m + k // 4)
            last.then_inc(sem("w_used"), 1)
            if beside is not None:
                beside(3)

        def pe_tok(pe, n0, out):
            s = slot_of(n0)
            pe.wait_ge(sem("w_lo_ready"), n0 + 1)
            for tt in range(2):
                for k in range(KD):
                    for j, (wp, ap) in enumerate(PASSES):
                        last = pe.matmul(out[:, tt, :], (xh, xl)[ap][:, k, tt * P:tt * P + P],
                                         (whi, wlo)[wp][:, s, k * 256:k * 256 + 256],
                                         start=(k == 0 and j == 0), stop=(k == KD - 1 and j == 2))
            last.then_inc(sem("w_used"), 1)

        def pe_out(pe, n0, hi, lo, first, last_block, i=0, per=0, acc=ACC, banks_free=None, between=None, beside=None):
            s = slot_of(n0)
            pe.wait_ge(sem("w_lo_ready"), n0 + 1 + per * i)
            for d in range(KD):
                if d == 4 and between is not None:
                    between()
                if d == 4 and banks_free is not None:
                    pe.wait_ge(sem(banks_free[0]), banks_free[1])
                for kt in range(2):
                    for j, (wp, ap) in enumerate(PASSES):
                        c = kt * D + d * P
                        mm = pe.matmul(pair(acc[d // 2])[:, d % 2, :], (whi, wlo)[wp][:, s, c:c + P],
                                       (hi, lo)[ap][:, kt, :], start=(first and d % 2 == 0 and kt == 0 and j == 0),
                                       stop=(last_block and kt == 1 and j == 2), skip_group_check=True)
                if last_block and d % 2 == 1 and d < KD - 1:
                    mm.then_inc(sem("acc_ready"), 1)
                if beside is not None and d in (1, 3, 5):
                    beside(d // 2)
            mm.then_inc(sem("w_used"), 1)
            if beside is not None:
                beside(3)

        def dve_residual(dve, n, r, last, scale=None, gain=None, acc=ACC):
            for b in range(4):
                if b < 3:
                    dve.wait_ge(sem("acc_ready"), 3 * r + b + 1)
                else:
                    dve.wait_ge(sem("w_used"), last + 1)
                if gain is None:
                    dve.scalar_tensor_tensor(out=x[:, 2 * b:2 * b + 2, :], in0=pair(acc[b]), scalar=scale,
                                             in1=x[:, 2 * b:2 * b + 2, :], op0=ALU.mult, op1=ALU.add)\
                       .then_inc(sem("x_updated"), 1)
                else:
                    for m in range(2):
                        ins = dve.scalar_tensor_tensor(out=x[:, 2 * b + m, :], in0=pair(acc[b])[:, m, :],
                                                       scalar=gain[:, 2 * b + m:2 * b + m + 1],
                                                       in1=x[:, 2 * b + m, :], op0=ALU.mult, op1=ALU.add)
                    ins.then_inc(sem("x_updated"), 1)
                if b >= 1 and n + 1 < len(phases):
                    dve_pair(dve, n + 1, b - 1)
            if n + 1 < len(phases):
                dve_gain(dve, n + 1)
                dve_pair(dve, n + 1, 3)

        def dve_pair(dve, n, b):
            dve.wait_ge(sem("x_squared"), 4 * n + b + 1)
            dve.tensor_tensor(xm[:, 2 * b, :], xm[:, 2 * b, :], xm[:, 2 * b + 1, :], ALU.add).then_inc(sem("x_paired"), 1)

        def act_norm(act, n, split=True, shift=None):
            act.activation(std[:, 2:3], cols[:, 64:65], ACT.Sqrt).then_inc(sem("table_loaded"), 1)
            for b in range(4):
                if n == 0:
                    act.wait_ge(sem(f"x_loaded{b // 2}"), 16)
                else:
                    act.wait_ge(sem("x_updated"), 4 * (n - 1) + b + 1)
                act.activation(xm[:, 2 * b:2 * b + 2, :], x[:, 2 * b:2 * b + 2, :], ACT.Square, scale=D ** -0.5)\
                   .then_inc(sem("x_squared"), 1)
            if n == 0:
                act_split_halves(act, 0)
            act.wait_ge(sem("x_summed"), n + 1)
            act.activation(std[:, 0:2], STAT[:, T:T + 2], ACT.Sqrt, bias=cols[:, 64:65]).then_inc(sem("std_ready"), 1)
            if split:
                for k in range(KD):
                    act.wait_ge(sem("xn_ready"), 8 * split_index[n] + k + 1)
                    if shift is None:
                        ins = act.activation(xh[:, k, :], xm[:, k, :], ACT.Copy)
                    else:
                        ins = act.activation(xh[:, k, :], xm[:, k, :], ACT.Identity, bias=shift[:, k:k + 1])
                    ins.then_inc(sem("xn_rounded"), 1)

        WARM = (12, 6, 10, 24)

        def pe_keep_warm(pe, n, count):
            bank_ = GATE if phases[n - 1][0] in ("ffn", "final") else ACC[0]
            for _ in range(count if n > 0 else 0):
                pe.matmul(bank_[:, 0:P], ident_b[:, :], ident_b[:, :], start=True, stop=True, skip_group_check=True)

        def pe_norm(pe, n):
            if n > 0 and phases[n - 1][0] == "final":
                pe.wait_ge(sem("x_updated"), 4 * n)
            for b in range(4):
                if b == 0 and n > 0:
                    pe.wait_ge(sem("silu_done"), STEPS * sum(kind == "ffn" for kind, _, _ in phases[:n]))
                if b >= 2:
                    pe_keep_warm(pe, n, WARM[b - 2])
                pe.wait_ge(sem("x_paired"), 4 * n + b + 1)
                for tt in range(2):
                    mm = pe.matmul(STAT[:, T + tt:T + tt + 1], xm[:, 2 * b, tt * P:tt * P + P], ones[:, 0:1],
                                   start=(b == 0 and tt == 0), stop=(b == 3), skip_group_check=True)
            mm.then_inc(sem("x_summed"), 1)
            pe_keep_warm(pe, n, WARM[2])
            pe.wait_ge(sem("rstd_ready"), n + 1)
            for tt in range(2):
                mm = pe.matmul(STAT[:, tt * P:tt * P + P], rstd[:, tt:tt + 1].to_broadcast([P, P]), ident,
                               start=(tt == 0), stop=True, skip_group_check=True)
            mm.then_inc(sem("rstd_spread"), 1)
            if phases[n][0] != "final":
                pe_keep_warm(pe, n, WARM[3])

        def dve_norm(dve, n, g, shift=None, split=True, whole=False):
            if n == 0:
                for b in range(4):
                    dve_pair(dve, n, b)
            dve_split_half(dve, n, 0)
            dve.wait_ge(sem("std_ready"), n + 1)
            dve.reciprocal(rstd[:, 0:2], std[:, 0:2]).then_inc(sem("rstd_ready"), 1)
            dve_split_half(dve, n, 1)
            dve.wait_ge(sem("rstd_spread"), n + 1)
            dst = xm if split else x

            def add_shift(k):
                dve.wait_ge(sem("xn_scaled"), 8 * shift_index[n] + k + 1)
                dve.tensor_scalar(xm[:, k, :], xm[:, k, :], shift[:, k:k + 1], None, ALU.add).then_inc(sem("xn_ready"), 1)

            for k in range(KD):
                ins = dve.scalar_tensor_tensor(out=dst[:, k, :], in0=x[:, k, :], scalar=g[:, k:k + 1],
                                               in1=STAT[:, 0:T], op0=ALU.mult, op1=ALU.mult)
                if not split:
                    if k % 2 == 1:
                        ins.then_inc(sem("x_updated"), 1)
                        if k >= 3 and n + 1 < len(phases):
                            dve_pair(dve, n + 1, k // 2 - 1)
                elif whole:
                    ins.then_inc(sem("xn_scaled"), 1)
                    if k >= 1:
                        add_shift(k - 1)
                else:
                    ins.then_inc(sem("xn_ready"), 1)
            if not split and n + 1 < len(phases):
                dve_gain(dve, n + 1)
                dve_pair(dve, n + 1, 3)
            if whole:
                add_shift(KD - 1)
            if n in MOD_OF:
                layer, j = MOD_OF[n]
                dve.wait_ge(sem("x_updated"), 4 * n)
                dve.tensor_scalar(gres[:, :], mod_col(layer, j + 2), 1.0 if j == 3 else 0.5, None,
                                  ALU.mult).then_inc(sem("gres_ready"), 1)
            for k in range(KD if split else 0):
                dve.wait_ge(sem("xn_rounded"), 8 * split_index[n] + k + 1)
                if shift is None or whole:
                    ins = dve.tensor_tensor(xl[:, k, :], xm[:, k, :], xh[:, k, :].bitcast(F32), ALU.subtract)
                else:
                    ins = dve.scalar_tensor_tensor(out=xl[:, k, :], in0=xm[:, k, :], scalar=shift[:, k:k + 1],
                                                   in1=xh[:, k, :].bitcast(F32), op0=ALU.add, op1=ALU.subtract)
                ins.then_inc(sem("xn_split"), 1)

        split_index, shift_index, k_split, k_shift = {}, {}, 0, 0
        for n, (kind, idx, _) in enumerate(phases):
            if kind != "final":
                split_index[n] = k_split
                k_split += 1
                if kind in ("mix2", "mix3"):
                    shift_index[n] = k_shift
                    k_shift += 1
        residual_index = split_index

        def mod_col(layer, j):
            c = (9 * layer + j) * KD
            return mod_tab[:, c:c + KD]

        MOD_OF = {4: (0, 0), 5: (0, 3), 6: (0, 6), 7: (1, 0), 8: (1, 3), 9: (1, 6)}
        GAIN_OF = {0: "g_ffn1", 1: "g_mix", 2: "g_ffn2", 3: "g_final", 10: "g_final2"}

        def dve_gain(dve, n):
            if n in MOD_OF:
                layer, j = MOD_OF[n]
                g = prm("norm_g2")[:, (3 * layer + j // 3) * KD:(3 * layer + j // 3 + 1) * KD]
                dve.scalar_tensor_tensor(out=gmod[:, :], in0=mod_col(layer, j + 1), scalar=1.0, in1=g,
                                         op0=ALU.add, op1=ALU.mult).then_inc(sem("gmod_ready"), 1)

        def dve_phase_norm(dve, n):
            if n in MOD_OF:
                layer, j = MOD_OF[n]
                dve.wait_ge(sem("gmod_ready"), 1 + sum(m < n for m in MOD_OF))
                dve_norm(dve, n, gmod, mod_col(layer, j), whole=phases[n][0] != "ffn")
            else:
                dve_norm(dve, n, prm(GAIN_OF[n]), None, split=(n not in (3, 10)))

        def dve_phase_residual(dve, n):
            last = first_block[n] + phases[n][2] - 1
            acc = ACC if phases[n][0] == "ffn" else MIX_ACC
            if n in MOD_OF:
                dve.wait_ge(sem("gres_ready"), 1 + sum(m < n for m in MOD_OF))
                dve_residual(dve, n, residual_index[n], last, gain=gres, acc=acc)
            else:
                dve_residual(dve, n, residual_index[n], last, acc=acc, scale=0.5 if n != 1 else 1.0)

        def pe_ffn(pe, n, f, groups):
            F0, S0 = first_block[n], STEPS * f
            pe_norm(pe, n)
            if S0:
                pe.wait_ge(sem("silu_done"), S0)
                pe.wait_ge(sem("hid_ready"), S0)
            pe_in(pe, F0, pair(GATE), first_pass_waits=8 * split_index[n])
            pe_in(pe, F0 + 1, pair(UP))

            def step(q, i, with_mod, g0):
                b = F0 + 2 + 3 * q
                pe.wait_ge(sem("silu_done"), S0 + 1 + q + 2 * i)
                pe_in(pe, b, pair(GATE), i, 6)
                pe.wait_ge(sem("hid_ready"), S0 + 1 + q + 2 * i)
                pe_in(pe, b + 1, pair(UP), i, 6)
                pe.wait_ge(sem("hid_split"), S0 + 1 + q + 2 * i)
                return b + 2

            def mod_reduce(i, g0):
                pe.wait_ge(sem("mod_step"), 8 * (g0 + 1) + 8 * i)
                for j in range(KD):
                    mm = pe.matmul(MODP[:, j:j + 1], mod_acc[:, j * P:j * P + P], ones[:, 0:1], start=True, stop=True)
                mm.then_inc(sem("mod_reduced"), 1)

            def turns(lo, hi, with_mod):
                g0 = group0[f]
                def turn(i, first):
                    for q in range(2):
                        b = step(q, i, with_mod, g0)
                        pe_out(pe, b, hid_hi[:, q], hid_lo[:, q], first and q == 0, False, i, 6,
                               between=(lambda: mod_reduce(i, g0)) if with_mod and q == 1 else None)
                if lo == 0:
                    turn(0, True)
                    lo = 1
                if hi > lo:
                    with pe.Fori(lo, hi) as i:
                        turn(i, False)

            if groups:
                turns(0, groups, True)
            if groups < 5:
                turns(groups, 5, False)
            pe.wait_ge(sem("hid_split"), S0 + STEPS)
            pe_out(pe, F0 + 32, hid_hi[:, 0], hid_lo[:, 0], False, True)

        def act_ffn(act, n, f, groups):
            F0, S0 = first_block[n], STEPS * f
            act_norm(act, n, shift=mod_col(MOD_OF[n][0], MOD_OF[n][1]) if n in MOD_OF else None)
            if n == TABLES_AT:
                act.dma_start(pos_i[:, :], a_pos).then_inc(sem("pos_loaded"), 16)
            if n == 0:
                act_split(act, 1)
                act.wait_ge(sem("params_loaded"), 16)
                act.activation(c_act[:, :], prm("c"), ACT.Silu).then_inc(sem("c_ready"), 1)
            act_split(act, F0 + 2)

            def post(gate_block, s, parity, i=0, per=0, ps=0):
                act.wait_ge(sem("w_used"), gate_block + 1 + per * i)
                act.activation(gate[:, :, :], pair(GATE), ACT.Silu).then_inc(sem("silu_done"), 1)
                act.wait_ge(sem("hid_ready"), s + 1 + ps * i)
                act.activation(hid_hi[:, parity], hid[:, :, :], ACT.Copy).then_inc(sem("hid_rounded"), 1)

            if n == TABLES_AT:
                act_tables(act)
            post(F0, S0, 0)
            with act.Fori(0, 5) as i:
                for q in range(2):
                    b = F0 + 2 + 3 * q
                    act_split(act, b + 1, i, 6)
                    act_split(act, b + 2, i, 6)
                    act_split(act, b + 3, i, 6)
                    post(b, S0 + 1 + q, (1 + q) % 2, i, 6, 2)
            act_split(act, F0 + 33)
            act_split_halves(act, n + 1)

        def dve_ffn(dve, n, f, groups):
            F0, S0 = first_block[n], STEPS * f
            dve_phase_norm(dve, n)
            if n == 0:
                dve_split(dve, 1)
                dve.wait_ge(sem("params_loaded"), 16)
                dve.wait_ge(sem("c_ready"), 1)
            if n == TABLES_AT:
                dve_tables(dve)
            dve_split(dve, F0 + 2)

            def post(up_block, s, parity, i=0, per=0, ps=0):
                dve.wait_ge(sem("silu_done"), s + 1 + ps * i)
                dve.wait_ge(sem("w_used"), up_block + 1 + per * i)
                dve.tensor_tensor(hid[:, :, :], gate[:, :, :], pair(UP), ALU.mult).then_inc(sem("hid_ready"), 1)
                dve.wait_ge(sem("hid_rounded"), s + 1 + ps * i)
                dve.tensor_tensor(hid_lo[:, parity], hid[:, :, :], hid_hi[:, parity].bitcast(F32), ALU.subtract)\
                   .then_inc(sem("hid_split"), 1)

            def mod_block(q, g0, i):
                s = q % 2
                dve.wait_ge(sem(f"mod_loaded{s}"), 16 * (2 * g0 + q // 2 + 1) + 32 * i)
                for t in range(2):
                    k = 2 * q + t
                    if k == 0:
                        ins = dve.tensor_scalar(mod_acc[:, :], mod_raw[:, s, 0:D], c_act[:, 0:1], None, ALU.mult)
                    else:
                        dve.wait_ge(sem("mod_step"), 8 * g0 + k + 8 * i)
                        ins = dve.scalar_tensor_tensor(out=mod_acc[:, :], in0=mod_raw[:, s, t * D:t * D + D],
                                                       scalar=c_act[:, k:k + 1], in1=mod_acc[:, :],
                                                       op0=ALU.mult, op1=ALU.add)
                    ins.then_inc(sem("mod_step"), 1)

            def mod_store(g0, i):
                dve.wait_ge(sem("mod_reduced"), g0 + 1 + i)
                lo, _ = P_AT["mod_b"]
                dve.tensor_tensor(mod_tab[:, ds(8 * g0 + 8 * i, 8)], MODP[:, 0:8],
                                  params[:, ds(lo + 8 * g0 + 8 * i, 8)], ALU.add).then_inc(sem("mod_stored"), 1)

            post(F0 + 1, S0, 0)

            def turns(lo, hi, with_mod):
                g0 = group0[f]
                with dve.Fori(lo, hi) as i:
                    for q in range(2):
                        b = F0 + 2 + 3 * q
                        dve_split(dve, b + 1, i, 6)
                        if with_mod:
                            mod_block(2 * q, g0, i)
                        dve_split(dve, b + 2, i, 6)
                        if with_mod:
                            mod_block(2 * q + 1, g0, i)
                        dve_split(dve, b + 3, i, 6)
                        post(b + 1, S0 + 1 + q, (1 + q) % 2, i, 6, 2)
                        if with_mod and q == 1:
                            mod_store(g0, i)

            if groups:
                turns(0, groups, True)
            if groups < 5:
                turns(groups, 5, False)
            dve_split(dve, F0 + 33)
            if groups:
                dve.wait_ge(sem("mod_stored"), group0[f] + groups)
            dve_phase_residual(dve, n)

        group0, g = {}, 0
        for f in range(6):
            group0[f] = g
            g += MOD_GROUPS[f]

        MIX_ACC = (STAT, MODP, GATE, UP)

        def over(ap, shape):
            return ap.unsqueeze(1).to_broadcast(shape)

        def row_pick(n_rows, r):
            return ident[0:n_rows, r:r + 1].to_broadcast([n_rows, P])

        def act_conv(act, name, src, dst, w, b, t0):
            for m in range(2):
                act.activation(dst[:, m, :], src[:, m, :], ACT.Identity, scale=w[:, 4 * (t0 + m) + 3:4 * (t0 + m) + 4],
                               bias=b[:, t0 + m:t0 + m + 1]).then_inc(sem(name + "_start"), 1)

        def dve_conv(dve, name, src, dst, w, t0, done):
            step = 0
            for s in range(1, 4):
                for m in range(2):
                    wcol = w[:, 4 * (t0 + m) + 3 - s:4 * (t0 + m) + 4 - s]
                    if s == 1 and m == 0:
                        dve.wait_ge(sem(name + "_start"), t0 + 2)
                    elif s > 1:
                        dve.wait_ge(sem(name), done + step - 1)
                    dve.scalar_tensor_tensor(out=dst[:, m, s:T], in0=src[:, m, 0:T - s], scalar=wcol,
                                             in1=dst[:, m, s:T], op0=ALU.mult, op1=ALU.add).then_inc(sem(name), 1)
                    step += 1

        def pe_mask(pe, out, which):
            lhsT, rhs = (ident_b, mask_b) if which == "maskT" else (mask_b, ident_b)
            return pe.matmul(out, lhsT[:, :], rhs[:, :], start=False, stop=True, skip_group_check=True)

        (qk, v_tok, fo, gsu, sgu_v, pre, e1, p1) = region(
            m1_qk=([P, 16, T], F32), m1_v=([P, 2, D], F32), m1_fo=([P, KD, T], F32), m1_gsu=([P, KD, T], F32),
            m1_sgu_v=([P, 2, D], F32), m1_pre=([P, 2, 2, T], F32), m1_e=([P, 2, 384], F32), m1_p=([P, 2, 384], F32))
        sgu_gb = gsu
        _, merged_hi, _, merged_lo = region(
            m1_over_q=([P, KD, T], F32), m1_merged_hi=([P, KD, T], F32R), m1_over_v=([P, 2, D], F32),
            m1_merged_lo=([P, KD, T], F32R))
        HEAD_A = {12: 0, 14: 1, 16: 2, 18: 3}
        HEAD_B = {13: 0, 15: 1, 17: 2, 19: 3}
        ROWS_AFTER, CCOLS_AFTER, MEAN_AFTER, VAR_AFTER, SPREAD_AFTER, SGU_AFTER = 8, 10, 20, 22, 23, 27

        def pe_mix1(pe, n, _):
            F0 = first_block[n]
            pe_norm(pe, n)

            def blk(j, **kw):
                if 2 <= j < 10:
                    pe.wait_ge(sem("m1_conv"), 6 * (j - 1))
                elif j >= 10:
                    pe.wait_ge(sem("m1_evac"), j - 9)
                out = pair((GATE, UP)[j % 2])
                (pe_tok if 8 <= j < 16 else pe_in)(pe, F0 + j, out, **kw)

            def gates():
                for k in range(KD):
                    mm = pe.matmul(MODP[0:64, 0:T], prm("w_if")[:, k * 64:k * 64 + 64], xm[:, k, :],
                                   start=(k == 0), stop=(k == KD - 1))
                mm.then_inc(sem("m1_gates"), 1)

            def ccols():
                pe.wait_ge(sem("m1_row"), 13)
                for tt in range(2):
                    mm = pe.matmul(STAT[:, 4 * tt:4 * tt + 4], rows[0:4, 0, tt * P:tt * P + P], ident[0:4, 0:4],
                                   start=True, stop=True)
                mm.then_inc(sem("m1_ccols"), 1)

            def head_a(h):
                if h >= 1:
                    pe.wait_ge(sem("m1_p"), h)
                else:
                    pe.wait_ge(sem("m1_silu"), 8)
                for st in range(2):
                    for k in range(2):
                        mm = pe.matmul(ACC[0][:, 256 * st:256 * st + T - P * st], qk[:, 8 + 2 * h + k, st * P:st * P + P],
                                       qk[:, 2 * h + k, st * P:T], start=(st == 0 and k == 0), stop=(k == 1),
                                       skip_group_check=True)
                mm.then_inc(sem("m1_scores"), 1)
                if h >= 1:
                    pe.wait_ge(sem("m1_e_ready"), 2 * h)
                pe.matmul(ACC[1][:, 0:T], row_pick(4, h), rows[0:4, 2, :], start=True, stop=True, skip_group_check=True)
                pe.matmul(ACC[1][:, 256:384], row_pick(4, h), rows[0:4, 2, P:T], start=False, stop=True,
                          skip_group_check=True)
                pe_mask(pe, ACC[1][:, 0:P], "maskT")
                pe_mask(pe, ACC[1][:, 256:384], "maskT").then_inc(sem("m1_bias"), 1)

            def head_b(h):
                if h >= 1:
                    pe.wait_ge(sem("m1_h"), h)
                pe.wait_ge(sem("m1_p"), h + 1)
                p = p1[:, h % 2, :]
                pe.matmul(ACC[3][:, 0:T], ones, p[:, 0:T], start=True, stop=False, skip_group_check=True)
                pe.matmul(ACC[3][:, P:T], ones, p[:, 256:384], start=False, stop=True, skip_group_check=True)
                pe.matmul(ACC[3][:, T:2 * T], row_pick(4, h), rows[0:4, 3, :], start=False, stop=True,
                          skip_group_check=True).then_inc(sem("m1_den"), 1)
                for e in range(2):
                    c = h * DH_M + e * P
                    pe.matmul(ACC[2][:, e * T:e * T + T], v_tok[:, 0, c:c + P], p[:, 0:T], start=(e == 0), stop=False,
                              skip_group_check=True)
                    mm = pe.matmul(ACC[2][:, e * T + P:e * T + T], v_tok[:, 1, c:c + P], p[:, 256:384], start=False,
                                   stop=True, skip_group_check=True)
                mm.then_inc(sem("m1_num"), 1)

            def means():
                pe.wait_ge(sem("m1_p"), 4)
                pe.wait_ge(sem("m1_e_ready"), 8)
                for h in range(HEADS_M):
                    pe.wait_ge(sem("m1_h"), h + 1)
                    for e in range(2):
                        mm = pe.matmul(pair(ACC[h // 2])[:, h % 2, :], ones, qk[:, 2 * h + e, :], start=(e == 0),
                                       stop=(e == 1))
                    mm.then_inc(sem("m1_mean"), 1)

            def variances():
                for h in range(HEADS_M):
                    pe.wait_ge(sem("m1_squared"), h + 1)
                    for e in range(2):
                        for tt in range(2):
                            c = 2 * h + tt
                            mm = pe.matmul(ACC[2][:, c:c + 1], xm[:, 2 * h + e, tt * P:tt * P + P], ones[:, 0:1],
                                           start=(h == 0 and e == 0 and tt == 0), stop=(e == 1), skip_group_check=True)
                mm.then_inc(sem("m1_var"), 1)

            def spread():
                pe.wait_ge(sem("m1_inv"), 1)
                for h in range(HEADS_M):
                    for tt in range(2):
                        c = 2 * h + tt
                        mm = pe.matmul(pair(ACC[2 + h // 2])[:, h % 2, tt * P:tt * P + P],
                                       cols[:, 32 + c:33 + c].to_broadcast([P, P]), ident,
                                       start=(h % 2 == 0 and tt == 0), stop=True, skip_group_check=True)
                    if h % 2 == 1:
                        mm.then_inc(sem("m1_spread"), 1)

            def sgu():
                pe.wait_ge(sem("m1_centred"), 4)
                pe.wait_ge(sem("m1_normed"), 4)
                pe.wait_ge(sem("m1_sgu_ready"), 2)
                for c in range(KD):
                    for nb in range(2):
                        out = pair(ACC[c // 2])[:, c % 2, nb * P:nb * P + P]
                        pe.matmul(out, sgu_v[:, nb, c * P:c * P + P], prm("sgu_wT")[:, (c // 2) * P:(c // 2) * P + P],
                                  start=True, stop=False, skip_group_check=True)
                        mm = pe.matmul(out, row_pick(4, c // 2), prm("sgu_bs")[0:4, :], start=False, stop=True,
                                       skip_group_check=True)
                    if c % 2 == 1:
                        mm.then_inc(sem("m1_sgu_mixed"), 1)

            for j in range(MIX1_IN):
                blk(j, **({"first_pass_waits": 8 * split_index[n]} if j == 0 else {}))
                if j == 1:
                    gates()
                if j == CCOLS_AFTER:
                    ccols()
                if j in HEAD_A:
                    head_a(HEAD_A[j])
                if j in HEAD_B:
                    head_b(HEAD_B[j])
                if j == MEAN_AFTER:
                    means()
                if j == VAR_AFTER:
                    variances()
                if j == SPREAD_AFTER:
                    spread()
                if j == SGU_AFTER:
                    sgu()
            for b in range(MIX1_OUT):
                pe.wait_ge(sem("m1_split"), b + 1)
                pe_out(pe, F0 + MIX1_IN + b, merged_hi[:, 2 * b:2 * b + 2, :], merged_lo[:, 2 * b:2 * b + 2, :], b == 0,
                       b == MIX1_OUT - 1, acc=MIX_ACC, banks_free=("m1_evac", 24) if b == 0 else None)

        def act_mix1(act, n, _):
            F0 = first_block[n]
            act.dma_start(sgu_gb[:, :, :], a_sgu.rearrange("p (k t) -> p k t", k=KD)).then_inc(sem("sgu_loaded"), 16)
            act_norm(act, n)
            r = rows

            def row_chain():
                act.wait_ge(sem("m1_gates"), 1)
                act.activation(r[0:4, 0, :], MODP[0:4, 0:T], ACT.Identity, bias=prm("b_i")[0:4, :]).then_inc(sem("m1_row"), 1)
                act.activation(r[0:4, 1, :], MODP[32:36, 0:T], ACT.Identity, bias=prm("b_f")[32:36, :])\
                   .then_inc(sem("m1_row"), 1)
                act.wait_ge(sem("m1_row"), 2)
                act.activation(r[0:4, 2, :], r[0:4, 1, :], ACT.Abs).then_inc(sem("m1_row"), 1)
                act.wait_ge(sem("m1_row"), 3)
                act.activation(r[0:4, 2, :], r[0:4, 2, :], ACT.Exp, scale=-1.0).then_inc(sem("m1_row"), 1)
                act.wait_ge(sem("m1_row"), 4)
                act.activation(r[0:4, 2, :], r[0:4, 2, :], ACT.Ln, bias=cst("ones")[0:4, 0:1]).then_inc(sem("m1_row"), 1)

            def row_end():
                act.wait_ge(sem("m1_row"), 12)
                act.activation(r[0:4, 3, :], r[0:4, 3, :], ACT.Exp, scale=-1.0).then_inc(sem("m1_row"), 1)

            def head_a(h):
                if h == 0:
                    act.wait_ge(sem("m1_cols"), 1)
                if h >= 2:
                    act.wait_ge(sem("m1_p"), h - 1)
                act.wait_ge(sem("m1_bias"), h + 1)
                for st in range(2):
                    c0, c1 = 256 * st, 256 * st + T - P * st
                    act.activation(e1[:, h % 2, c0:c1], ACC[1][:, c0:c1], ACT.Exp,
                                   bias=cols[:, 4 * st + h:4 * st + h + 1]).then_inc(sem("m1_e_ready"), 1)

            def head_b(h):
                act.wait_ge(sem("m1_den"), h + 1)
                if h >= 1:
                    act.wait_ge(sem("m1_h"), h)
                act.activation(std[:, :], ACC[3][:, 0:T], ACT.Abs).then_inc(sem("m1_abs"), 1)

            def blk(j):
                if j >= 1:
                    act_split(act, F0 + j + 2)
                bank_j = pair((GATE, UP)[j % 2])
                if j < 8:
                    act.wait_ge(sem("w_used"), F0 + j + 1)
                    if j >= 2:
                        act.wait_ge(sem("m1_silu"), j - 1)
                    act_conv(act, "m1_conv", bank_j, pre[:, j % 2], prm("conv_w1"), prm("conv_b1"), 2 * j)
                if 1 <= j < 9:
                    i = j - 1
                    act.wait_ge(sem("m1_conv"), 6 * i + 6)
                    act.activation(qk[:, 2 * i:2 * i + 2, :], pre[:, i % 2], ACT.Silu).then_inc(sem("m1_silu"), 1)
                if j < 8:
                    return
                act.wait_ge(sem("w_used"), F0 + j + 1)
                c = (j % 4) * 256
                if j < 12:
                    act.activation(v_tok[:, :, c:c + 256], bank_j, ACT.Copy).then_inc(sem("m1_evac"), 1)
                elif j < 16:
                    act.activation(sgu_v[:, :, c:c + 256], bank_j, ACT.Gelu).then_inc(sem("m1_evac"), 1)
                else:
                    if j == 16:
                        for tt in range(2):
                            act.wait_ge(sem("m1_sgu_var"), tt + 1)
                            act.activation(cols[:, 20 + tt:21 + tt], cols[:, 17 + 2 * tt:18 + 2 * tt], ACT.Sqrt,
                                           bias=cols[:, 65:66]).then_inc(sem("m1_sgu_std"), 1)
                    k = 2 * (j % 4)
                    if j < 20:
                        dst, f = fo[:, k:k + 2, :], ACT.Sigmoid
                    elif j < 24:
                        dst, f = pre[:, j % 2], ACT.Sigmoid
                    elif j < 28:
                        dst, f = gsu[:, k:k + 2, :], ACT.Sigmoid
                    else:
                        dst, f = pre[:, j % 2], ACT.Gelu
                    if j == 24:
                        act.wait_ge(sem("m1_sgu_ready"), 2)
                    if 22 <= j < 24:
                        act.wait_ge(sem("m1_gated"), j - 21)
                    if j >= 28:
                        act.wait_ge(sem("m1_gated"), 4 + max(0, j - 29))
                    act.activation(dst, bank_j, f).then_inc(sem("m1_evac"), 1)

            act_split(act, F0 + 2)
            for j in range(MIX1_IN):
                blk(j)
                if j == ROWS_AFTER:
                    row_chain()
                if j == ROWS_AFTER + 1:
                    row_end()
                if j in HEAD_A:
                    head_a(HEAD_A[j])
                if j in HEAD_B:
                    head_b(HEAD_B[j])
                if j == MEAN_AFTER:
                    for h in range(HEADS_M):
                        act.wait_ge(sem("m1_centred"), h + 1)
                        act.activation(xm[:, 2 * h:2 * h + 2, :], qk[:, 2 * h:2 * h + 2, :], ACT.Square)\
                           .then_inc(sem("m1_squared"), 1)
                if j == VAR_AFTER:
                    act.wait_ge(sem("m1_var"), 1)
                    act.activation(cols[:, 24:32], ACC[2][:, 0:8], ACT.Sqrt, scale=1.0 / DH_M, bias=cols[:, 65:66])\
                       .then_inc(sem("m1_std"), 1)
                if j >= 28:
                    b = j - 28
                    act.wait_ge(sem("m1_merged"), b + 1)
                    act.activation(merged_hi[:, 2 * b:2 * b + 2, :], xm[:, 2 * b:2 * b + 2, :], ACT.Copy)\
                       .then_inc(sem("m1_rounded"), 1)
            for b in range(3):
                act_split(act, F0 + MIX1_IN + 2 + b)
            act_split_halves(act, n + 1)

        def dve_mix1(dve, n, _):
            F0 = first_block[n]
            dve_phase_norm(dve, n)
            wt = prm("sgu_wT").rearrange("p (g t) -> p g t", g=SGU_G)
            dve.memset(wt[64:128, :, 0:64], 0.0).then_inc(sem("m1_masked"), 1)

            def row_chain():
                r = rows
                dve.wait_ge(sem("m1_row"), 5)
                dve.tensor_scalar(r[0:4, 3, :], r[0:4, 1, :], 0.0, None, ALU.min).then_inc(sem("m1_row"), 1)
                dve.wait_ge(sem("m1_row"), 6)
                dve.tensor_tensor(r[0:4, 3, :], r[0:4, 3, :], r[0:4, 2, :], ALU.subtract).then_inc(sem("m1_row"), 1)
                dve.wait_ge(sem("m1_row"), 7)
                dve.tensor_tensor_scan(r[0:4, 4, :], ones[0:4, 0:1].to_broadcast([4, T]), r[0:4, 3, :], 0.0,
                                       ALU.mult, ALU.add).then_inc(sem("m1_row"), 1)
                dve.wait_ge(sem("m1_row"), 8)
                dve.tensor_tensor(r[0:4, 0, :], r[0:4, 0, :], r[0:4, 4, :], ALU.subtract).then_inc(sem("m1_row"), 1)
                dve.wait_ge(sem("m1_row"), 9)
                dve.tensor_tensor_scan(r[0:4, 1, :], r[0:4, 0, :], r[0:4, 0, :], 0.0, ALU.max, ALU.max)\
                   .then_inc(sem("m1_row"), 1)
                dve.wait_ge(sem("m1_row"), 10)
                dve.tensor_tensor(r[0:4, 3, :], r[0:4, 4, :], r[0:4, 1, :], ALU.add).then_inc(sem("m1_row"), 1)
                dve.tensor_scalar(r[0:4, 2, :], r[0:4, 1, :], -1.0, None, ALU.mult).then_inc(sem("m1_row"), 1)

            def head_a(h):
                dve.wait_ge(sem("m1_scores"), h + 1)
                dve.wait_ge(sem("m1_e_ready"), 2 * h + 2)
                if h >= 2:
                    dve.wait_ge(sem("m1_num"), h - 1)
                dve.scalar_tensor_tensor(out=p1[:, h % 2, :], in0=ACC[0][:, 0:384], scalar=DH_M ** -0.5,
                                         in1=e1[:, h % 2, :], op0=ALU.mult, op1=ALU.mult).then_inc(sem("m1_p"), 1)

            def head_b(h):
                dve.wait_ge(sem("m1_abs"), h + 1)
                dve.tensor_tensor(rstd[:, :], std[:, :], ACC[3][:, T:2 * T], ALU.max).then_inc(sem("m1_div"), 1)
                dve.wait_ge(sem("m1_div"), 2 * h + 1)
                dve.reciprocal(rstd[:, :], rstd[:, :]).then_inc(sem("m1_div"), 1)
                dve.wait_ge(sem("m1_div"), 2 * h + 2)
                dve.wait_ge(sem("m1_num"), h + 1)
                dve.tensor_tensor(qk[:, 2 * h:2 * h + 2, :], pair(ACC[2]), over(rstd[:, :], [P, 2, T]), ALU.mult)\
                   .then_inc(sem("m1_h"), 1)

            def sgu_stats():
                for tt in range(2):
                    st = rstats[:, tt]
                    dve.wait_ge(sem("m1_evac"), 8)
                    for half in range(2):
                        dve.bn_stats(st[:, 6 * half:6 * half + 6], sgu_v[:, tt, 512 * half:512 * half + 512])\
                           .then_inc(sem("m1_bn"), 1)
                    dve.wait_ge(sem("m1_bn"), 2 * tt + 2)
                    dve.bn_aggr(cols[:, 16 + 2 * tt:18 + 2 * tt], st).then_inc(sem("m1_sgu_var"), 1)

            def sgu_norm(step):
                gb = sgu_gb[:, :, :].rearrange("p k t -> p (k t)")
                tt, i = step // 3, step % 3
                v = sgu_v[:, tt, :]
                if i == 0:
                    dve.wait_ge(sem("m1_sgu_std"), tt + 1)
                    dve.reciprocal(cols[:, 22 + tt:23 + tt], cols[:, 20 + tt:21 + tt]).then_inc(sem("m1_sgu_step"), 1)
                    dve.wait_ge(sem("m1_sgu_step"), 3 * tt + 1)
                    dve.tensor_scalar(v, v, cols[:, 16 + 2 * tt:17 + 2 * tt], cols[:, 22 + tt:23 + tt], ALU.subtract,
                                      ALU.mult).then_inc(sem("m1_sgu_step"), 1)
                elif i == 1:
                    dve.wait_ge(sem("m1_sgu_step"), 3 * tt + 2)
                    dve.wait_ge(sem("sgu_loaded"), 16)
                    dve.tensor_tensor(v, v, gb[:, 0:D], ALU.mult).then_inc(sem("m1_sgu_step"), 1)
                else:
                    dve.wait_ge(sem("m1_sgu_step"), 3 * tt + 3)
                    dve.tensor_tensor(v, v, gb[:, D:2 * D], ALU.add).then_inc(sem("m1_sgu_ready"), 1)

            def blk(j):
                bank_j = pair((GATE, UP)[j % 2])
                if j < 8:
                    dve_conv(dve, "m1_conv", bank_j, pre[:, j % 2], prm("conv_w1"), 2 * j, 6 * j)
                elif 20 <= j < 24:
                    k = 2 * (j % 4)
                    dve.wait_ge(sem("m1_evac"), j - 7)
                    dve.tensor_tensor(fo[:, k:k + 2, :], fo[:, k:k + 2, :], pre[:, j % 2], ALU.mult)\
                       .then_inc(sem("m1_gated"), 1)
                elif j >= 28:
                    k = 2 * (j % 4)
                    dve.wait_ge(sem("m1_evac"), j - 7)
                    dve.tensor_tensor(gsu[:, k:k + 2, :], gsu[:, k:k + 2, :], pre[:, j % 2], ALU.mult)\
                       .then_inc(sem("m1_gated"), 1)

            def finish_heads(b):
                for h in (2 * b, 2 * b + 1):
                    hp = qk[:, 2 * h:2 * h + 2, :]
                    dve.wait_ge(sem("m1_spread"), b + 1)
                    dve.tensor_tensor(hp, hp, over(pair(ACC[2 + b])[:, h % 2, :], [P, 2, T]), ALU.mult)\
                       .then_inc(sem("m1_normed"), 1)
                for k in range(4 * b, 4 * b + 4):
                    if k % 2 == 0:
                        dve.wait_ge(sem("m1_normed"), k // 2 + 1)
                    if k == 0:
                        dve.wait_ge(sem("m1_gated"), 4)
                    dve.scalar_tensor_tensor(out=qk[:, k, :], in0=qk[:, k, :], scalar=prm("head_g")[:, k:k + 1],
                                             in1=fo[:, k, :], op0=ALU.mult, op1=ALU.mult).then_inc(sem("m1_branch"), 1)

            def merge(b):
                k = 2 * b
                dve.wait_ge(sem("m1_sgu_mixed"), b + 1)
                dve.wait_ge(sem("m1_gated"), 4 + b + 1)
                dve.wait_ge(sem("m1_branch"), k + 2)
                dve.tensor_tensor(xm[:, k:k + 2, :], pair(ACC[b]), gsu[:, k:k + 2, :], ALU.mult).then_inc(sem("m1_sum"), 1)
                dve.wait_ge(sem("m1_sum"), b + 1)
                dve.tensor_tensor(xm[:, k:k + 2, :], xm[:, k:k + 2, :], qk[:, k:k + 2, :], ALU.add)\
                   .then_inc(sem("m1_merged"), 1)
                dve.wait_ge(sem("m1_rounded"), b + 1)
                dve.tensor_tensor(merged_lo[:, 2 * b:2 * b + 2, :], xm[:, 2 * b:2 * b + 2, :],
                                  merged_hi[:, 2 * b:2 * b + 2, :].bitcast(F32), ALU.subtract).then_inc(sem("m1_split"), 1)

            dve_split(dve, F0 + 2)
            for j in range(MIX1_IN):
                if j >= 1:
                    dve_split(dve, F0 + j + 2)
                blk(j)
                if j == ROWS_AFTER:
                    row_chain()
                if j == CCOLS_AFTER:
                    dve.wait_ge(sem("m1_ccols"), 1)
                    dve.tensor_copy(cols[:, 0:8], STAT[:, 0:8]).then_inc(sem("m1_cols"), 1)
                if j == 15:
                    sgu_stats()
                if j in HEAD_A:
                    head_a(HEAD_A[j])
                if j in HEAD_B:
                    head_b(HEAD_B[j])
                if j == MEAN_AFTER:
                    for h in range(HEADS_M):
                        dve.wait_ge(sem("m1_mean"), 2 * (h // 2) + 2)
                        hp = qk[:, 2 * h:2 * h + 2, :]
                        mean = over(ACC[h // 2][:, (h % 2) * T:(h % 2) * T + T], [P, 2, T])
                        dve.scalar_tensor_tensor(out=hp, in0=mean, scalar=-1.0 / DH_M, in1=hp, op0=ALU.mult, op1=ALU.add)\
                           .then_inc(sem("m1_centred"), 1)
                if 16 <= j < 22:
                    sgu_norm(j - 16)
                if j == VAR_AFTER:
                    dve.wait_ge(sem("m1_std"), 1)
                    dve.reciprocal(cols[:, 32:40], cols[:, 24:32]).then_inc(sem("m1_inv"), 1)
                if j in (24, 25):
                    finish_heads(j - 24)
                if j >= 28:
                    merge(j - 28)
            for b in range(3):
                dve_split(dve, F0 + MIX1_IN + 2 + b)
            dve_phase_residual(dve, n)

        (xbc, pu, zs, x_tok, cb, pre2, e2, p2, cat_hi, cat_lo) = region(
            m2_xbc=([P, 12, T], F32), m2_pu=([P, 4, T], F32), m2_zs=([P, KD, T], F32), m2_x_tok=([P, 2, D], F32),
            m2_cb=([P, 2, 384], F32), m2_pre=([P, 2, 2, T], F32), m2_e=([P, 2, 384], F32), m2_p=([P, 2, 384], F32),
            m2_cat_hi=([P, 4, T], F32R), m2_cat_lo=([P, 4, T], F32R))
        NEG_A, DT_C = 0, 32
        POOLED = (MODP, STAT)
        M2_ROWS_AFTER = 6
        SSD_STEPS = {9: ((), (), (), (0,)), 10: ((1,), (2,), (3,), (4, 5)), 11: ((6,), (7,), (8,), (9, 10)),
                     12: ((11,), (12,), (13,), (14, 15, 16))}
        m2_y = pre2[:, :, :, :].rearrange("p a b t -> p (a b) t")

        def pe_mix2(pe, n, _):
            F0 = first_block[n]
            pe_norm(pe, n)

            def blk(j, **kw):
                if 2 <= j < 8:
                    pe.wait_ge(sem("m2_conv"), 6 * (j - 1))
                elif j >= 8:
                    pe.wait_ge(sem("m2_evac"), j - 7)
                pe_in(pe, F0 + j, pair((GATE, UP)[j % 2]), beside=beside(j), **kw)

            def beside(j):
                return (lambda quarter: steps(SSD_STEPS[j][quarter])) if j in SSD_STEPS else None

            def steps(hs):
                for h in hs:
                    if h < SSD_H:
                        bias(h)
                    if h >= 1:
                        head(h - 1)

            def squares_sum(g):
                if g == 0:
                    pe.wait_ge(sem("m2_e_ready"), 2 * SSD_H)
                for k in range(4 * g, 4 * g + 4):
                    if k % 2 == 0:
                        pe.wait_ge(sem("m2_squared"), k // 2 + 1)
                    mm = pe.matmul(ACC[g][:, 0:T], ones, zs[:, k, :], start=(k % 4 == 0), stop=(k % 4 == 3))
                mm.then_inc(sem("m2_var"), 1)

            def dt():
                for k in range(KD):
                    mm = pe.matmul(MODP[0:16, 0:T], prm("w_dt")[:, k * 16:k * 16 + 16], xm[:, k, :],
                                   start=(k == 0), stop=(k == KD - 1))
                mm.then_inc(sem("m2_dt"), 1)

            def columns():
                pe.wait_ge(sem("m2_row"), 9)
                for r in range(2):
                    for tt in range(2):
                        mm = pe.matmul(STAT[:, 32 * r + 16 * tt:32 * r + 16 * tt + 16],
                                       rows[0:16, 4 - r, tt * P:tt * P + P], ident[0:16, 0:16], start=True, stop=True)
                mm.then_inc(sem("m2_columns"), 1)

            def turn_x():
                pe.wait_ge(sem("m2_silu"), 4)
                for q in range(4):
                    tt, half = q // 2, q % 2
                    for c in range(4):
                        mm = pe.transpose(ACC[q][:, c * P:c * P + P], xbc[:, 4 * half + c, tt * P:tt * P + P], ident)
                    mm.then_inc(sem("m2_turned"), 1)

            def cb_products():
                pe.wait_ge(sem("m2_silu"), 6)
                for g in range(2):
                    pe.wait_ge(sem("m2_x_tok"), g + 1)
                    pe.matmul(ACC[g][:, 0:T], xbc[:, 8 + g, 0:P], xbc[:, 10 + g, :], start=True, stop=True,
                              skip_group_check=True)
                    pe.matmul(ACC[g][:, 256:384], xbc[:, 8 + g, P:T], xbc[:, 10 + g, P:T], start=False, stop=True,
                              skip_group_check=True).then_inc(sem("m2_cb"), 1)

            def pool():
                pe.wait_ge(sem("m2_cols"), 2)
                pe.wait_ge(sem("m2_pool_d"), 4)
                for g in range(4):
                    mm = pe.matmul(pair(POOLED[g // 2])[:, g % 2, :], prm("pool_w")[:, g * P:g * P + P], xm[:, g, :],
                                   start=True, stop=True)
                    if g % 2 == 1:
                        mm.then_inc(sem("m2_pooled"), 1)

            def bias(h):
                b = ACC[h % 2]
                if h == 0:
                    pe.wait_ge(sem("m2_cb_read"), 2)
                if h >= 2:
                    pe.wait_ge(sem("m2_e_ready"), 2 * (h - 1))
                pe.matmul(b[:, 0:T], row_pick(16, h), rows[0:16, 4, :], start=True, stop=True, skip_group_check=True)
                pe.matmul(b[:, 256:384], row_pick(16, h), rows[0:16, 4, P:T], start=False, stop=True,
                          skip_group_check=True)
                pe_mask(pe, b[:, 0:P], "maskT")
                pe_mask(pe, b[:, 256:384], "maskT").then_inc(sem("m2_bias"), 1)

            def head(h):
                k, r0 = h // 2, 64 * (h % 2)
                out = ACC[2 + k % 2]
                pe.wait_ge(sem("m2_m_ready"), 2 * h + 2)
                if h == 0:
                    pe.wait_ge(sem("m2_x_tok"), 4)
                if h >= 4 and h % 2 == 0:
                    pe.wait_ge(sem("m2_y"), k - 1)
                p = p2[:, h % 2, :]
                pe.matmul(out[r0:r0 + 64, 0:T], x_tok[:, 0, h * 64:h * 64 + 64], p[:, 0:T], start=True, stop=False,
                          skip_group_check=True)
                pe.matmul(out[r0:r0 + 64, P:T], x_tok[:, 1, h * 64:h * 64 + 64], p[:, 256:384], start=False, stop=True,
                          skip_group_check=True).then_inc(sem("m2_head"), 1)

            for j in range(MIX2_IN):
                blk(j, **({"first_pass_waits": 8 * split_index[n]} if j == 0 else {}))
                if j == 1:
                    dt()
                if j == 5:
                    turn_x()
                if j == 7:
                    columns()
                    cb_products()
                if j == 10:
                    pool()
            for b in range(MIX2_OUT):
                if b < 2:
                    if b == 0:
                        pe.wait_ge(sem("m2_evac"), 6)
                    pe.wait_ge(sem("m2_cat"), 4)
                    hi, lo = cat_hi[:, 2 * b:2 * b + 2, :], cat_lo[:, 2 * b:2 * b + 2, :]
                else:
                    pe.wait_ge(sem("m2_split"), b - 1)
                    hi, lo = xh[:, 2 * b - 4:2 * b - 2, :], xl[:, 2 * b - 4:2 * b - 2, :]
                pe_out(pe, F0 + MIX2_IN + b, hi, lo, b == 0, b == MIX2_OUT - 1, acc=MIX_ACC, beside=beside(MIX2_IN + b))
                if b == 0:
                    squares_sum(0)
                if b == 2:
                    squares_sum(1)

        def act_mix2(act, n, _):
            F0 = first_block[n]
            act_norm(act, n)
            r = rows

            def row_chain():
                act.wait_ge(sem("m2_dt"), 1)
                act.activation(r[0:16, 0, :], MODP[0:16, 0:T], ACT.Identity, bias=prm("dt_bias")[0:16, :])\
                   .then_inc(sem("m2_row"), 1)
                act.activation(rstd[0:16, 0:1], prm("a_log")[0:16, :], ACT.Exp).then_inc(sem("m2_row"), 1)
                act.wait_ge(sem("m2_row"), 2)
                act.activation(r[0:16, 1, :], r[0:16, 0, :], ACT.Abs).then_inc(sem("m2_row"), 1)
                act.wait_ge(sem("m2_row"), 3)
                act.activation(r[0:16, 1, :], r[0:16, 1, :], ACT.Exp, scale=-1.0).then_inc(sem("m2_row"), 1)
                act.wait_ge(sem("m2_row"), 4)
                act.activation(r[0:16, 1, :], r[0:16, 1, :], ACT.Ln, bias=cst("ones")[0:16, 0:1]).then_inc(sem("m2_row"), 1)

            def blk(j):
                bank_j = pair((GATE, UP)[j % 2])
                if j < 6:
                    act.wait_ge(sem("w_used"), F0 + j + 1)
                    if j >= 2:
                        act.wait_ge(sem("m2_silu"), j - 1)
                    act_conv(act, "m2_conv", bank_j, pre2[:, j % 2], prm("conv_w2"), prm("conv_b2"), 2 * j)
                if 1 <= j < 7:
                    i = j - 1
                    act.wait_ge(sem("m2_conv"), 6 * i + 6)
                    act.activation(xbc[:, 2 * i:2 * i + 2, :], pre2[:, i % 2], ACT.Silu).then_inc(sem("m2_silu"), 1)
                if j < 6:
                    return
                act.wait_ge(sem("w_used"), F0 + j + 1)
                k = 2 * (j - 6) if j < 8 else 2 * (j - 8)
                act.activation((pu if j < 8 else zs)[:, k:k + 2, :], bank_j, ACT.Silu if j in (8, 9) else ACT.Copy)\
                   .then_inc(sem("m2_evac"), 1)

            def head(h):
                act.wait_ge(sem("m2_bias"), h + 1)
                if h == 0:
                    act.wait_ge(sem("m2_cols"), 2)
                if h >= 2:
                    act.wait_ge(sem("m2_m_ready"), 2 * (h - 1))
                for st in range(2):
                    c0, c1 = 256 * st, 256 * st + T - P * st
                    a = NEG_A + 16 * st + h
                    act.activation(e2[:, h % 2, c0:c1], ACC[h % 2][:, c0:c1], ACT.Exp, bias=cols[:, a:a + 1])\
                       .then_inc(sem("m2_e_ready"), 1)

            act_split(act, F0 + 2)
            for j in range(MIX2_IN):
                if 1 <= j < 10:
                    act_split(act, F0 + j + 2)
                if j >= 10:
                    head(SSD_STEPS[j][0][0])
                    act_split(act, F0 + j + 2)
                    head(SSD_STEPS[j][1][0])
                    if j == 11:
                        for g in range(4):
                            act.wait_ge(sem("m2_pooled"), g // 2 + 1)
                            act.activation(cat_hi[:, g, :], pair(POOLED[g // 2])[:, g % 2, :], ACT.Identity,
                                           scale=prm("pool_scale")[:, g:g + 1]).then_inc(sem("m2_cat_hi"), 1)
                    head(SSD_STEPS[j][2][0])
                blk(j)
                if j == M2_ROWS_AFTER:
                    row_chain()
                if j == 6:
                    for q in range(4):
                        act.wait_ge(sem("m2_turned"), q + 1)
                        act.activation(x_tok[:, q // 2, 512 * (q % 2):512 * (q % 2) + 512], ACC[q][:, :], ACT.Copy)\
                           .then_inc(sem("m2_x_tok"), 1)
                for h in SSD_STEPS[j][3] if j >= 9 else ():
                    head(h)

            def squares(b):
                act.wait_ge(sem("m2_gated"), b + 1)
                act.activation(zs[:, 2 * b:2 * b + 2, :], xm[:, 2 * b:2 * b + 2, :], ACT.Square)\
                   .then_inc(sem("m2_squared"), 1)

            def root(g):
                act.wait_ge(sem("m2_var"), g + 1)
                act.activation(e2[:, g, 0:T], ACC[g][:, 0:T], ACT.Sqrt, scale=1.0 / 512, bias=cols[:, 64:65])\
                   .then_inc(sem("m2_std"), 1)

            def round_heads(b):
                act.wait_ge(sem("m2_normed"), b + 1)
                act.activation(xh[:, 2 * b:2 * b + 2, :], xm[:, 2 * b:2 * b + 2, :], ACT.Copy).then_inc(sem("m2_rounded"), 1)

            head(11)
            act_split(act, F0 + MIX2_IN + 2)
            for h in (12, 13, 14, 15):
                head(h)
            squares(0)
            squares(1)
            act.wait_ge(sem("m2_m_ready"), 2 * SSD_H)
            root(0)
            for b in (2, 3):
                if b == 2:
                    act.wait_ge(sem("m2_evac"), 6)
                act.activation(zs[:, 2 * b:2 * b + 2, :], zs[:, 2 * b:2 * b + 2, :], ACT.Silu).then_inc(sem("m2_z_silu"), 1)
            round_heads(0)
            round_heads(1)
            act_split(act, F0 + MIX2_IN + 3)
            squares(2)
            squares(3)
            root(1)
            act_split(act, F0 + MIX2_IN + 4)
            round_heads(2)
            round_heads(3)
            for b in range(3, MIX2_OUT - 1):
                act_split(act, F0 + MIX2_IN + 2 + b)
            act_split_halves(act, n + 1)

        def dve_mix2(dve, n, _):
            F0 = first_block[n]
            dve_phase_norm(dve, n)
            r = rows

            def row_chain():
                dve.wait_ge(sem("m2_row"), 5)
                dve.tensor_scalar(r[0:16, 2, :], r[0:16, 0, :], 0.0, None, ALU.max).then_inc(sem("m2_row"), 1)
                dve.wait_ge(sem("m2_row"), 6)
                dve.tensor_tensor(r[0:16, 3, :], r[0:16, 2, :], r[0:16, 1, :], ALU.add).then_inc(sem("m2_row"), 1)
                dve.wait_ge(sem("m2_row"), 7)
                dve.tensor_scalar(r[0:16, 0, :], r[0:16, 3, :], rstd[0:16, 0:1], -1.0, ALU.mult, ALU.mult)\
                   .then_inc(sem("m2_row"), 1)
                dve.wait_ge(sem("m2_row"), 8)
                dve.tensor_tensor_scan(r[0:16, 4, :], ones[0:16, 0:1].to_broadcast([16, T]), r[0:16, 0, :], 0.0,
                                       ALU.mult, ALU.add).then_inc(sem("m2_row"), 1)

            def pool(part):
                halves = (xm[:, 0:4, :], xm[:, 4:8, :])
                step, src = (0, pu) if part == 0 else (5, halves[0])
                dve.wait_ge(sem("m2_evac"), 2)
                for lv in ((0, 1), (2, 3))[part]:
                    sh, dst = 1 << lv, halves[(lv + 1) % 2]
                    if lv:
                        dve.wait_ge(sem("m2_pool"), step)
                    if lv:
                        dve.tensor_copy(dst[:, 0:lv, :], src[:, 0:lv, :]).then_inc(sem("m2_pool"), 1)
                        step += 1
                    dve.tensor_copy(dst[:, lv:4, 0:sh], src[:, lv:4, 0:sh]).then_inc(sem("m2_pool"), 1)
                    dve.tensor_tensor(dst[:, lv:4, sh:T], src[:, lv:4, sh:T], src[:, lv:4, 0:T - sh], ALU.add)\
                       .then_inc(sem("m2_pool"), 1)
                    step += 2
                    src = dst
                if part == 0:
                    return
                fix = cst("pool_fix").rearrange("p (g t) -> p g t", g=4)
                dve.wait_ge(sem("m2_pool"), step)
                dve.tensor_tensor(src[:, :, 0:16], src[:, :, 0:16], fix, ALU.mult).then_inc(sem("m2_pool"), 1)
                dve.wait_ge(sem("m2_pool"), step + 1)
                assert step == 11
                for g in range(4):
                    ins = dve.scalar_tensor_tensor(out=src[:, g, :], in0=src[:, g, :], scalar=1.0 / (2 << g),
                                                   in1=pu[:, g, :], op0=ALU.mult, op1=ALU.subtract)
                    ins.then_inc(sem("m2_pool_d"), 1)

            def head(h):
                if h == 0:
                    dve.wait_ge(sem("m2_cb_read"), 2)
                    dve.wait_ge(sem("m2_cols"), 2)
                if h >= 2:
                    dve.wait_ge(sem("m2_head"), h - 1)
                for st in range(2):
                    c0, c1 = 256 * st, 256 * st + T - P * st
                    d = DT_C + 16 * st + h
                    dve.wait_ge(sem("m2_e_ready"), 2 * h + st + 1)
                    dve.scalar_tensor_tensor(out=p2[:, h % 2, c0:c1], in0=e2[:, h % 2, c0:c1], scalar=cols[:, d:d + 1],
                                             in1=cb[:, h // 8, c0:c1], op0=ALU.mult, op1=ALU.mult)\
                       .then_inc(sem("m2_m_ready"), 1)
                if h % 2 == 1:
                    y_pair(dve, h // 2 - 1)

            dve_split(dve, F0 + 2)
            for j in range(MIX2_IN):
                if 1 <= j < 10:
                    dve_split(dve, F0 + j + 2)
                if j >= 10:
                    for q in (0, 1):
                        head(SSD_STEPS[j][q][0])
                    dve_split(dve, F0 + j + 2)
                    head(SSD_STEPS[j][2][0])
                    if j == 11:
                        for g in range(4):
                            dve.wait_ge(sem("m2_cat_hi"), 2 * (g // 2) + 2)
                            dve.scalar_tensor_tensor(out=cat_lo[:, g, :], in0=pair(POOLED[g // 2])[:, g % 2, :],
                                                     scalar=prm("pool_scale")[:, g:g + 1], in1=cat_hi[:, g, :].bitcast(F32),
                                                     op0=ALU.mult, op1=ALU.subtract).then_inc(sem("m2_cat"), 1)
                if j < 6:
                    dve_conv(dve, "m2_conv", pair((GATE, UP)[j % 2]), pre2[:, j % 2], prm("conv_w2"), 2 * j, 6 * j)
                if j == M2_ROWS_AFTER:
                    row_chain()
                if j == 8:
                    dve.wait_ge(sem("m2_columns"), 1)
                    dve.tensor_scalar(cols[:, NEG_A:NEG_A + 32], STAT[:, 0:32], -1.0, None, ALU.mult)\
                       .then_inc(sem("m2_cols"), 1)
                    dve.tensor_copy(cols[:, DT_C:DT_C + 32], STAT[:, 32:64]).then_inc(sem("m2_cols"), 1)
                    for g in range(2):
                        dve.wait_ge(sem("m2_cb"), g + 1)
                        dve.tensor_copy(cb[:, g, :], ACC[g][:, 0:384]).then_inc(sem("m2_cb_read"), 1)
                    pool(0)
                if j == 9:
                    pool(1)
                if j >= 9:
                    for h in SSD_STEPS[j][3]:
                        head(h)

            def gate(b):
                dve.wait_ge(sem("m2_y"), 2 * b + 2)
                if b == 0:
                    dve.wait_ge(sem("m2_evac"), 4)
                    dve.wait_ge(sem("m2_pooled"), 2)
                if b >= 2:
                    dve.wait_ge(sem("m2_z_silu"), b - 1)
                y = m2_y[:, 2 * b:2 * b + 2, :] if b < 2 else xm[:, 2 * b:2 * b + 2, :]
                dve.tensor_tensor(xm[:, 2 * b:2 * b + 2, :], y, zs[:, 2 * b:2 * b + 2, :], ALU.mult)\
                   .then_inc(sem("m2_gated"), 1)

            def rest(b):
                dve.wait_ge(sem("m2_rounded"), b + 1)
                dve.tensor_tensor(xl[:, 2 * b:2 * b + 2, :], xm[:, 2 * b:2 * b + 2, :],
                                  xh[:, 2 * b:2 * b + 2, :].bitcast(F32), ALU.subtract).then_inc(sem("m2_split"), 1)

            def normalise(g):
                dve.wait_ge(sem("m2_std"), g + 1)
                dve.reciprocal(e2[:, g, 0:T], e2[:, g, 0:T]).then_inc(sem("m2_inv"), 1)
                dve.wait_ge(sem("m2_inv"), g + 1)
                for k in range(4 * g, 4 * g + 4):
                    ins = dve.scalar_tensor_tensor(out=xm[:, k, :], in0=xm[:, k, :], scalar=prm("ssd_g")[:, k:k + 1],
                                                   in1=e2[:, g, 0:T], op0=ALU.mult, op1=ALU.mult)
                    if k % 2 == 1:
                        ins.then_inc(sem("m2_normed"), 1)

            head(11)
            head(12)
            dve_split(dve, F0 + MIX2_IN + 2)
            gate(0)
            gate(1)
            for h in (13, 14, 15):
                head(h)
            y_pair(dve, 7)
            normalise(0)
            rest(0)
            rest(1)
            dve_split(dve, F0 + MIX2_IN + 3)
            gate(2)
            gate(3)
            normalise(1)
            dve_split(dve, F0 + MIX2_IN + 4)
            rest(2)
            rest(3)
            for b in range(3, MIX2_OUT - 1):
                dve_split(dve, F0 + MIX2_IN + 2 + b)
            dve_phase_residual(dve, n)

        def y_pair(dve, k):
            if k < 0:
                return
            dve.wait_ge(sem("m2_head"), 2 * k + 2)
            y = m2_y if k < 4 else xm
            dve.scalar_tensor_tensor(out=y[:, k, :], in0=xbc[:, k, :], scalar=prm("ssd_d")[:, k:k + 1],
                                     in1=ACC[2 + k % 2][:, 0:T], op0=ALU.mult, op1=ALU.add).then_inc(sem("m2_y"), 1)

        (kt, v3, qt, qs, t1, e3, pt3, kr, nm, o_hi, o_lo) = region(
            m3_kt=([P, MLA_H, T], F32), m3_v=([P, 2, D], F32), m3_qt=([P, 4, T], F32), m3_qs=([P, 2, 2, T], F32),
            m3_t1=([P, 2, T], F32), m3_e=([P, 2, 384], F32), m3_pt=([P, 2, 384], F32), m3_kr=([P, T], F32),
            m3_nm=([P, MLA_H, 8], F32), m3_o_hi=([P, KD, T], F32R), m3_o_lo=([P, KD, T], F32R))
        m3_squares = v3[:, :, :].rearrange("p a (b t) -> p (a b) t", t=T)
        (_, pos_i, pos_f, turns_t, ang) = region(tab_gap=([P, 16, T], F32), tab_pos=([P, T], I32),
                                                 tab_pos_f=([P, T], F32), tab_turns=([P, T], F32), tab_angle=([P, 2, T], F32))
        SCALE = float(DQ) ** -0.5
        UKV0, UQ0 = MIX3_IN, MIX3_IN + MIX3_UKV
        OUT0 = UQ0 + MIX3_UQ
        V_BANKS = (GATE, UP, MODP, STAT)
        LAG = 2
        M3_TURNS = MIX3_UQ + LAG + 1

        def latent_tiles(j):
            return 6 if j == 0 else 2 * j - 2

        def dve_tables(dve):
            TWO_PI = 2 * np.pi
            C1 = 6.28125
            C2 = float(TWO_PI - C1)
            ROUND = 1.5 * 2.0 ** 23
            LIMIT = 3.1415925
            dve.wait_ge(sem("pos_loaded"), 16)
            dve.tensor_copy(pos_f[:, :], pos_i[:, :]).then_inc(sem("rope_pos"), 1)
            dve.wait_ge(sem("rope_pos"), 1)
            dve.tensor_scalar(pos_f[:, :], pos_f[:, :], cst("inv_freq"), None, ALU.mult).then_inc(sem("rope_pos"), 1)
            dve.wait_ge(sem("rope_pos"), 2)
            a = sem("rope_angle_step")
            for i, quarter in enumerate((0.0, 0.25)):
                turns, dst = turns_t[:, :], ang[:, i, :]
                dve.tensor_scalar(turns, pos_f[:, :], 1.0 / TWO_PI, quarter, ALU.mult, ALU.add).then_inc(a, 1)
                dve.wait_ge(a, 5 * i + 1)
                dve.tensor_scalar(turns, turns, ROUND, ROUND, ALU.add, ALU.subtract).then_inc(a, 1)
                dve.wait_ge(a, 5 * i + 2)
                dve.scalar_tensor_tensor(out=dst, in0=turns, scalar=-C1, in1=pos_f[:, :], op0=ALU.mult, op1=ALU.add)\
                   .then_inc(a, 1)
                dve.wait_ge(a, 5 * i + 3)
                dve.scalar_tensor_tensor(out=dst, in0=turns, scalar=-C2, in1=dst, op0=ALU.mult, op1=ALU.add)\
                   .then_inc(a, 1)
                dve.wait_ge(a, 5 * i + 4)
                dve.tensor_scalar(dst, dst, quarter * TWO_PI, LIMIT, ALU.add, ALU.min).then_inc(a, 1)
                dve.wait_ge(a, 5 * i + 5)
                dve.tensor_scalar(dst, dst, -LIMIT, None, ALU.max).then_inc(sem("rope_angle"), 1)

        def act_tables(act):
            for i, dst in enumerate((sin96, cos96)):
                act.wait_ge(sem("rope_angle"), i + 1)
                act.activation(dst[:, :], ang[:, i, :], ACT.Sin).then_inc(sem("rope_tables"), 1)

        def pe_mix3(pe, n, _):
            F0 = first_block[n]
            pe_norm(pe, n)

            def krope():
                for k in range(KD):
                    mm = pe.matmul(MODP[0:DQ, 0:T], prm("w_krope")[:, k * DQ:k * DQ + DQ], xm[:, k, :],
                                   start=(k == 0), stop=(k == KD - 1))
                mm.then_inc(sem("m3_krope"), 1)

            def swap_k():
                pe.wait_ge(sem("m3_ks"), 1)
                pe.matmul(MODP[0:DQ, 0:T], cst("rope_perm")[0:DQ, :], qs[0:DQ, 1, 0, :], start=True, stop=True)\
                  .then_inc(sem("m3_kswap"), 1)

            def latent_sums(g, ks):
                for i, k in enumerate(ks):
                    if k % 2 == 0:
                        pe.wait_ge(sem("m3_squared"), 1 if g == 0 else 2 + k // 2)
                    mm = pe.matmul(STAT[:, g * T:g * T + T], ones, m3_squares[:, k, :], start=(i == 0),
                                   stop=(i == len(ks) - 1), skip_group_check=True)
                mm.then_inc(sem("m3_var"), 1)

            def uk():
                b = F0 + UKV0
                s = slot_of(b)
                pe.wait_ge(sem("w_lo_ready"), b + 1)
                pe.wait_ge(sem("m3_split"), 1)
                for m in range(8):
                    if m == 2:
                        pe.wait_ge(sem("m3_std"), 1)
                        latent_sums(1, range(0, 6))
                    for k in range(2):
                        for i, (wp, ap) in enumerate(PASSES):
                            c = k * D + m * P
                            mm = pe.matmul(pair(ACC[m // 2])[:, m % 2, :], (whi, wlo)[wp][:, s, c:c + P],
                                           (xh, xl)[ap][:, 6 + k, :], start=(k == 0 and i == 0), stop=(k == 1 and i == 2))
                mm.then_inc(sem("w_used"), 1)

            def uv():
                b = F0 + UKV0 + 1
                s = slot_of(b)
                pe.wait_ge(sem("w_lo_ready"), b + 1)
                pe.wait_ge(sem("m3_evac"), MIX3_IN)
                for q in range(4):
                    tt, half = q // 2, q % 2
                    if q == 2:
                        pe.wait_ge(sem("m3_kr"), 2)
                    if q == 3:
                        pe.wait_ge(sem("m3_std"), 2)
                    for k in range(2):
                        for i, (wp, ap) in enumerate(PASSES):
                            c = k * D + half * 512
                            mm = pe.matmul(V_BANKS[q][:, :], (xh, xl)[ap][:, 6 + k, tt * P:tt * P + P],
                                           (whi, wlo)[wp][:, s, c:c + 512], start=(k == 0 and i == 0),
                                           stop=(k == 1 and i == 2))
                    if q < 3:
                        mm.then_inc(sem("m3_v_bank"), 1)
                mm.then_inc(sem("w_used"), 1)

            def uq(j, hd):
                b = F0 + UQ0 + j
                s = slot_of(b)
                out = pair((GATE, UP)[j % 2])
                if hd == 0:
                    pe.wait_ge(sem("w_lo_ready"), b + 1)
                    if j == 0:
                        pe.wait_ge(sem("m3_split"), 4)
                        pe.wait_ge(sem("m3_v_act"), 1)
                    if j == 1:
                        pe.wait_ge(sem("m3_v_dve"), 1)
                    if j >= 2:
                        pe.wait_ge(sem("m3_qs"), j - 1)
                for k in range(6):
                    for i, (wp, ap) in enumerate(PASSES):
                        c = k * 2 * DQ + hd * DQ
                        mm = pe.matmul(out[0:DQ, hd, :], (whi, wlo)[wp][:, s, c:c + DQ], (xh, xl)[ap][:, k, :],
                                       start=(k == 0 and i == 0), stop=(k == 5 and i == 2))
                if hd == 1:
                    mm.then_inc(sem("w_used"), 1)

            def swap_q(j):
                pe.wait_ge(sem("m3_qs"), j + 1)
                if j == 0:
                    pe.wait_ge(sem("m3_v_act"), 2)
                else:
                    pe.wait_ge(sem("m3_q"), j)
                pe.matmul(MODP[0:DQ, :], cst("rope_perm")[0:DQ, :], qs[0:DQ, j % 2].rearrange("p a t -> p (a t)"),
                          start=True, stop=True).then_inc(sem("m3_qswap"), 1)

            def scores(h):
                b = ACC[h % 2]
                if h == 0:
                    pe.wait_ge(sem("m3_k"), 8)
                    pe.wait_ge(sem("m3_v_act"), 2)
                    pe.wait_ge(sem("m3_v_dve"), 2)
                    pe.wait_ge(sem("m3_k_rope"), 1)
                if h >= 2:
                    pe.wait_ge(sem("m3_e"), 2 * (h - 1))
                pe.wait_ge(sem("m3_q"), h // 2 + 1)
                q, k = qt[0:DQ, h % 4, :], kt[0:DQ, h, :]
                pe.matmul(b[:, 0:P], q[:, 0:P], k[:, 0:P], start=True, stop=True, skip_group_check=True)
                pe.matmul(b[:, P:384], q[:, P:T], k[:, :], start=False, stop=True, skip_group_check=True)
                pe_mask(pe, b[:, 0:P], "mask")
                pe_mask(pe, b[:, 256:384], "mask").then_inc(sem("m3_scores"), 1)

            def turn(h):
                if h >= 1:
                    pe.wait_ge(sem("m3_pt"), h)
                pe.wait_ge(sem("m3_p"), 2 * h + 2)
                for c in range(3):
                    mm = pe.transpose(ACC[2][:, c * P:c * P + P], e3[:, h % 2, c * P:c * P + P], ident)
                mm.then_inc(sem("m3_turned"), 1)

            def sums(h):
                r0 = 64 * (h % 2)
                if h >= 2 and h % 2 == 0:
                    pe.wait_ge(sem("m3_o"), h // 2)
                pe.wait_ge(sem("m3_pt"), h + 1)
                p = pt3[:, h % 2, :]
                pe.matmul(ACC[3][r0:r0 + 64, 0:T], v3[:, 0, h * 64:h * 64 + 64], p[:, 0:T], start=True, stop=False,
                          skip_group_check=True)
                pe.matmul(ACC[3][r0:r0 + 64, P:T], v3[:, 1, h * 64:h * 64 + 64], p[:, 256:384], start=False, stop=True,
                          skip_group_check=True).then_inc(sem("m3_sums"), 1)

            def attend(h):
                if 0 <= h < MLA_H:
                    scores(h)
                if 1 <= h <= MLA_H:
                    turn(h - 1)
                if 2 <= h < MLA_H + 2:
                    sums(h - 2)

            def out(b, between=None):
                if b == 0:
                    pe.wait_ge(sem("m3_q"), MIX3_UQ)
                pe.wait_ge(sem("m3_o"), 2 * b + 2)
                pe_out(pe, F0 + OUT0 + b, o_hi[:, 2 * b:2 * b + 2, :], o_lo[:, 2 * b:2 * b + 2, :], b == 0,
                       b == MIX3_OUT - 1, acc=MIX_ACC, between=between)

            for j in range(MIX3_IN):
                if j >= 2:
                    pe.wait_ge(sem("m3_evac"), j - 1)
                pe_in(pe, F0 + j, pair((GATE, UP)[j % 2]), **({"first_pass_waits": 8 * split_index[n]} if j == 0 else {}))
                if j == 0:
                    krope()
                if j == 2:
                    swap_k()
                    latent_sums(0, range(6, 8))
            uk()
            uv()
            for j in range(M3_TURNS):
                h = 2 * (j - LAG)
                if j < MIX3_UQ:
                    uq(j, 0)
                attend(h)
                if j < MIX3_UQ:
                    uq(j, 1)
                    if h >= 0:
                        attend(h + 1)
                    swap_q(j)
                else:
                    out(j - MIX3_UQ, between=lambda: attend(h + 1))
            out(MIX3_OUT - 1)

        def act_mix3(act, n, _):
            F0 = first_block[n]
            act_norm(act, n)
            act_split(act, F0 + 2)

            def round_latent(b):
                act.wait_ge(sem("m3_normed"), 1 if b == 3 else b + 2)
                act.activation(xh[:, 2 * b:2 * b + 2, :], xm[:, 2 * b:2 * b + 2, :], ACT.Copy).then_inc(sem("m3_rounded"), 1)

            def root(g):
                act.wait_ge(sem("m3_var"), g + 1)
                act.activation(e3[:, g, 0:T], STAT[:, g * T:g * T + T], ACT.Sqrt, scale=1.0 / (256, 768)[g],
                               bias=cols[:, 64:65]).then_inc(sem("m3_std"), 1)

            for j in range(MIX3_IN):
                k = latent_tiles(j)
                if j >= 1:
                    act_split(act, F0 + j + 2)
                act.wait_ge(sem("w_used"), F0 + j + 1)
                if j == 0:
                    act.wait_ge(sem("m3_krope"), 1)
                if j == 3:
                    round_latent(3)
                act.activation(xm[:, k:k + 2, :], pair((GATE, UP)[j % 2]), ACT.Copy).then_inc(sem("m3_evac"), 1)
                act.wait_ge(sem("m3_evac"), j + 1)
                act.activation(m3_squares[:, k:k + 2, :], xm[:, k:k + 2, :], ACT.Square).then_inc(sem("m3_squared"), 1)
                if j == 0:
                    act.activation(qs[0:DQ, 1, 0, :], MODP[0:DQ, 0:T], ACT.Copy).then_inc(sem("m3_ks"), 1)
                if j == 2:
                    root(0)
            act_split(act, F0 + 6)
            root(1)
            act.wait_ge(sem("w_used"), F0 + UKV0 + 1)
            for q in range(4):
                for r in range(2):
                    act.activation(kt[0:64, 4 * q + r:4 * q + r + 3:2, :], pair(ACC[q])[64 * r:64 * r + 64], ACT.Copy)\
                       .then_inc(sem("m3_k"), 1)
                if q < 3:
                    round_latent(q)
            act.wait_ge(sem("w_used"), F0 + UKV0 + 2)
            for i in range(2):
                act.activation(v3[:, i, 0:512], V_BANKS[2 * i][:, :], ACT.Copy).then_inc(sem("m3_v_act"), 1)
            act_split(act, F0 + 7)

            def exps(h):
                act.wait_ge(sem("m3_max"), h + 1)
                if h >= 2:
                    act.wait_ge(sem("m3_turned"), h - 1)
                for lt, (c0, c1) in enumerate(((0, P), (P, 384))):
                    act.activation(e3[:, h % 2, c0:c1], ACC[h % 2][:, c0:c1], ACT.Exp, bias=nm[:, h, 2 + lt:3 + lt],
                                   scale=SCALE, accum_out=nm[:, h, 4 + lt:5 + lt]).then_inc(sem("m3_e"), 1)

            def turned(h):
                act.wait_ge(sem("m3_turned"), h + 1)
                if h >= 2:
                    act.wait_ge(sem("m3_sums"), h - 1)
                act.activation(pt3[:, h % 2, :], ACC[2][:, 0:384], ACT.Copy).then_inc(sem("m3_pt"), 1)

            def attend(h):
                if 0 <= h < MLA_H:
                    exps(h)
                if 1 <= h <= MLA_H:
                    turned(h - 1)
                if h >= 3 and h % 2 == 1:
                    k = (h - 3) // 2
                    act.wait_ge(sem("m3_sums"), 2 * k + 2)
                    act.activation(o_hi[:, k, :], ACC[3][:, 0:T], ACT.Copy).then_inc(sem("m3_o_hi"), 1)

            for j in range(M3_TURNS):
                h = 2 * (j - LAG)
                attend(h)
                act_split(act, F0 + UQ0 + j + 2)
                if j < MIX3_UQ:
                    act.wait_ge(sem("w_used"), F0 + UQ0 + j + 1)
                    if j == 1:
                        act.wait_ge(sem("m3_kr"), 1)
                    if j >= 2:
                        act.wait_ge(sem("m3_q_read"), j - 1)
                        act.wait_ge(sem("m3_qswap"), j - 1)
                    act.activation(qs[0:DQ, j % 2], pair((GATE, UP)[j % 2])[0:DQ], ACT.Copy).then_inc(sem("m3_qs"), 1)
                if h >= 0:
                    attend(h + 1)
            act_split_halves(act, n + 1)

        def pool_mix3(pool):
            pool.wait_ge(sem("m3_kr"), 3)
            pool.tensor_copy(kt[64:DQ, :, :], kr[64:DQ, :].unsqueeze(1).to_broadcast([32, MLA_H, T]))\
                .then_inc(sem("m3_k_rope"), 1)

        def dve_mix3(dve, n, _):
            F0 = first_block[n]
            dve_phase_norm(dve, n)

            def rest(b):
                i = 0 if b == 3 else b + 1
                dve.wait_ge(sem("m3_rounded"), i + 1)
                dve.tensor_tensor(xl[:, 2 * b:2 * b + 2, :], xm[:, 2 * b:2 * b + 2, :],
                                  xh[:, 2 * b:2 * b + 2, :].bitcast(F32), ALU.subtract).then_inc(sem("m3_split"), 1)

            def scale_latent(g):
                gain = prm(("kv_g", "q_g")[g])
                inv = e3[:, g, 0:T]
                k0, k1 = ((6, 8), (0, 6))[g]
                dve.wait_ge(sem("m3_std"), g + 1)
                dve.reciprocal(inv, inv).then_inc(sem("m3_inv"), 1)
                dve.wait_ge(sem("m3_inv"), g + 1)
                for k in range(k0, k1):
                    ins = dve.scalar_tensor_tensor(out=xm[:, k, :], in0=xm[:, k, :], scalar=gain[:, k - k0:k - k0 + 1],
                                                   in1=inv, op0=ALU.mult, op1=ALU.mult)
                    if k % 2 == 1:
                        ins.then_inc(sem("m3_normed"), 1)

            def rotate_k():
                dve.wait_ge(sem("rope_tables"), 2)
                dve.wait_ge(sem("m3_kswap"), 1)
                dve.tensor_tensor(t1[0:DQ, 0, :], qs[0:DQ, 1, 0, :], cos96[0:DQ, :], ALU.mult).then_inc(sem("m3_kr"), 1)
                dve.tensor_tensor(kr[0:DQ, :], MODP[0:DQ, 0:T], sin96[0:DQ, :], ALU.mult).then_inc(sem("m3_kr"), 1)
                dve.wait_ge(sem("m3_kr"), 2)
                dve.tensor_tensor(kr[0:DQ, :], kr[0:DQ, :], t1[0:DQ, 0, :], ALU.add).then_inc(sem("m3_kr"), 1)

            dve_split(dve, F0 + 2)
            dve_split(dve, F0 + 3)
            dve_split(dve, F0 + 4)
            rotate_k()
            scale_latent(0)
            dve_split(dve, F0 + 5)
            rest(3)
            dve_split(dve, F0 + 6)
            scale_latent(1)
            for b in range(3):
                rest(b)
            for i in range(2):
                dve.wait_ge(sem("w_used"), F0 + UKV0 + 2)
                dve.tensor_copy(v3[:, i, 512:D], V_BANKS[2 * i + 1][:, :]).then_inc(sem("m3_v_dve"), 1)
            dve_split(dve, F0 + 7)
            dve.wait_ge(sem("m3_kr"), 3)

            def rope_q(j):
                q = qt[0:DQ, 2 * (j % 2):2 * (j % 2) + 2, :]
                dve.wait_ge(sem("m3_qs"), j + 1)
                if j >= 1:
                    dve.wait_ge(sem("m3_q"), j)
                dve.tensor_tensor(t1[0:DQ], qs[0:DQ, j % 2], over(cos96[0:DQ, :], [DQ, 2, T]), ALU.mult)\
                   .then_inc(sem("m3_q_read"), 1)
                dve.wait_ge(sem("m3_qswap"), j + 1)
                if j >= 2:
                    dve.wait_ge(sem("m3_scores"), 2 * (j - 1))
                dve.tensor_tensor(q, pair(MODP)[0:DQ], over(sin96[0:DQ, :], [DQ, 2, T]), ALU.mult)\
                   .then_inc(sem("m3_q_part"), 1)
                dve.wait_ge(sem("m3_q_part"), j + 1)
                dve.wait_ge(sem("m3_q_read"), j + 1)
                dve.tensor_tensor(q, q, t1[0:DQ], ALU.add).then_inc(sem("m3_q"), 1)

            def maxima(h):
                dve.wait_ge(sem("m3_scores"), h + 1)
                for lt, (c0, c1) in enumerate(((0, P), (P, 384))):
                    dve.tensor_reduce(nm[:, h, lt:lt + 1], ACC[h % 2][:, c0:c1], AX.X, ALU.max).then_inc(sem("m3_max_part"), 1)
                dve.wait_ge(sem("m3_max_part"), 2 * h + 2)
                dve.tensor_scalar(nm[:, h, 2:4], nm[:, h, 0:2], -SCALE, None, ALU.mult).then_inc(sem("m3_max"), 1)

            def weights(h):
                dve.wait_ge(sem("m3_e"), 2 * h + 2)
                dve.reciprocal(nm[:, h, 6:8], nm[:, h, 4:6]).then_inc(sem("m3_rsum"), 1)
                dve.wait_ge(sem("m3_rsum"), h + 1)
                for lt, (c0, c1) in enumerate(((0, P), (P, 384))):
                    dve.tensor_scalar(e3[:, h % 2, c0:c1], e3[:, h % 2, c0:c1], nm[:, h, 6 + lt:7 + lt], None, ALU.mult)\
                       .then_inc(sem("m3_p"), 1)

            def attend(h, rotate=None):
                if 0 <= h < MLA_H:
                    maxima(h)
                if rotate is not None:
                    rotate()
                if 0 <= h < MLA_H:
                    weights(h)
                if h >= 3 and h % 2 == 1:
                    k = (h - 3) // 2
                    dve.wait_ge(sem("m3_o_hi"), k + 1)
                    dve.tensor_tensor(o_lo[:, k, :], ACC[3][:, 0:T], o_hi[:, k, :].bitcast(F32), ALU.subtract)\
                       .then_inc(sem("m3_o"), 1)

            for j in range(M3_TURNS):
                h = 2 * (j - LAG)
                rotate = (lambda: rope_q(j - 1)) if 1 <= j <= MIX3_UQ else None
                attend(h, rotate)
                dve_split(dve, F0 + UQ0 + j + 2)
                if h >= 0:
                    attend(h + 1)
            dve_phase_residual(dve, n)

        PE = {"ffn": lambda pe, n, f: pe_ffn(pe, n, f, MOD_GROUPS[f]), "final": lambda pe, n, f: pe_norm(pe, n),
              "mix1": pe_mix1, "mix2": pe_mix2, "mix3": pe_mix3}
        ACTS = {"ffn": lambda e, n, f: act_ffn(e, n, f, MOD_GROUPS[f]),
                "final": lambda e, n, f: act_norm(e, n, split=False),
                "mix1": act_mix1, "mix2": act_mix2, "mix3": act_mix3}
        DVE = {"ffn": lambda e, n, f: dve_ffn(e, n, f, MOD_GROUPS[f]), "final": lambda e, n, f: dve_phase_norm(e, n),
               "mix1": dve_mix1, "mix2": dve_mix2, "mix3": dve_mix3}

        block = ctx.enter_context(nc.Block())

        @block.sync
        def _(sp):
            for i in range(2):
                sp.dma_start(x[:, 4 * i:4 * i + 4, :], a_x[:, 4 * i:4 * i + 4, :]).then_inc(sem(f"x_loaded{i}"), 16)
            sp.dma_start(consts[:, :], a_consts).then_inc(sem("consts_loaded"), 16)
            sp.dma_start(params[:, 0:4 * KD], a_params[:, 0:4 * KD]).then_inc(sem("consts_loaded"), 16)
            for n in range(min(SLOTS, N_BLOCKS)):
                sp.dma_start(raw[:, n, :], a_stream[n * P:n * P + P, :]).then_inc(sem(f"w_loaded{n}"), 16)
            sp.dma_start(params[:, 4 * KD:P_N], a_params[:, 4 * KD:P_N]).then_inc(sem("params_loaded"), 16)
            full = N_BLOCKS // SLOTS

            def load(s, turn):
                sp.wait_ge(sem("w_lo_ready"), s - SLOTS + 1 + SLOTS * turn)
                sp.dma_start(raw[:, s, :], a_stream[ds(s * P + SLOTS * P * turn, P), :])\
                  .then_inc(sem(f"w_loaded{s}"), 16)

            if full > 1:
                with sp.Fori(1, full) as turn:
                    for s in range(SLOTS):
                        load(s, turn)
            for s in range(N_BLOCKS % SLOTS):
                load(s, full)
            sp.wait_ge(sem("x_updated"), 4 * (len(phases)))
            sp.dma_start(a_out, x[:, :, :]).then_inc(sem("stored"), 16)
            sp.wait_ge(sem("stored"), 16)

        @block.gpsimd
        def _(pool):
            def load(s, turn):
                pool.dma_start(mod_raw[:, s, :], a_mod[ds(s * P + 2 * P * turn, P), :])\
                    .then_inc(sem(f"mod_loaded{s}"), 16)

            if N_GROUPS:
                pool.wait_ge(sem("w_loaded1"), 16)
                for s in range(2):
                    load(s, 0)
                with pool.Fori(1, 2 * N_GROUPS) as turn:
                    for s in range(2):
                        pool.wait_ge(sem("mod_step"), 2 * s + 2 - 4 + 4 * turn)
                        load(s, turn)
            if any(kind == "mix3" for kind, _, _ in phases):
                pool_mix3(pool)

        @block.tensor
        def _(pe):
            pe.wait_ge(sem("consts_loaded"), 32)
            for n, (kind, f, _) in enumerate(phases):
                if n == 1:
                    pe.wait_ge(sem("params_loaded"), 16)
                    pe.wait_ge(sem("masks_ready"), 2)
                PE[kind](pe, n, f)

        @block.scalar
        def _(act):
            act.wait_ge(sem("eps_ready"), 2)
            for n, (kind, f, _) in enumerate(phases):
                ACTS[kind](act, n, f)

        @block.vector
        def _(dve):
            dve.memset(cols[:, 64:65], RMS_EPS).then_inc(sem("eps_ready"), 1)
            dve.memset(cols[:, 65:66], LN_EPS).then_inc(sem("eps_ready"), 1)
            dve.wait_ge(sem("consts_loaded"), 32)
            dve.tensor_copy(ident_b[:, :], ident).then_inc(sem("masks_ready"), 1)
            dve.tensor_copy(mask_b[:, :], cst("maskT")).then_inc(sem("masks_ready"), 1)
            for n, (kind, f, _) in enumerate(phases):
                DVE[kind](dve, n, f)


def _in_blocks(w, width=256):
    k, n = w.shape
    b = w.reshape(k // P, P, n // width, width).transpose(2, 1, 0, 3).reshape(n // width, P, -1)
    return np.pad(b, ((0, 0), (0, 0), (0, BLK - b.shape[2])))


def _out_blocks(w):
    k, n = w.shape
    return w.reshape(k // (2 * P), 2, P, n).transpose(0, 2, 1, 3).reshape(k // (2 * P), P, 2 * n)


def _ffn_blocks(w_in, w_out):
    g, u, d = _in_blocks(w_in[:, :DFF]), _in_blocks(w_in[:, DFF:]), _out_blocks(w_out)
    order = [g[0], u[0]]
    for s in range(1, STEPS):
        order += [g[s], u[s], d[s - 1]]
    return np.stack(order + [d[STEPS - 1]])


def _cols(v):
    v = np.asarray(v)
    return np.moveaxis(v.reshape(-1, v.shape[-1] // P, P), 2, 0).reshape(P, -1)


def _top(a):
    a = np.asarray(a)
    return np.pad(a, ((0, P - a.shape[0]), (0, 0)))


def _stream(v):
    mix = v["w_mix_in"][0]
    M = HEADS_M * DH_M
    z0 = 4 * M + 2 * HEADS_M
    g0 = z0 + 2 * D
    q, k, vv, o = (mix[:, i * M:(i + 1) * M] for i in range(4))
    zu, zv, gm, gs = mix[:, z0:z0 + D], mix[:, z0 + D:g0], mix[:, g0:g0 + D], mix[:, g0 + D:g0 + 2 * D]
    parts = [_ffn_blocks(v["ffn1_w_in"][0], v["ffn1_w_out"][0])]
    parts += [_in_blocks(w) for w in (q, k, vv, zv, o, gm, gs, zu)] + [_out_blocks(v["w_mix_out"][0])]
    parts += [_ffn_blocks(v["ffn2_w_in"][0], v["ffn2_w_out"][0])]
    w13, w2 = v["ffn_w13_2"], v["ffn_w2_2"]
    parts += [_ffn_blocks(w13[0, 0], w2[0, 0])]
    ab = v["ab_w_in_2"][0]
    ab = np.concatenate([ab[:, 1536:3072], ab[:, :1536]], axis=1)
    parts += [_in_blocks(ab), _out_blocks(v["ab_w_out_2"][0])]
    parts += [_ffn_blocks(w13[0, 1], w2[0, 1]), _ffn_blocks(w13[1, 0], w2[1, 0])]
    ukv = v["mla_w_ukv_2"][0].reshape(256, MLA_H, 2, 64)
    parts += [_in_blocks(np.roll(v["mla_w_in_2"][0][:, :1024], 256, axis=1)),
              _in_blocks(ukv[:, :, 0].reshape(256, 1024), 1024), _in_blocks(ukv[:, :, 1].reshape(256, 1024), 1024),
              _in_blocks(v["mla_w_uq_2"][0], 2 * DQ),
              _out_blocks(v["mla_w_o_2"][0])]
    parts += [_ffn_blocks(w13[1, 1], w2[1, 1])]
    return np.concatenate(parts).reshape(-1, BLK)


def _params(v):
    mix = v["w_mix_in"][0]
    i0 = 4 * D
    w_if = np.zeros((D, 64), np.float32)
    w_if[:, 0:4] = mix[:, i0:i0 + 4]
    w_if[:, 32:36] = mix[:, i0 + 4:i0 + 8]
    w_kr = np.zeros((D, DQ), np.float32)
    w_kr[:, NOPE:] = v["mla_w_in_2"][0][:, 1024:]

    def ktiles(w):
        return w.reshape(KD, P, -1).transpose(1, 0, 2).reshape(P, -1)

    def conv(w):
        return w.reshape(4, -1, P).transpose(2, 1, 0).reshape(P, -1)

    col = lambda a: np.asarray(a).reshape(-1, 1)
    b_f = np.zeros((P, 1), np.float32)
    b_f[32:36] = col(v["mlstm_b_fgate"][0])
    at = {"g_ffn1": _cols(v["ffn1_norm_g"]), "g_mix": _cols(v["mix_norm_g"]), "g_ffn2": _cols(v["ffn2_norm_g"]),
          "g_final": _cols(v["final_norm_g"]), "conv_w1": conv(v["mlstm_conv_w"][0]),
          "conv_b1": _cols(v["mlstm_conv_b"]), "b_i": _top(col(v["mlstm_b_igate"][0])), "b_f": b_f,
          "head_g": _cols(v["mlstm_head_norm_g"]), "sgu_bs": _top(v["sgu_b_s"][0]), "mod_b": _cols(v["mod_b_2"]),
          "norm_g2": _cols(v["norm_g_2"].reshape(6, D)), "pool_scale": _cols(v["pool_scale_2"]),
          "conv_w2": conv(v["ssd_conv_w_2"][0]), "conv_b2": _cols(v["ssd_conv_b_2"]),
          "dt_bias": _top(col(v["ssd_dt_bias_2"][0])), "a_log": _top(col(v["ssd_a_log_2"][0])),
          "ssd_d": _cols(np.repeat(v["ssd_d_2"], SSD_P, axis=1)), "ssd_g": _cols(v["ssd_norm_g_2"]),
          "q_g": _cols(v["mla_q_norm_g_2"]), "kv_g": _cols(v["mla_kv_norm_g_2"]), "g_final2": _cols(v["final_norm_g_2"]),
          "c": _cols(v["c_2"]), "w_if": ktiles(w_if), "w_dt": ktiles(v["ab_w_in_2"][0][:, 3072:]),
          "w_krope": ktiles(w_kr), "pool_w": v["pool_w_2"][0].transpose(1, 0, 2).reshape(P, -1),
          "sgu_wT": v["sgu_w_s"][0].transpose(2, 0, 1).reshape(P, -1)}
    return np.concatenate([at[name].reshape(P, width) for name, width in PARAMS], axis=1)


def _consts():
    r = np.arange(P)
    later = np.where(r[:, None] <= r[None, :], 0.0, NEG)
    perm = np.zeros((P, DQ))
    half = ROPE // 2
    for m in range(half):
        perm[NOPE + half + m, NOPE + m] = -1.0
        perm[NOPE + m, NOPE + half + m] = 1.0
    freq = np.zeros((P, 1))
    f = np.float32(10000.0) ** (-np.arange(0, ROPE, 2, dtype=np.float32) / np.float32(ROPE))
    freq[NOPE:NOPE + half, 0] = f
    freq[NOPE + half:NOPE + ROPE, 0] = f
    fix = np.stack([w / np.minimum(np.arange(16) + 1, w) for w in (2, 4, 8, 16)])
    at = {"ident": np.eye(P), "maskT": later, "ones": np.ones((P, P)), "rope_perm": perm,
          "inv_freq": freq, "pool_fix": np.broadcast_to(fix.reshape(1, -1), (P, 64))}
    return np.concatenate([at[name].reshape(P, width) for name, width in CONSTS], axis=1).astype(np.float32)


def kernel(**inputs):
    import concourse.bacc as bacc
    from concourse.bass_utils import run_bass_kernel_spmd as run

    v = {k: np.asarray(a) for k, a in inputs.items()}
    arrays = {
        "x_in": np.ascontiguousarray(v["x"][0].reshape(T, KD, P).transpose(2, 1, 0)),
        "pos_in": np.ascontiguousarray(np.broadcast_to(v["positions_2"].astype(np.int32), (P, T))),
        "stream_in": _stream(v),
        "mod_in": np.ascontiguousarray(v["mod_w_2"].reshape(2, 4, 2, P, 9, D).transpose(0, 4, 1, 3, 2, 5)).reshape(-1, BLK),
        "params_in": _params(v),
        "consts_in": _consts(),
        "sgu_in": np.ascontiguousarray(np.broadcast_to(
            np.concatenate([v["sgu_norm_g"][0], v["sgu_norm_b"][0]])[None], (P, 2 * D))),
    }
    nc = bacc.Bacc("TRN2", target_bir_lowering=False, num_devices=1)
    aps = [nc.dram_tensor(name, a.shape, mybir.dt.from_np(a.dtype), kind="ExternalInput").ap()
           for name, a in arrays.items()]
    out = nc.dram_tensor("y_out", (P, KD, T), mybir.dt.float32, kind="ExternalOutput").ap()
    build_program(nc, *aps, out)
    y = run(nc, [arrays], core_ids=[0]).results[0]["y_out"]
    return np.ascontiguousarray(y.transpose(2, 1, 0)).reshape(1, T, D)
```
